# Optimizing a Trainium2 kernel written in Bass

```python
import math
import jax, jax.numpy as jnp
from jax import lax
import numpy as np

D_MODEL = 1024
BATCH = 1
SEQ = 256
DEPTH = 1

GDN_HEAD_K = 128
GDN_HEAD_V = 128
GDN_HEADS = D_MODEL // GDN_HEAD_V
GDN_CONV = 4
GDN_CHUNK = 64
GDN_QK_DIM = GDN_HEADS * GDN_HEAD_K
GDN_V_DIM = GDN_HEADS * GDN_HEAD_V
GDN_CONV_DIM = 2 * GDN_QK_DIM + GDN_V_DIM

ATT_HEAD_DIM = 128
ATT_HEADS = D_MODEL // ATT_HEAD_DIM
ATT_KV_HEADS = 2
ATT_Q_DIM = ATT_HEADS * ATT_HEAD_DIM
ATT_KV_DIM = ATT_KV_HEADS * ATT_HEAD_DIM
IDX_HEADS = 8
IDX_DIM = 64
TOPK_MAX = 256
Q_BLOCK = 128

ROPE_THETA = 500000.0
ROPE_FRACTION = 4
D_FF = 4 * D_MODEL
EPS = 1e-6

IN_SPLITS = (GDN_CONV_DIM, GDN_V_DIM, GDN_HEADS, GDN_HEADS,
             ATT_Q_DIM, ATT_KV_DIM, ATT_KV_DIM,
             IDX_HEADS * IDX_DIM, IDX_DIM, IDX_HEADS,
             D_MODEL, D_MODEL)
IN_PROJ_DIM = (GDN_CONV_DIM + GDN_V_DIM + 2 * GDN_HEADS + ATT_Q_DIM + 2 * ATT_KV_DIM
               + IDX_HEADS * IDX_DIM + IDX_DIM + IDX_HEADS + 2 * D_MODEL)


def rms_norm(x, g):
    xf = x.astype(jnp.float32)
    y = xf * lax.rsqrt(jnp.mean(xf * xf, axis=-1, keepdims=True) + EPS)
    return (y * g.astype(jnp.float32)).astype(x.dtype)

def l2_normalize(x):
    xf = x.astype(jnp.float32)
    return xf * lax.rsqrt(jnp.sum(xf * xf, axis=-1, keepdims=True) + EPS)

def rope_tables(seq, rot_dim):
    inv_freq = ROPE_THETA ** (-jnp.arange(0, rot_dim, 2, dtype=jnp.float32) / rot_dim)
    ang = jnp.arange(seq, dtype=jnp.float32)[:, None] * inv_freq[None, :]
    return jnp.cos(ang), jnp.sin(ang)

def apply_partial_rope(t, cos, sin):
    half = cos.shape[-1]
    shape = (t.shape[1],) + (1,) * (t.ndim - 3) + (half,)
    c, s = cos.reshape(shape), sin.reshape(shape)
    tf = t.astype(jnp.float32)
    x1, x2 = tf[..., :half], tf[..., half:2 * half]
    out = jnp.concatenate([x1 * c - x2 * s, x2 * c + x1 * s, tf[..., 2 * half:]], axis=-1)
    return out.astype(t.dtype)

def causal_short_conv(u, w):
    k = w.shape[0]
    s = u.shape[1]
    up = jnp.pad(u, ((0, 0), (k - 1, 0), (0, 0)))
    y = up[:, 0:s] * w[0]
    for j in range(1, k):
        y = y + up[:, j:j + s] * w[j]
    return y

def gated_delta_rule_chunked(q, k, v, g, beta):
    B, S, H, dk = q.shape
    dv = v.shape[-1]
    C = GDN_CHUNK
    N = S // C
    f32 = jnp.float32

    def chunks(t):
        t = jnp.swapaxes(t.astype(f32), 1, 2)
        return t.reshape((B, H, N, C) + t.shape[3:])

    q, k, v, g, beta = chunks(q), chunks(k), chunks(v), chunks(g), chunks(beta)
    g_cum = jnp.cumsum(g, axis=-1)
    pos = jnp.arange(C)
    incl = pos[:, None] >= pos[None, :]
    strict = pos[:, None] > pos[None, :]
    diff = g_cum[..., :, None] - g_cum[..., None, :]
    decay = jnp.where(incl, jnp.exp(jnp.where(incl, diff, 0.0)), 0.0)
    k_beta = k * beta[..., None]
    a_mat = jnp.where(strict, jnp.einsum('bhnid,bhnjd->bhnij', k_beta, k) * decay, 0.0)
    lhs = a_mat + jnp.eye(C, dtype=f32)
    rhs = jnp.concatenate([v * beta[..., None], k_beta * jnp.exp(g_cum)[..., None]], axis=-1)
    sol = lax.linalg.triangular_solve(lhs, rhs, left_side=True, lower=True, unit_diagonal=True)
    u, w = sol[..., :dv], sol[..., dv:]
    qk = jnp.where(incl, jnp.einsum('bhnid,bhnjd->bhnij', q, k) * decay, 0.0)
    q_dec = q * jnp.exp(g_cum)[..., None]
    g_last = g_cum[..., -1]
    k_dec = k * jnp.exp(g_last[..., None] - g_cum)[..., None]

    def step(state, xs):
        u_n, w_n, qk_n, q_n, k_n, gl_n = xs
        v_new = u_n - jnp.einsum('bhcd,bhde->bhce', w_n, state)
        o_n = (jnp.einsum('bhcd,bhde->bhce', q_n, state)
               + jnp.einsum('bhij,bhje->bhie', qk_n, v_new))
        state = state * jnp.exp(gl_n)[..., None, None] + jnp.einsum('bhcd,bhce->bhde', k_n, v_new)
        return state, o_n

    xs = tuple(jnp.moveaxis(t, 2, 0) for t in (u, w, qk, q_dec, k_dec, g_last))
    state0 = jnp.zeros((B, H, dk, dv), f32)
    _, o = lax.scan(step, state0, xs)
    o = jnp.moveaxis(o, 0, 2).reshape(B, H, S, dv)
    return jnp.swapaxes(o, 1, 2)

def dsa_sparse_attention(q, k, v, q_idx, k_idx, w_idx):
    B, S, H, hd = q.shape
    kvh = k.shape[2]
    grp = H // kvh
    n_blk = S // Q_BLOCK
    k_sel = min(TOPK_MAX, S // 4)
    scale = hd ** -0.5
    key_pos = jnp.arange(S, dtype=jnp.int32)
    k_idx_f = k_idx.astype(jnp.float32)

    def to_blocks(t):
        return jnp.moveaxis(t.reshape((B, n_blk, Q_BLOCK) + t.shape[2:]), 1, 0)

    def block(args):
        blk, qb, qib, wb = args
        t = blk * Q_BLOCK + jnp.arange(Q_BLOCK, dtype=jnp.int32)
        logits = jnp.einsum('bqhd,bsd->bqhs', qib.astype(jnp.float32), k_idx_f)
        score = jnp.einsum('bqh,bqhs->bqs', wb.astype(jnp.float32), jax.nn.relu(logits))
        causal = key_pos[None, :] <= t[:, None]
        score = jnp.where(causal[None], score, -jnp.inf)
        _, sel = lax.top_k(score, k_sel)
        valid = sel <= t[None, :, None]
        k_g = jax.vmap(lambda kb, ib: kb[ib])(k, sel)
        v_g = jax.vmap(lambda vb, ib: vb[ib])(v, sel)
        qg = qb.reshape(B, Q_BLOCK, kvh, grp, hd)
        s = jnp.einsum('bqcgd,bqncd->bqcgn', qg, k_g).astype(jnp.float32) * scale
        s = jnp.where(valid[:, :, None, None, :], s, -jnp.inf)
        p = jax.nn.softmax(s, axis=-1).astype(v_g.dtype)
        o = jnp.einsum('bqcgn,bqncd->bqcgd', p, v_g)
        return o.reshape(B, Q_BLOCK, H * hd)

    o = lax.map(block, (jnp.arange(n_blk, dtype=jnp.int32), to_blocks(q),
                        to_blocks(q_idx), to_blocks(w_idx)))
    return jnp.moveaxis(o, 0, 1).reshape(B, S, H * hd)

def hybrid_layer(x, norm_mix_g, w_in, conv_w, a_log, dt_bias, gdn_norm_g,
                 q_norm_g, k_norm_g, w_out, norm_mlp_g, w_mlp_up, w_mlp_down):
    B, S, _ = x.shape
    h = rms_norm(x, norm_mix_g)
    proj = h @ w_in
    points = np.cumsum(np.array(IN_SPLITS))[:-1].tolist()
    (g_qkv, g_z, g_a, g_b, a_q, a_k, a_v,
     i_q, i_k, i_w, gate_a, gate_b) = jnp.split(proj, points, axis=-1)

    qkv = jax.nn.silu(causal_short_conv(g_qkv, conv_w))
    gq, gk, gv = jnp.split(qkv, [GDN_QK_DIM, 2 * GDN_QK_DIM], axis=-1)
    gq = l2_normalize(gq.reshape(B, S, GDN_HEADS, GDN_HEAD_K)) * (GDN_HEAD_K ** -0.5)
    gk = l2_normalize(gk.reshape(B, S, GDN_HEADS, GDN_HEAD_K))
    gv = gv.reshape(B, S, GDN_HEADS, GDN_HEAD_V)
    beta = jax.nn.sigmoid(g_b.astype(jnp.float32))
    g = -jnp.exp(a_log.astype(jnp.float32)) * jax.nn.softplus(
        g_a.astype(jnp.float32) + dt_bias.astype(jnp.float32))
    o_gdn = gated_delta_rule_chunked(gq, gk, gv, g, beta)
    z = jax.nn.silu(g_z.reshape(B, S, GDN_HEADS, GDN_HEAD_V).astype(jnp.float32))
    o_gdn = (rms_norm(o_gdn, gdn_norm_g) * z).reshape(B, S, GDN_V_DIM).astype(x.dtype)

    cos, sin = rope_tables(S, ATT_HEAD_DIM // ROPE_FRACTION)
    a_q = apply_partial_rope(rms_norm(a_q.reshape(B, S, ATT_HEADS, ATT_HEAD_DIM), q_norm_g), cos, sin)
    a_k = apply_partial_rope(rms_norm(a_k.reshape(B, S, ATT_KV_HEADS, ATT_HEAD_DIM), k_norm_g), cos, sin)
    a_v = a_v.reshape(B, S, ATT_KV_HEADS, ATT_HEAD_DIM)
    cos_i, sin_i = rope_tables(S, IDX_DIM // ROPE_FRACTION)
    i_q = apply_partial_rope(i_q.reshape(B, S, IDX_HEADS, IDX_DIM), cos_i, sin_i)
    i_k = apply_partial_rope(i_k, cos_i, sin_i)
    i_w = i_w * (IDX_HEADS ** -0.5 * IDX_DIM ** -0.5)
    o_att = dsa_sparse_attention(a_q, a_k, a_v, i_q, i_k, i_w).astype(x.dtype)

    merged = jax.nn.sigmoid(gate_a) * o_gdn + jax.nn.sigmoid(gate_b) * o_att
    x = x + merged @ w_out

    h2 = rms_norm(x, norm_mlp_g)
    x = x + jnp.square(jax.nn.relu(h2 @ w_mlp_up)) @ w_mlp_down
    return x

def first_inputs(seed: int = 0) -> dict:
    key = jax.random.key(seed)
    ks = jax.random.split(key, 14)
    f32 = jnp.float32

    def gain(k, n):
        return 1.0 + 0.02 * jax.random.normal(k, (DEPTH, n), f32)

    x = jax.random.normal(ks[0], (BATCH, SEQ, D_MODEL), f32)
    norm_mix_g = gain(ks[1], D_MODEL)
    w_in = jax.random.normal(ks[2], (DEPTH, D_MODEL, IN_PROJ_DIM), f32) * D_MODEL ** -0.5
    conv_w = jax.random.normal(ks[3], (DEPTH, GDN_CONV, GDN_CONV_DIM), f32) * GDN_CONV ** -0.5
    a_log = jnp.log(jax.random.uniform(ks[4], (DEPTH, GDN_HEADS), f32, 1.0, 16.0))
    dt = jnp.exp(jax.random.uniform(ks[5], (DEPTH, GDN_HEADS), f32, math.log(1e-3), math.log(1e-1)))
    dt_bias = dt + jnp.log(-jnp.expm1(-dt))
    gdn_norm_g = gain(ks[6], GDN_HEAD_V)
    q_norm_g = gain(ks[7], ATT_HEAD_DIM)
    k_norm_g = gain(ks[8], ATT_HEAD_DIM)
    w_out = jax.random.normal(ks[9], (DEPTH, D_MODEL, D_MODEL), f32) * D_MODEL ** -0.5
    norm_mlp_g = gain(ks[10], D_MODEL)
    w_mlp_up = jax.random.normal(ks[11], (DEPTH, D_MODEL, D_FF), f32) * D_MODEL ** -0.5
    w_mlp_down = jax.random.normal(ks[12], (DEPTH, D_FF, D_MODEL), f32) * D_FF ** -0.5
    return {"x": x, "norm_mix_g": norm_mix_g, "w_in": w_in, "conv_w": conv_w,
            "a_log": a_log, "dt_bias": dt_bias, "gdn_norm_g": gdn_norm_g,
            "q_norm_g": q_norm_g, "k_norm_g": k_norm_g, "w_out": w_out,
            "norm_mlp_g": norm_mlp_g, "w_mlp_up": w_mlp_up, "w_mlp_down": w_mlp_down}

def first_block(x, norm_mix_g, w_in, conv_w, a_log, dt_bias, gdn_norm_g, q_norm_g, k_norm_g,
              w_out, norm_mlp_g, w_mlp_up, w_mlp_down):
    for layer in range(DEPTH):
        x = hybrid_layer(x, norm_mix_g[layer], w_in[layer], conv_w[layer], a_log[layer],
                         dt_bias[layer], gdn_norm_g[layer], q_norm_g[layer], k_norm_g[layer],
                         w_out[layer], norm_mlp_g[layer], w_mlp_up[layer], w_mlp_down[layer])
    return x


CHUNK = 64
HEAD_DIM = 64
N_RET_HEADS = 8
N_FOX_HEADS = 8
RET_WIDTH = N_RET_HEADS * HEAD_DIM
FOX_WIDTH = N_FOX_HEADS * HEAD_DIM
MIX_WIDTH = RET_WIDTH + FOX_WIDTH
N_MEM = 256
N_XATTN_HEADS = 4
XATTN_HEAD_DIM = D_MODEL // N_XATTN_HEADS
D_FF_2 = -(-8 * D_MODEL // (3 * 256)) * 256
ROPE_BASE = 10000.0
NEG_INF = -1e30
IN_SIZES = (RET_WIDTH, RET_WIDTH, RET_WIDTH, RET_WIDTH, FOX_WIDTH, FOX_WIDTH, FOX_WIDTH, N_FOX_HEADS)
IN_WIDTH = sum(IN_SIZES)


def _split_points(sizes):
    pts, acc = [], 0
    for s in sizes[:-1]:
        acc += s
        pts.append(acc)
    return pts

def rmsnorm(x, g):
    xf = x.astype(jnp.float32)
    y = xf * lax.rsqrt(jnp.mean(xf * xf, axis=-1, keepdims=True) + EPS)
    return (y * g.astype(jnp.float32)).astype(x.dtype)

def head_group_norm(x, g):
    xf = x.astype(jnp.float32)
    mu = jnp.mean(xf, axis=-1, keepdims=True)
    xc = xf - mu
    var = jnp.mean(xc * xc, axis=-1, keepdims=True)
    return (xc * lax.rsqrt(var + EPS) * g.astype(jnp.float32)).astype(x.dtype)

def rotary(x, pos):
    d = x.shape[-1]
    inv_freq = ROPE_BASE ** (-jnp.arange(0, d, 2, dtype=jnp.float32) / d)
    ang = pos[:, None] * inv_freq[None, :]
    cos = jnp.cos(ang)[:, None, :].astype(x.dtype)
    sin = jnp.sin(ang)[:, None, :].astype(x.dtype)
    x1, x2 = x[..., : d // 2], x[..., d // 2:]
    return jnp.concatenate([x1 * cos - x2 * sin, x1 * sin + x2 * cos], axis=-1)

def chunk_retention(q, k, v):
    B, T, H, d = q.shape
    dv = v.shape[-1]
    nc = T // CHUNK
    dt = q.dtype
    log_g = jnp.log(1.0 - 2.0 ** (-5.0 - jnp.arange(H, dtype=jnp.float32)))
    idx = jnp.arange(CHUNK, dtype=jnp.float32)
    intra_decay = jnp.exp(log_g[:, None, None] * jnp.abs(idx[:, None] - idx[None, :])).astype(dt)
    q_decay = jnp.exp(log_g[None, :] * (idx[:, None] + 1.0)).astype(dt)
    k_decay = jnp.exp(log_g[None, :] * (CHUNK - 1.0 - idx[:, None])).astype(dt)
    chunk_decay = jnp.exp(log_g * CHUNK).astype(dt)[:, None, None]

    qc = (q * (d ** -0.5)).reshape(B, nc, CHUNK, H, d)
    kc = k.reshape(B, nc, CHUNK, H, d)
    vc = v.reshape(B, nc, CHUNK, H, dv)

    scores = jnp.einsum('bnihd,bnjhd->bnhij', qc, kc) * intra_decay
    intra = jnp.einsum('bnhij,bnjhe->bnihe', scores, vc)

    kv = jnp.einsum('bnjhd,bnjhe->nbhde', kc * k_decay[:, :, None], vc)

    def step(state, kv_c):
        return state * chunk_decay + kv_c, state

    _, s_prev = lax.scan(step, jnp.zeros((B, H, d, dv), kv.dtype), kv)
    inter = jnp.einsum('bnihd,nbhde->bnihe', qc * q_decay[:, :, None], s_prev)
    return (intra + inter).reshape(B, T, H, dv)

def forgetting_attention(q, k, v, log_f):
    B, T, H, d = q.shape
    F = jnp.cumsum(log_f, axis=1).transpose(0, 2, 1)
    qh = (q * (d ** -0.5)).transpose(0, 2, 1, 3)
    kh = k.transpose(0, 2, 1, 3)
    vh = v.transpose(0, 2, 1, 3)
    qpos = jnp.arange(Q_BLOCK)
    outs = []
    for blk in range(T // Q_BLOCK):
        q0 = blk * Q_BLOCK
        kend = q0 + Q_BLOCK
        logits = jnp.einsum('bhqd,bhkd->bhqk', qh[:, :, q0:kend], kh[:, :, :kend]).astype(jnp.float32)
        logits = logits + F[:, :, q0:kend, None] - F[:, :, None, :kend]
        causal = (q0 + qpos)[:, None] >= jnp.arange(kend)[None, :]
        logits = jnp.where(causal, logits, NEG_INF)
        p = jax.nn.softmax(logits, axis=-1).astype(v.dtype)
        outs.append(jnp.einsum('bhqk,bhkd->bhqd', p, vh[:, :, :kend]))
    return jnp.concatenate(outs, axis=2).transpose(0, 2, 1, 3)

def memory_cross_attention(hn, mem, w_xq, w_xkv, g_mem, g_xq, g_xk, w_xo):
    B, T, _ = hn.shape
    M = mem.shape[1]
    q = (hn @ w_xq).reshape(B, T, N_XATTN_HEADS, XATTN_HEAD_DIM)
    q = rmsnorm(q, g_xq)
    kv = rmsnorm(mem, g_mem) @ w_xkv
    k, v = jnp.split(kv, 2, axis=-1)
    k = rmsnorm(k.reshape(B, M, N_XATTN_HEADS, XATTN_HEAD_DIM), g_xk)
    v = v.reshape(B, M, N_XATTN_HEADS, XATTN_HEAD_DIM)
    logits = jnp.einsum('bthd,bmhd->bhtm', q, k).astype(jnp.float32) * (XATTN_HEAD_DIM ** -0.5)
    p = jax.nn.softmax(logits, axis=-1).astype(v.dtype)
    o = jnp.einsum('bhtm,bmhd->bthd', p, v).reshape(B, T, D_MODEL)
    return o @ w_xo

def second_inputs(seed: int = 0) -> dict:
    key = jax.random.key(seed)
    ks = jax.random.split(key, 24)
    f32 = jnp.float32
    D = D_MODEL

    def w(k, shape, fan_in):
        return jax.random.normal(k, shape, f32) * fan_in ** -0.5

    def gain(k, shape):
        return 1.0 + 0.02 * jax.random.normal(k, shape, f32)

    return {
        "x": jax.random.normal(ks[0], (BATCH, SEQ, D), f32),
        "mem": jax.random.normal(ks[1], (BATCH, N_MEM, D), f32),
        "g_mix": gain(ks[2], (DEPTH, D)),
        "w_in": w(ks[3], (DEPTH, D, IN_WIDTH), D),
        "b_forget": jax.random.uniform(ks[4], (DEPTH, N_FOX_HEADS), f32, 1.0, 4.0),
        "g_ret_out": gain(ks[5], (DEPTH, N_RET_HEADS, HEAD_DIM)),
        "g_fox_q": gain(ks[6], (DEPTH, HEAD_DIM)),
        "g_fox_k": gain(ks[7], (DEPTH, HEAD_DIM)),
        "w_out": w(ks[8], (DEPTH, MIX_WIDTH, D), MIX_WIDTH),
        "g_xattn": gain(ks[9], (DEPTH, D)),
        "w_xq": w(ks[10], (DEPTH, D, D), D),
        "w_xkv": w(ks[11], (DEPTH, D, 2 * D), D),
        "g_mem": gain(ks[12], (DEPTH, D)),
        "g_xq": gain(ks[13], (DEPTH, XATTN_HEAD_DIM)),
        "g_xk": gain(ks[14], (DEPTH, XATTN_HEAD_DIM)),
        "w_xo": w(ks[15], (DEPTH, D, D), D),
        "g_ffn": gain(ks[16], (DEPTH, D)),
        "w_gate": w(ks[17], (DEPTH, D, D_FF_2), D),
        "w_up": w(ks[18], (DEPTH, D, D_FF_2), D),
        "w_down": w(ks[19], (DEPTH, D_FF_2, D), D_FF_2),
    }

def second_block(x, mem, g_mix, w_in, b_forget, g_ret_out, g_fox_q, g_fox_k, w_out,
              g_xattn, w_xq, w_xkv, g_mem, g_xq, g_xk, w_xo,
              g_ffn, w_gate, w_up, w_down):
    B, T, _ = x.shape
    pos = jnp.arange(T, dtype=jnp.float32)
    splits = _split_points(IN_SIZES)
    h = x
    for l in range(DEPTH):
        hn = rmsnorm(h, g_mix[l])
        proj = hn @ w_in[l]
        rq, rk, rv, rg, fq, fk, fv, ff = jnp.split(proj, splits, axis=-1)

        rq = rotary(rq.reshape(B, T, N_RET_HEADS, HEAD_DIM), pos)
        rk = rotary(rk.reshape(B, T, N_RET_HEADS, HEAD_DIM), pos)
        ret = chunk_retention(rq, rk, rv.reshape(B, T, N_RET_HEADS, HEAD_DIM))
        ret = head_group_norm(ret, g_ret_out[l]).reshape(B, T, RET_WIDTH)
        ret = jax.nn.silu(rg) * ret

        fq = rmsnorm(fq.reshape(B, T, N_FOX_HEADS, HEAD_DIM), g_fox_q[l])
        fk = rmsnorm(fk.reshape(B, T, N_FOX_HEADS, HEAD_DIM), g_fox_k[l])
        log_f = jax.nn.log_sigmoid(ff.astype(jnp.float32) + b_forget[l].astype(jnp.float32))
        fox = forgetting_attention(fq, fk, fv.reshape(B, T, N_FOX_HEADS, HEAD_DIM), log_f)
        fox = fox.reshape(B, T, FOX_WIDTH)

        h = h + jnp.concatenate([ret, fox], axis=-1) @ w_out[l]

        h = h + memory_cross_attention(rmsnorm(h, g_xattn[l]), mem, w_xq[l], w_xkv[l],
                                       g_mem[l], g_xq[l], g_xk[l], w_xo[l])

        hn = rmsnorm(h, g_ffn[l])
        h = h + (jax.nn.silu(hn @ w_gate[l]) * (hn @ w_up[l])) @ w_down[l]
    return h


def setup_inputs(seed=0):
    out = dict(first_inputs(seed))
    for name, value in second_inputs(seed + 1).items():
        if name != "x":
            out[name + "_2"] = value
    return out


def reference(
    x, norm_mix_g, w_in, conv_w, a_log, dt_bias, gdn_norm_g, q_norm_g, k_norm_g, w_out,
    norm_mlp_g, w_mlp_up, w_mlp_down, mem_2, g_mix_2, w_in_2, b_forget_2, g_ret_out_2,
    g_fox_q_2, g_fox_k_2, w_out_2, g_xattn_2, w_xq_2, w_xkv_2, g_mem_2, g_xq_2, g_xk_2, w_xo_2,
    g_ffn_2, w_gate_2, w_up_2, w_down_2,
):
    x = first_block(
        x, norm_mix_g, w_in, conv_w, a_log, dt_bias, gdn_norm_g, q_norm_g, k_norm_g, w_out,
        norm_mlp_g, w_mlp_up, w_mlp_down,
    )
    return second_block(
        x, mem_2, g_mix_2, w_in_2, b_forget_2, g_ret_out_2, g_fox_q_2, g_fox_k_2, w_out_2,
        g_xattn_2, w_xq_2, w_xkv_2, g_mem_2, g_xq_2, g_xk_2, w_xo_2, g_ffn_2, w_gate_2, w_up_2,
        w_down_2,
    )


_drawn_inputs = setup_inputs


def setup_inputs(seed=0):
    import zlib

    import numpy as np

    out = dict(_drawn_inputs(seed))
    spreads = {}
    factors = {'gdn_norm_g': 7.23,
     'q_norm_g': 8.0,
     'k_norm_g': 8.0,
     'norm_mlp_g': 2.917,
     'g_mix_2': 4.637,
     'g_ret_out_2': 8.0,
     'g_fox_q_2': 8.0,
     'g_fox_k_2': 8.0,
     'g_xattn_2': 8.0,
     'g_mem_2': 8.0,
     'g_xq_2': 8.0,
     'g_xk_2': 8.0,
     'g_ffn_2': 15.438}
    for name, (base, spread) in spreads.items():
        noise = np.random.default_rng([zlib.crc32(name.encode()), seed]).standard_normal(out[name].shape)
        drawn = base * np.exp(spread * noise) if base else spread * noise
        out[name] = __import__('jax').numpy.asarray(drawn.astype(out[name].dtype))
    for name, factor in factors.items():
        out[name] = (out[name] * factor).astype(out[name].dtype)
    return out
```

```python
from contextlib import ExitStack

import concourse.bass as bass
from concourse import mybir

F32 = mybir.dt.float32
F32R = mybir.dt.float32r
ALU = mybir.AluOpType
ACT = mybir.ActivationFunctionType
AX_X = mybir.AxisListType.X

P = 128
SEQ = 256
NT = SEQ // P
D = 1024
KT = D // P
EPS = 1e-6
NCOL = 512
CK = 4
SLOTS = 4
DFF = 4096
DFF2 = 2816
MEMORIES = 256

A0 = 4096
A_W = 2136
AQ, AK, AV, IQ, IK, IW = 16, 1040, 1296, 1552, 2064, 2128
RQ, RK, RV, RG, FQ, FK, FV, FG = 0, 512, 1024, 1536, 2048, 2560, 3072, 3584
W2 = 3592

EXCLUDED = -1e30
UNREACHED = -3.0e38
TAKEN = -3.4e38
BETWEEN = -3.2e38

C_ID, C_U64, C_BD, C_SEL, C_ONES, C_CUM, C_TRI, C_TRIX = 0, 128, 256, 384, 640, 768, 1024, 1152
C_UC, C_IC, C_NEG, C_LEV = 1280, 1344, 1408, 1472
C_ROPE_A, C_ROPE_I, C_ROPE_R = 1856, 1920, 1952
C_N = 2080

WORK_A = [(0, range(0, 4)), (0, range(4, 8))] + [(1, range(h, h + 2)) for h in range(0, 8, 2)]
WORK_X = [(t, range(h, h + 2)) for t in range(NT) for h in (0, 2)]


def keys_of(work, k):
    return NCOL // len(work[k][1])



def constants():
    import numpy as np

    c = np.zeros((P, C_N), np.float32)
    row, col = np.arange(P)[:, None], np.arange(P)[None, :]
    same = row // 64 == col // 64
    c[:, C_ID:C_ID + P] = row == col
    c[:, C_U64:C_U64 + P] = same & (row <= col)
    c[:, C_BD:C_BD + P] = same
    c[:64, C_SEL:C_SEL + P] = 1
    c[64:, C_SEL + P:C_SEL + 2 * P] = 1
    c[:, C_ONES:C_ONES + P] = 1
    c[:, C_CUM:C_CUM + P] = row <= col
    c[:, C_TRI:C_TRI + P] = np.where(col <= row, 0, EXCLUDED)
    c[:, C_TRIX:C_TRIX + P] = np.where(col <= row, 0, UNREACHED)
    j, i = np.arange(P)[:, None] % 64, np.arange(64)[None, :]
    c[:, C_UC:C_UC + 64] = j <= i
    c[:, C_IC:C_IC + 64] = j == i
    c[:, C_NEG:C_NEG + 64] = np.where(i >= j, 0, EXCLUDED)
    for n in range(6):
        s = 1 << n
        c[:, C_LEV + 64 * n:C_LEV + 64 * n + 64] = (j // (2 * s) == i // (2 * s)) & (j // s % 2 == 0) & (i // s % 2 == 1)

    def rope(at, half, rot, theta):
        inv = np.float32(theta) ** (-np.arange(0, rot, 2, dtype=np.float32) / np.float32(rot))
        ang = np.arange(SEQ, dtype=np.float32)[:, None] * inv.astype(np.float32)[None, :]
        for t in range(NT):
            a = ang[P * t:P * t + P].astype(np.float64)
            c[:, at + t * half:at + t * half + half] = np.cos(a)
            c[:, at + (NT + t) * half:at + (NT + t) * half + half] = np.sin(a)

    rope(C_ROPE_A, 16, 32, 500000.0)
    rope(C_ROPE_I, 8, 16, 500000.0)
    rope(C_ROPE_R, 32, 64, 10000.0)
    return c


def retention_weights():
    import numpy as np

    w = np.zeros((P, 8 * 384), np.float32)
    s, t = np.arange(SEQ)[:, None], np.arange(SEQ)[None, :]
    for h in range(8):
        gamma = 1.0 - 2.0 ** (-5.0 - h)
        full = np.where(s // 64 <= t // 64, gamma ** np.abs(t - s), 0) / 8
        p, q = h % 2, h // 2
        w[:, 512 * (2 * p + q // 2) + 256 * (q % 2):][:, :256] = full[:P]
        w[:, 2048 + 512 * p + 128 * q:][:, :128] = full[P:, P:]
    return w


def build(nc, x_in, norm_mix_g, w_in, conv_w, a_log, dt_bias, gdn_norm_g, q_norm_g, k_norm_g, w_out,
          norm_mlp_g, w_mlp_up, w_mlp_down, mem_2, g_mix_2, w_in_2, b_forget_2, g_ret_out_2,
          g_fox_q_2, g_fox_k_2, w_out_2, g_xattn_2, w_xq_2, w_xkv_2, g_mem_2, g_xq_2, g_xk_2, w_xo_2,
          g_ffn_2, w_gate_2, w_up_2, w_down_2, consts, ret_w, out):
    ctx = ExitStack()
    with ctx:
        def sb(name, shape, dt=F32, stack=None):
            return (stack or ctx).enter_context(nc.sbuf_tensor(name, shape, dt))

        named = {}

        def sem(name):
            if name not in named:
                named[name] = ctx.enter_context(nc.semaphore(name))
            return named[name]

        blocks = []

        def segment(name, w, first, widths, kt=KT):
            start = len(blocks)
            for width in widths:
                chunk0 = blocks[-1]["chunk0"] + blocks[-1]["chunks"] if blocks else 0
                blocks.append(dict(seg=name, w=w, col=first, n=width, kt=kt, chunk0=chunk0, chunks=-(-kt // CK)))
                first += width
            return start

        win = w_in[0]
        B_A = segment("a", win, A0, [512] * 4 + [88])
        B_Q = segment("qkv", win, 0, [512] * 6)
        B_GB = segment("gate_b", win, 7256, [512] * 2)
        B_Z = segment("z", win, 3072, [512] * 2)
        B_GA = segment("gate_a", win, 6232, [512] * 2)
        B_O = segment("out", w_out[0], 0, [512] * 2)
        B_UP = segment("up", w_mlp_up[0], 0, [512] * 8)
        B_DN = segment("down", w_mlp_down[0], 0, [512] * 2, kt=DFF // P)
        B_2 = segment("in2", w_in_2[0], 0, [512] * 7 + [8])
        B_KV = segment("kv", w_xkv_2[0], 0, [512] * 4)
        B_O2 = segment("out2", w_out_2[0], 0, [512] * 2)
        B_XQ = segment("xq", w_xq_2[0], 0, [512] * 2)
        B_XO = segment("xo", w_xo_2[0], 0, [512] * 2)
        B_GU = len(blocks)
        for c in range(0, DFF2, 512):
            n = min(512, DFF2 - c)
            segment("gate2", w_gate_2[0], c, [n])
            segment("up2", w_up_2[0], c, [n])
        B_D2 = segment("down2", w_down_2[0], 0, [512] * 2, kt=DFF2 // P)
        B_END = len(blocks)

        with nc.sbuf_tensor("raw", [P, SLOTS, CK, NCOL], F32) as raw:
            pass
        w_lo = sb("w_lo", [P, SLOTS, CK, NCOL], F32R)
        w_hi = sb("w_hi", [P, SLOTS, CK, NCOL], F32R)
        s_hi = sb("s_hi", [P, KT, SEQ], F32R)
        s_lo = sb("s_lo", [P, KT, SEQ], F32R)
        x = sb("x", [P, NT, D])
        cst = sb("cst", [P, C_N])
        gains = sb("gains", [P, 6, KT])
        cw = sb("cw", [P, 4, 24])
        vec = sb("vec", [P, 960])
        sm = sb("sm", [P, 640])
        ident = cst[:, C_ID:C_ID + P]
        junk = sb("junk", [P, D], mybir.dt.bfloat16)

        G = [[ctx.enter_context(nc.psum_tensor(f"gemm{s}{t}", [P, NCOL], F32)) for t in range(NT)] for s in range(2)]
        M = [ctx.enter_context(nc.psum_tensor(f"mixbank{i}", [P, NCOL], F32)) for i in range(4)]

        V_QG, V_KG, V_GN, V_DT, V_AL, V_BF, V_FQ, V_FK = 0, 128, 256, 384, 392, 400, 408, 472
        V_XQ, V_XK = 536, 536 + 256
        vec2 = sb("vec2", [P, 512 + 256])
        NORMS = dict(mix=0, mlp=1, mix2=2, xattn=3, mem=4, ffn=5)

        def arena(name, words, stack):
            return sb(name, [P, words], F32, stack)

        a1 = ExitStack()
        ar = arena("mix1", 24800, a1)
        a1.close()
        a2 = ExitStack()
        hT_hi = sb("hT_hi", [P, DFF // P, SEQ], F32R, a2)
        hT_lo = sb("hT_lo", [P, DFF // P, SEQ], F32R, a2)
        hid = sb("hid", [P, 2, NT, NCOL], F32, a2)
        a2.close()
        a3 = ExitStack()
        ar2 = arena("mix2", 24800, a3)
        a3.close()
        a4 = ExitStack()
        h2_hi = sb("h2_hi", [P, DFF2 // P, SEQ], F32R, a4)
        h2_lo = sb("h2_lo", [P, DFF2 // P, SEQ], F32R, a4)
        hid2 = sb("hid2", [P, 2, NT, NCOL], F32, a4)
        sg2 = sb("sg2", [P, 2, NT, NCOL], F32, a4)
        a4.close()

        def view(base, at, *shape):
            n = 1
            for s in shape:
                n *= s
            v = base[:, at:at + n]
            if len(shape) == 1:
                return v
            names = "abcd"[:len(shape)]
            return v.rearrange(f"p ({' '.join(names)}) -> p {' '.join(names)}", **dict(zip(names, shape)))

        def spread(ap, axis, n):
            v = ap.unsqueeze(axis)
            shape = list(v.shape)
            shape[axis] = n
            return v.to_broadcast(shape)

        PA = view(ar, 0, NT, A_W)
        PQ = view(ar, 4272, NT, 3072)
        ZG = view(ar, 10416, NT, D)
        OA = view(ar, 12464, NT, 8, 128)
        TMP = view(ar, 14512, 2, NCOL)
        YT = view(ar, 15536, 24, SEQ)
        FREE1 = 21680
        SQ = view(ar, 15536, NT, 10, 128)
        qT = view(ar, 15536, 8, SEQ)
        kT = view(ar, 17584, 2, SEQ)
        iqT = view(ar, 18096, 4, SEQ)
        ikT = view(ar, 19120, SEQ)
        IKD = view(ar, 19376, NT, 2, 64)
        SC = view(ar, 19632, NT, SEQ)
        BIAS = view(ar, 20144, NT, SEQ)
        RT = view(ar, 20656, 4, NT * 160)
        RTI = view(ar, 21936, 4, NT * 72)
        RL = view(ar, 22512, 8, SEQ)
        LM = view(ar, 20656, 2, NCOL)
        PTS = view(ar, 22512, 2, NCOL)
        KN = view(ar, 4272, NT, 8, 128)
        VB = view(ar, 6320, NT, 8, 128)
        KBG = view(ar, 8368, NT, 8, 128)
        KTN = view(ar, 15536 + 2048, 8, SEQ)
        KD = view(ar, 15536 + 4096, NT, 8, 128)
        DM = view(ar, 0, 16, 64)
        AT = view(ar, 1024, 16, 64)
        QK = view(ar, 2048, 16, 64)
        XI = view(ar, 3072, 16, 64)
        XT = view(ar, 21680, 16, 64)
        LT = view(ar, 22704, 16, 64)
        PS = view(ar, 23728, 16, 64)
        SQ2 = view(ar, 22704, 8, SEQ)
        WT = view(ar, 15536 + 2048, 16, 128)
        UV = view(ar, 22704, NT, 8, 128)
        ST = [None, view(ar, 0, 8, 128), view(ar, 4272, 8, 128), view(ar, 5296, 8, 128)]
        SD = view(ar, 3072, 8, 128)
        O1 = view(ar, 6320, NT, 8, 128)
        SQ3 = view(ar, 8368, NT, 8, 128)

        def st(at, n):
            return sm[:, at:at + n]

        SS, RS = st(0, 12), st(12, 12)
        HRS = st(24, 2)
        QRS = st(26, 2)
        SSA, RNA = st(28, 20), st(48, 20)
        IWS = st(68, 16)
        MX8 = st(84, 16)
        NEGM, SUMS, RSUM = st(100, 32), st(132, 32), st(164, 32)
        GA_, BT = st(196, 16), st(212, 16)
        SP = st(228, 48)
        GC = st(276, 64)
        EG, ED, EL, BEG = st(340, 16), st(356, 16), st(372, 32), st(404, 16)
        SSK, RQK = st(420, 32), st(452, 32)
        SSO, RSO = st(484, 16), st(500, 16)
        HBT = st(516, 16)
        EXPA = st(532, 8)
        MHALF = st(540, 64)
        HALFRS2 = st(604, 4)

        GU, BI = XI, XT
        CT = view(ar, 21680, 2, 2, SEQ)
        hidden_rows, conv_rows = ar[:, 4272:4400], ar[:, 4400:4528]
        FL = st(608, 16).rearrange("p (t h) -> p t h", t=2)
        SSF, RNF = SSK, RQK
        SSX, RNX = st(28, 8), st(48, 16)
        MU, VAR, RSTD = GA_, BT, EG
        RS5H, RS5Q = st(624, 2), st(626, 2)

        P2R = view(ar2, 0, NT, 2048)
        P2F = view(ar2, 4096, NT, W2 - 2048)
        WR = view(ar2, 7184, 3072)
        MG2 = view(ar2, 10256, NT, D)
        MEM = view(ar2, 12304, NT, D)
        T0 = 14352
        RT2 = view(ar2, T0, 4, NT * 512)
        rqT = view(ar2, T0, 4, SEQ)
        rkT = view(ar2, T0 + 1024, 4, SEQ)
        PT2 = view(ar2, T0 + 2048, 3072)
        SQR = view(ar2, 21584, NT, 16, 64)
        TG = view(ar2, T0, NT, NCOL)
        RSQ = view(ar2, T0 + 1024, NT, NCOL)
        QA = view(ar2, 19472, NT, 8, 66)
        KA = view(ar2, 20528, NT, 8, 66)
        qaT = view(ar2, T0, 8, SEQ)
        kaT = view(ar2, T0 + 2048, 8, SEQ)
        LM2 = view(ar2, 21584, 2, NCOL)
        PTS2 = view(ar2, 22608, 2, NCOL)
        KV = view(ar2, 0, NT, 2048)
        XQ = view(ar2, 7184, NT, D)
        XO = view(ar2, 10256, NT, D)
        SQX = view(ar2, T0 + 5120, NT, D)
        xqT = view(ar2, T0, 8, SEQ)
        xkT = view(ar2, T0 + 2048, 8, SEQ)
        KVT = 23632

        block = ctx.enter_context(nc.Block())

        def at(base, step, i):
            return base if i is None else base + step * i

        def chunk_shape(b, c):
            return min(CK, blocks[b]["kt"] - CK * c), blocks[b]["n"]

        def fox_mask(t):
            return cst[:, C_TRI - P * t:C_TRI + P]

        @block.sync
        def _(sp):
            def load(b, c, i=None):
                n = blocks[b]["chunk0"] + c
                kn, width = chunk_shape(b, c)
                slot = n % SLOTS
                if n >= SLOTS:
                    sp.wait_ge(sem("mm_done"), at(n - SLOTS + 1, 4, i))
                rows = blocks[b]["w"][CK * P * c:CK * P * c + kn * P]
                src = rows[:, bass.ds(at(blocks[b]["col"], 2 * NCOL, i), width)]
                sp.dma_start(raw[:, slot, 0:kn, 0:width], src.rearrange("(k p) n -> p k n", p=P))\
                    .then_inc(sem(f"loaded{slot}"), 16)

            for t in range(NT):
                sp.dma_start(x[:, t, :], x_in[0, P * t:P * t + P, :]).then_inc(sem("x_in"), 16)
            b = 0
            while b < B_END:
                pairs = 0
                while (b >= 2 and b + 2 * pairs + 1 < B_END
                       and all(blocks[b + 2 * pairs + j]["seg"] == blocks[b]["seg"] and blocks[b + 2 * pairs + j]["n"] == NCOL
                               and blocks[b + 2 * pairs + j]["chunks"] == 2 for j in range(2))):
                    pairs += 1
                if pairs >= 2:
                    with sp.Fori(0, pairs) as i:
                        for j in range(2):
                            for c in range(2):
                                load(b + j, c, i)
                    b += 2 * pairs
                else:
                    for c in range(blocks[b]["chunks"]):
                        load(b, c)
                    b += 1
            for t in range(NT):
                sp.wait_ge(sem("x_final"), t + 1)
                sp.dma_start(out[0, P * t:P * t + P, :], x[:, t, :]).then_inc(sem("stored"), 16)
            sp.wait_ge(sem("stored"), 16 * NT)

        @block.tensor
        def _(pe):
            act_w = (s_hi, s_lo)

            def mm(b, i=None, stat=act_w, waits=()):
                blk = blocks[b]
                if b >= 2:
                    pe.wait_ge(sem("ev0"), at(b - 1, 2, i))
                    pe.wait_ge(sem("ev1"), at(b - 1, 2, i))
                for s, v in waits:
                    pe.wait_ge(sem(s), v)
                for c in range(blk["chunks"]):
                    n = blk["chunk0"] + c
                    kn, width = chunk_shape(b, c)
                    pe.wait_ge(sem("split_lo"), at(n + 1, 4, i))
                    for k in range(kn):
                        kt = CK * c + k
                        for t in range(NT):
                            o = G[b % 2][t][:, 0:width]
                            hi, lo = (s[:, kt, P * t:P * t + P] for s in stat)
                            wh, wl = (s[:, n % SLOTS, k, 0:width] for s in (w_hi, w_lo))
                            nc.tensor.matmul(o, hi, wh, start=kt == 0, stop=False)
                            nc.tensor.matmul(o, hi, wl, start=False, stop=False)
                            last = nc.tensor.matmul(o, lo, wh, start=False, stop=kt == blk["kt"] - 1)
                    last.then_inc(sem("mm_done"), 1)

            turns = [0]

            def turn(src, waits):
                for q in range(4):
                    for s, v in waits(q):
                        pe.wait_ge(sem(s), v)
                    for kk in range(2):
                        for t in range(NT):
                            last = nc.tensor.transpose(M[q][:, (2 * kk + t) * P:(2 * kk + t + 1) * P], src(2 * q + kk, t), ident)
                    last.then_inc(sem("turn_pe"), 1)
                turns[0] += 4

            def xtile(kt, t):
                return x[:, t, P * kt:P * kt + P]

            pe.wait_ge(sem("consts_in"), 16)
            pe.wait_ge(sem("rows_in"), 16 * 7)
            nc.tensor.transpose(M[0][:, 0:48], hidden_rows[0:48, :], ident[0:48, 0:48])
            nc.tensor.transpose(M[0][:, 128:224], conv_rows[0:96, :], ident[0:96, 0:96]).then_inc(sem("vec_pe"), 1)
            pe.wait_ge(sem("x_in"), 32)
            turn(xtile, lambda q: [("vec_dve", 2)])
            for k in range(5):
                mm(B_A + k, waits=[("turn_lo", 4)])
            mm(B_Q)

            pe.wait_ge(sem("idx_rot"), 1)
            for e in range(8):
                if e >= 4:
                    pe.wait_ge(sem("attT_act" if e % 2 == 0 else "attT_dve"), (e - 4) // 2 + 1)
                if e == 3:
                    pe.wait_ge(sem("att_rot"), 1)
                o = M[e % 4]
                if e < 2:
                    for j in range(2):
                        for t in range(NT):
                            c = IQ + P * (2 * e + j)
                            last = nc.tensor.transpose(o[:, (2 * j + t) * P:(2 * j + t + 1) * P], PA[:, t, c:c + P], ident)
                elif e == 2:
                    for t in range(NT):
                        last = nc.tensor.transpose(o[:, t * P:(t + 1) * P], IKD[:, t].rearrange("p a b -> p (a b)"), ident)
                else:
                    for j in range(2):
                        for t in range(NT):
                            c = (AK + P * j) if e == 3 else AQ + P * (2 * (e - 4) + j)
                            last = nc.tensor.transpose(o[:, (2 * j + t) * P:(2 * j + t + 1) * P], PA[:, t, c:c + P], ident)
                last.then_inc(sem("attT_pe"), 1)
            mm(B_Q + 1)
            pe.wait_ge(sem("attT_act"), 4)
            pe.wait_ge(sem("attT_dve"), 4)

            for t in range(NT):
                for par in (0, 1) if t == 0 else (1, 0):
                    for q in range(4):
                        bank = par if t == 0 else 2 * par + q // 2
                        if t == 1 and par == 0 and q % 2 == 0:
                            pe.wait_ge(sem("relu"), 2)
                        ns = P * (t + 1)
                        o = M[bank][:, (q % (4 // (t + 1))) * ns:][:, 0:ns]
                        last = nc.tensor.matmul(o, iqT[64 * par:64 * par + 64, q, P * t:P * t + P],
                                                ikT[64 * par:64 * par + 64, 0:ns], start=True, stop=True)
                        if q == 3 or (t == 1 and q == 1):
                            last.then_inc(sem("scores"), 1)
            mm(B_Q + 2)
            mm(B_Q + 3)
            mm(B_Q + 4)

            groups = [0]

            def attention(work, queries, keys, values, width, mixed=None, busy=()):
                g0, n = groups[0], len(work)

                def logits(k):
                    t, heads = work[k]
                    ns = keys_of(work, k)
                    g = g0 + k
                    if k >= 2:
                        pe.wait_ge(sem("att_max"), g - 1)
                        pe.wait_ge(sem("att_exp"), g - 1)
                    for j, h in enumerate(heads):
                        parts = queries(h)
                        for e, (qq, kk) in enumerate(zip(parts, keys(h))):
                            last = nc.tensor.matmul(M[g % 2][:, j * ns:(j + 1) * ns], qq[:, P * t:P * t + P], kk[:, 0:ns],
                                                    start=e == 0, stop=e == len(parts) - 1)
                    last.then_inc(sem("att_logits"), 1)

                def turned(k, buf):
                    t, heads = work[k]
                    ns = keys_of(work, k)
                    g = g0 + k
                    pe.wait_ge(sem("att_exp"), g + 1)
                    if k >= 1:
                        pe.wait_ge(sem("att_ptc"), g)
                    for c in range(4):
                        last = nc.tensor.transpose(M[2][:, c * P:(c + 1) * P], buf[:, g % 2, c * P:(c + 1) * P], ident)
                    last.then_inc(sem("att_pt"), 1)

                def weighed(k, pts):
                    t, heads = work[k]
                    ns = keys_of(work, k)
                    g = g0 + k
                    pe.wait_ge(sem("att_ptc"), g + 1)
                    if k >= 1:
                        pe.wait_ge(sem("att_norm"), g)
                    per = ns // P
                    for j, h in enumerate(heads):
                        for s in range(per):
                            last = nc.tensor.matmul(M[3][:, j * width:(j + 1) * width], pts[:, g % 2, (j * per + s) * P:][:, 0:P],
                                                    values(h, s), start=s == 0, stop=s == per - 1)
                    last.then_inc(sem("att_out"), 1)

                buf, pts = mixed
                for s, v in busy:
                    pe.wait_ge(sem(s), v)
                for k in range(n + 2):
                    if k < n:
                        logits(k)
                    if 1 <= k <= n:
                        turned(k - 1, buf)
                    if k >= 2:
                        weighed(k - 2, pts)
                    yield k
                groups[0] += n

            for k in attention(WORK_A, lambda h: [qT[:, h, :]], lambda h: [kT[:, h // 4, :]],
                               lambda h, s: PA[:, s, AV + P * (h // 4):AV + P * (h // 4) + P], P,
                               mixed=(LM, PTS), busy=[("relu", 6)]):
                if k == 3:
                    mm(B_Q + 5)

            pe.wait_ge(sem("att_norm"), 6)
            pe.wait_ge(sem("ev0"), B_Q + 6)
            pe.wait_ge(sem("ev1"), B_Q + 6)
            for e in range(12):
                if e >= 4:
                    pe.wait_ge(sem("conv_dve"), e - 3)
                for j in range(2):
                    for t in range(NT):
                        c = P * (2 * e + j)
                        last = nc.tensor.transpose(M[e % 4][:, (2 * j + t) * P:(2 * j + t + 1) * P], PQ[:, t, c:c + P], ident)
                last.then_inc(sem("conv_pe"), 1)
                if e == 3:
                    mm(B_GB)
                if e == 7:
                    mm(B_GB + 1)

            pe.wait_ge(sem("conv_dve"), 12)
            for part in range(2):
                pe.wait_ge(sem("gdn_sq"), part + 1)
                for t in range(NT):
                    for h in range(8):
                        c = 16 * part + 8 * t + h
                        last = nc.tensor.matmul(M[0][:, c:c + 1], SQ2[:, h, P * t:P * t + P], cst[:, C_ONES:C_ONES + 1], start=True, stop=True)
                last.then_inc(sem("gdn_ss"), 1)
            pe.wait_ge(sem("gdn_g"), 1)
            for e, c in enumerate((C_U64, C_BD, C_SEL, C_SEL + P)):
                last = nc.tensor.matmul(M[1][:, 16 * e:16 * e + 16], cst[:, c:c + P], GA_, start=True, stop=True)
            last.then_inc(sem("gdn_gc"), 1)
            for e in range(8):
                pe.wait_ge(sem("gdn_y"), 12 if e >= 4 else 8)
                if e >= 4:
                    pe.wait_ge(sem("gdn_kv"), e - 3)
                bank = M[(e + 2) % 4]
                if e in (2, 3):
                    pe.wait_ge(sem("gdn_ms" if e == 2 else "gdn_gcc"), 1)
                part, t, half = e // 4, e % 4 // 2, e % 2
                for j in range(4):
                    last = nc.tensor.transpose(bank[:, j * P:(j + 1) * P], YT[:, 8 + 8 * part + 4 * half + j, P * t:P * t + P], ident)
                last.then_inc(sem("gdn_kvT"), 1)
            mm(B_Z)
            for e in range(4):
                pe.wait_ge(sem("gdn_kv"), 8)
                for j in range(2):
                    for t in range(NT):
                        last = nc.tensor.transpose(M[e][:, (2 * j + t) * P:(2 * j + t + 1) * P], KN[:, t, 2 * e + j, :], ident)
                last.then_inc(sem("gdn_ktT"), 1)
            pe.wait_ge(sem("gdn_rows"), 1)
            for e in range(4):
                pe.wait_ge(sem("gdn_kt"), e + 1)
                src = (GU if e < 2 else BI).rearrange("p a b -> p (a b)")
                last = nc.tensor.matmul(M[e][:, :], cst[:, C_BD:C_BD + P], src[:, NCOL * (e % 2):NCOL * (e % 2) + NCOL], start=True, stop=True)
                last.then_inc(sem("gdn_bc"), 1)
            mm(B_Z + 1)
            for e in range(4):
                pe.wait_ge(sem("gdn_dm" if e < 2 else "gdn_db"), 1)
                for h in range(8):
                    for c in range(2):
                        t = e % 2
                        tok = slice(P * t + 64 * c, P * t + 64 * c + 64)
                        rhs = KTN if e < 2 else YT
                        last = nc.tensor.matmul(M[e][64 * c:64 * c + 64, 64 * h:64 * h + 64], KTN[:, h, tok], rhs[:, h, tok], start=True, stop=True)
                last.then_inc(sem("gdn_kk"), 1)

            def small(o, lhsT, rhs):
                for h in range(8):
                    for c in range(2):
                        r = slice(64 * c, 64 * c + 64)
                        last = nc.tensor.matmul(o[r, 64 * h:64 * h + 64], lhsT(r, h), rhs(r, h), start=True, stop=True)
                return last

            for lv in range(6):
                for t in range(NT):
                    if lv == 0:
                        pe.wait_ge(sem("inv_lt"), NT * lv + t + 1)
                        pe.wait_ge(sem("gdn_at"), 2)
                        small(M[t], lambda r, h: LT[r, 8 * t + h, :], lambda r, h: cst[r, C_IC:C_IC + 64]).then_inc(sem("inv_p"), 1)
                        continue
                    pe.wait_ge(sem("inv_lt"), NT * lv + t + 1)
                    pe.wait_ge(sem("inv_x"), NT * (lv - 1) + t + 1)
                    small(M[t], lambda r, h: LT[r, 8 * t + h, :], lambda r, h: XI[r, 8 * t + h, :]).then_inc(sem("inv_p"), 1)
                if lv == 1:
                    mm(B_GA)
                if lv == 3:
                    mm(B_GA + 1)
                if lv > 0:
                    for t in range(NT):
                        pe.wait_ge(sem("inv_pc"), NT * (lv - 1) + t + 1)
                        if lv < 5:
                            if lv == 1:
                                pe.wait_ge(sem("gdn_qk"), 2)
                            small(M[2 + t], lambda r, h: XT[r, 8 * t + h, :], lambda r, h: PS[r, 8 * t + h, :])
                        small(M[t], lambda r, h: PS[r, 8 * t + h, :], lambda r, h: XT[r, 8 * t + h, :]).then_inc(sem("inv_xp"), 1)

            pe.wait_ge(sem("inv_x"), 12)
            pe.wait_ge(sem("gdn_kbg"), 1)
            for c in range(2):
                for half in range(2):
                    r = slice(64 * c, 64 * c + 64)
                    for q in range(8):
                        n = 8 * half + q
                        last = nc.tensor.matmul(M[2 * c + half][:, 64 * q:64 * q + 64], KBG[r, n // 8, n % 8, :], XT[r, n, :], start=True, stop=True)
                    last.then_inc(sem("gdn_w"), 1)
            for e in range(4):
                t, half = e // 2, e % 2
                pe.wait_ge(sem("gdn_wc"), 4)
                for q in range(4):
                    h = 4 * half + q
                    for c in range(2):
                        r = slice(64 * c, 64 * c + 64)
                        last = nc.tensor.matmul(M[e][r, P * q:P * q + P], XT[r, 8 * t + h, :], VB[r, t, h, :], start=True, stop=True)
                last.then_inc(sem("gdn_u"), 1)

            pe.wait_ge(sem("gdn_uc"), 4)
            pe.wait_ge(sem("gdn_kd"), 1)
            for n in range(4):
                t, r = n // 2, slice(64 * (n % 2), 64 * (n % 2) + 64)
                for half in range(2):
                    if n > 0:
                        pe.wait_ge(sem("st_new"), 2 * (n - 1) + half + 1)
                        for q in range(4):
                            h = 4 * half + q
                            last = nc.tensor.matmul(M[half][r, P * q:P * q + P], WT[:, 8 * t + h, r], ST[n][:, h, :], start=True, stop=True)
                        last.then_inc(sem("st_ws"), 1)
                if n < 3:
                    for half in range(2):
                        if n > 0:
                            pe.wait_ge(sem("st_v"), 2 * (n - 1) + half + 1)
                        for q in range(4):
                            h = 4 * half + q
                            last = nc.tensor.matmul(M[2 + half][:, P * q:P * q + P], KD[r, t, h, :], UV[r, t, h, :], start=True, stop=True)
                        last.then_inc(sem("st_kv"), 1)

            for t in range(NT):
                pe.wait_ge(sem("st_v"), 6)
                if t == 1:
                    pe.wait_ge(sem("o_done"), 1)
                for half in range(2):
                    for q in range(4):
                        h = 4 * half + q
                        for c in range(2):
                            n = 2 * t + c
                            r = slice(64 * c, 64 * c + 64)
                            if n > 0:
                                nc.tensor.matmul(M[half][r, P * q:P * q + P], YT[:, h, P * t + 64 * c:P * t + 64 * c + 64], ST[n][:, h, :], start=True, stop=True)
                            last = nc.tensor.matmul(M[2 + half][r, P * q:P * q + P], QK[r, 8 * t + h, :], UV[r, t, h, :], start=True, stop=True)
                last.then_inc(sem("o_pe"), 1)

            turn(lambda kt, t: O1[:, t, kt, :], lambda q: [("o_done", 2)])
            for j in range(2):
                mm(B_O + j, waits=[("turn_lo", 8)])

            turn(xtile, lambda q: [("ev0", B_O + 1 + q // 2), ("ev1", B_O + 1 + q // 2), ("turn_lo", 8)])

            def hidden(b, i, mlp):
                pe.wait_ge(sem(mlp["ready"]), at(b + 1, 2, i))
                for q in range(2):
                    bank = M[2 * (b % 2) + q]
                    if b >= 2 or i is not None:
                        pe.wait_ge(sem(mlp["lo"]), at(2 * (b - 2) + q + 1, 4, i))
                    for kk in range(2):
                        for t in range(NT):
                            c = P * (2 * q + kk)
                            last = nc.tensor.transpose(bank[:, (2 * kk + t) * P:(2 * kk + t + 1) * P], mlp["hid"][:, b % 2, t, c:c + P], ident)
                    last.then_inc(sem(mlp["pe"]), 1)

            mlp1 = dict(ready="hid_sq", lo="hid_lo", pe="hid_pe", hid=hid)
            mm(B_UP, waits=[("turn_lo", 12)])
            mm(B_UP + 1)
            hidden(0, None, mlp1)
            mm(B_UP + 2)
            hidden(1, None, mlp1)
            with pe.Fori(0, 2) as i:
                for j in range(2):
                    mm(B_UP + 3 + j, i)
                    hidden(2 + j, i, mlp1)
            mm(B_UP + 7)
            hidden(6, None, mlp1)
            hidden(7, None, mlp1)
            for j in range(2):
                mm(B_DN + j, stat=(hT_hi, hT_lo), waits=[("hid_lo", 16)])

            turn(xtile, lambda q: [("ev0", B_DN + 1 + q // 2), ("ev1", B_DN + 1 + q // 2), ("hid_lo", 16)])
            for j in range(4):
                mm(B_2 + j, waits=[("turn_lo", 16)])
            pe.wait_ge(sem("ret_rot"), 1)
            for e in range(4):
                for j in range(2):
                    for t in range(NT):
                        c = (RQ if e < 2 else RK) + P * (2 * (e % 2) + j)
                        last = nc.tensor.transpose(M[e][:, (2 * j + t) * P:(2 * j + t + 1) * P], P2R[:, t, c:c + P], ident)
                last.then_inc(sem("retT"), 1)
            mm(B_2 + 4)
            mm(B_2 + 5)
            pe.wait_ge(sem("ret_act"), 2)
            pe.wait_ge(sem("ret_dve"), 2)
            for par in range(2):
                for half in range(2):
                    e = 2 * par + half
                    for j in range(2):
                        q = 2 * half + j
                        last = nc.tensor.matmul(M[e][:, 256 * j:256 * j + 256], rkT[64 * par:64 * par + 64, q, 0:P],
                                                rqT[64 * par:64 * par + 64, q, :], start=True, stop=True)
                    last.then_inc(sem("ret_s"), 1)
            for par in range(2):
                pe.wait_ge(sem("ret_w"), par + 1)
                for q in range(4):
                    last = nc.tensor.matmul(M[par][:, P * q:P * q + P], rkT[64 * par:64 * par + 64, q, P:2 * P],
                                            rqT[64 * par:64 * par + 64, q, P:2 * P], start=True, stop=True)
                last.then_inc(sem("ret_s"), 1)
            mm(B_2 + 6)
            mm(B_2 + 7)
            pe.wait_ge(sem("ret_w"), 6)
            for t in range(NT):
                for h in range(8):
                    par, q = h % 2, h // 2
                    o = M[2 + t][:, 64 * h:64 * h + 64]
                    early = PT2[:, 512 * (2 * par + q // 2) + 256 * (q % 2) + P * t:][:, 0:P]
                    v = [P2R[:, s, RV + 64 * h:RV + 64 * h + 64] for s in range(2)]
                    last = nc.tensor.matmul(o, early, v[0], start=True, stop=t == 0)
                    if t == 1:
                        late = PT2[:, 2048 + 512 * par + P * q:][:, 0:P]
                        last = nc.tensor.matmul(o, late, v[1], start=False, stop=True)
                last.then_inc(sem("ret_o"), 1)

            pe.wait_ge(sem("mem_in"), 32)
            turn(lambda kt, t: MEM[:, t, P * kt:P * kt + P], lambda q: [("ret_oc", 2)])
            pe.wait_ge(sem("fox_f"), 1)
            pe.wait_ge(sem("turn_lo"), 17)
            nc.tensor.matmul(M[0][:, 0:8], cst[:, C_CUM:C_CUM + P], FL[:, 0, :], start=True, stop=True)
            nc.tensor.matmul(M[0][:, 8:16], cst[:, C_ONES:C_ONES + P], FL[:, 0, :], start=True, stop=False)
            nc.tensor.matmul(M[0][:, 8:16], cst[:, C_CUM:C_CUM + P], FL[:, 1, :], start=False, stop=True).then_inc(sem("fox_fc"), 1)
            mm(B_KV, waits=[("turn_lo", 20)])
            mm(B_KV + 1)
            pe.wait_ge(sem("fox_aug"), 1)
            for e in range(8):
                src = QA if e < 4 else KA
                if e >= 4:
                    pe.wait_ge(sem("foxT_act" if e % 2 == 0 else "foxT_dve"), (e - 4) // 2 + 1)
                for j in range(2):
                    for t in range(NT):
                        last = nc.tensor.transpose(M[e % 4][0:66, (2 * j + t) * P:(2 * j + t + 1) * P], src[:, t, 2 * (e % 4) + j, :], ident)
                last.then_inc(sem("foxT_pe"), 1)
            pe.wait_ge(sem("foxT_act"), 4)
            pe.wait_ge(sem("foxT_dve"), 4)
            for k in attention(WORK_A, lambda h: [qaT[0:66, h, :]], lambda h: [kaT[0:66, h, :]],
                               lambda h, s: P2F[:, s, FV - 2048 + 64 * h:FV - 2048 + 64 * h + 64], 64, mixed=(LM2, PTS2)):
                if k == 1:
                    mm(B_KV + 2)
                if k == 4:
                    mm(B_KV + 3)
            turn(lambda kt, t: MG2[:, t, P * kt:P * kt + P], lambda q: [("att_norm", 12), ("ret_done", 1)])
            for j in range(2):
                mm(B_O2 + j, waits=[("turn_lo", 24)])

            turn(xtile, lambda q: [("ev0", B_O2 + 1 + q // 2), ("ev1", B_O2 + 1 + q // 2), ("turn_lo", 24)])
            for j in range(2):
                mm(B_XQ + j, waits=[("turn_lo", 28)])
            for e in range(8):
                pe.wait_ge(sem("x_k" if e < 4 else "x_q"), 1)
                if e >= 4:
                    pe.wait_ge(sem("xT_act" if e % 2 == 0 else "xT_dve"), (e - 4) // 2 + 1)
                for j in range(2):
                    for t in range(NT):
                        c = P * (2 * (e % 4) + j)
                        src = (KV if e < 4 else XQ)[:, t, c:c + P]
                        last = nc.tensor.transpose(M[e % 4][:, (2 * j + t) * P:(2 * j + t + 1) * P], src, ident)
                last.then_inc(sem("xT_pe"), 1)
            pe.wait_ge(sem("xT_act"), 4)
            pe.wait_ge(sem("xT_dve"), 4)
            for k in attention(WORK_X, lambda h: [xqT[:, 2 * h + e, :] for e in range(2)],
                               lambda h: [xkT[:, 2 * h + e, :] for e in range(2)],
                               lambda h, s: KV[:, s, D + 256 * h:D + 256 * h + 256], 256, mixed=(LM2, PTS2)):
                pass
            turn(lambda kt, t: XO[:, t, P * kt:P * kt + P], lambda q: [("att_norm", 16)])
            for j in range(2):
                mm(B_XO + j, waits=[("turn_lo", 32)])

            turn(xtile, lambda q: [("ev0", B_XO + 1 + q // 2), ("ev1", B_XO + 1 + q // 2), ("turn_lo", 32)])
            mlp2 = dict(ready="hid2_sq", lo="hid2_lo", pe="hid2_pe", hid=hid2)

            def hidden2(p, i=None, q_n=2):
                pe.wait_ge(sem("hid2_sq"), at(p + 1, 1, i))
                for q in range(q_n):
                    if p >= 1 or i is not None:
                        pe.wait_ge(sem("hid2_lo"), at(2 * (p - 1) + q + 1, 2, i))
                    for kk in range(2):
                        for t in range(NT):
                            c = P * (2 * q + kk)
                            last = nc.tensor.transpose(M[q][:, (2 * kk + t) * P:(2 * kk + t + 1) * P], hid2[:, 0, t, c:c + P], ident)
                    last.then_inc(sem("hid2_pe"), 1)

            for j in range(2):
                mm(B_GU + j, waits=[("turn_lo", 36)])
            mm(B_GU + 2)
            hidden2(0)
            with pe.Fori(0, 3) as i:
                mm(B_GU + 3, i)
                mm(B_GU + 4, i)
                hidden2(1, i)
            mm(B_GU + 9)
            mm(B_GU + 10)
            hidden2(4)
            mm(B_GU + 11)
            hidden2(5, q_n=1)
            for j in range(2):
                mm(B_D2 + j, stat=(h2_hi, h2_lo), waits=[("hid2_lo", 11)])

        @block.scalar
        def _(act):
            seen = {}

            def sig(ins, name):
                seen[name] = seen.get(name, 0) + 1
                ins.then_inc(sem(name), 1)

            def own(name):
                act.wait_ge(sem(name), seen[name])

            def split(b, c, i=None):
                n = blocks[b]["chunk0"] + c
                kn, width = chunk_shape(b, c)
                act.wait_ge(sem(f"loaded{n % SLOTS}"), at(16 * (n // SLOTS + 1), 16, i))
                nc.scalar.activation(w_hi[:, n % SLOTS, 0:kn, 0:width], raw[:, n % SLOTS, 0:kn, 0:width], ACT.Copy)\
                    .then_inc(sem("split_hi"), 1)

            def begin(b, i=None):
                for c in range(2, blocks[b]["chunks"]):
                    split(b, c, i)
                if b + 1 < B_END:
                    for c in range(2):
                        split(b + 1, c, i)

            def mm_finished(b, i=None):
                act.wait_ge(sem("mm_done"), at(blocks[b]["chunk0"] + blocks[b]["chunks"], 4, i))

            def project(b, dst, scale, i=None):
                mm_finished(b, i)
                nc.scalar.activation(dst, G[b % 2][0][:, 0:blocks[b]["n"]], ACT.Copy, scale=scale).then_inc(sem("ev0"), 1)

            def turn_hi(norm=None):
                for q in range(4):
                    act.wait_ge(sem("turn_pe"), seen.get("turn_hi", 0) + 1)
                    if norm is None:
                        ins = nc.scalar.activation(s_hi[:, 2 * q:2 * q + 2, :], M[q].rearrange("p (a b) -> p a b", a=2), ACT.Copy)
                    else:
                        for kk in range(2):
                            ins = nc.scalar.activation(s_hi[:, 2 * q + kk, :], M[q][:, SEQ * kk:SEQ * kk + SEQ], ACT.Copy,
                                                       scale=gains[:, norm, 2 * q + kk:2 * q + kk + 1])
                    sig(ins, "turn_hi")

            def squares(norm, src):
                for t in range(NT):
                    if norm + t > 0:
                        act.wait_ge(sem("stat_ss"), 2 * norm + t)
                    nc.scalar.activation(junk[:, :], src[:, t, :], ACT.Square, accum_out=SS[:, 2 * norm + t:2 * norm + t + 1])\
                        .then_inc(sem("stat_ss"), 1)

            act.dma_start(cst[:, :], consts).then_inc(sem("consts_in"), 16)
            for n, g in enumerate((norm_mix_g, norm_mlp_g, g_mix_2, g_xattn_2, g_mem_2, g_ffn_2)):
                act.dma_start(hidden_rows[8 * n:8 * n + 8, :], g[0].rearrange("(k p) -> k p", p=P)).then_inc(sem("rows_in"), 16)
            act.dma_start(conv_rows[0:96, :], conv_w[0].rearrange("j (k p) -> (j k) p", p=P)).then_inc(sem("rows_in"), 16)
            split(0, 0)
            split(0, 1)
            turn_hi(NORMS["mix"])
            act.wait_ge(sem("x_in"), 32)
            squares(0, x)
            act.wait_ge(sem("stat_rs"), 1)
            for k in range(4):
                begin(B_A + k)
                project(B_A + k, PA[:, 0, NCOL * k:NCOL * k + NCOL], RS[:, 0:1])
            begin(B_A + 4)
            project(B_A + 4, PA[:, 0, 2048:A_W], RS[:, 0:1])
            begin(B_Q)
            act.wait_ge(sem("ev1"), 5)
            act.wait_ge(sem("ev0"), 5)
            for t in range(NT):
                ins = nc.scalar.activation(SQ[:, t], PA[:, t, AQ:AV].rearrange("p (h d) -> p h d", d=P), ACT.Square)
            ins.then_inc(sem("att_sq"), 1)
            act.wait_ge(sem("vec_in"), 16 * 11)
            nc.scalar.activation(SP[:, 40:48], vec[:, V_AL:V_AL + 8], ACT.Exp)
            act.wait_ge(sem("g_abs"), 1)
            sig(nc.scalar.activation(SP[:, 16:32], SP[:, 0:16], ACT.Exp, scale=-1.0), "g_exp")
            sig(nc.scalar.activation(BT.rearrange("p (t h) -> p t h", t=2), PA[:, :, 8:16], ACT.Tanh, scale=0.5), "b_tanh")
            own("g_exp")
            nc.scalar.activation(SP[:, 16:32], SP[:, 16:32], ACT.Ln, bias=1.0).then_inc(sem("g_ln"), 1)
            project(B_Q, PQ[:, 0, 0:NCOL], RS[:, 0:1])
            begin(B_Q + 1)
            for e, dst in ((0, iqT[:, 0:2, :]), (2, ikT), (4, qT[:, 0:2, :]), (6, qT[:, 4:6, :])):
                act.wait_ge(sem("attT_pe"), e + 1)
                if e == 2:
                    ins = nc.scalar.activation(dst, M[2][:, 0:SEQ], ACT.Copy)
                else:
                    ins = nc.scalar.activation(dst, M[e % 4].rearrange("p (a b) -> p a b", a=2), ACT.Copy)
                sig(ins, "attT_act")
            project(B_Q + 1, PQ[:, 0, NCOL:2 * NCOL], RS[:, 0:1])
            begin(B_Q + 2)
            act.wait_ge(sem("scores"), 1)
            nc.scalar.activation(RL[:, 0:8:2, 0:P], M[0].rearrange("p (a b) -> p a b", a=4), ACT.Relu).then_inc(sem("relu"), 1)
            act.wait_ge(sem("scores"), 2)
            nc.scalar.activation(RL[:, 1:8:2, 0:P], M[1].rearrange("p (a b) -> p a b", a=4), ACT.Relu).then_inc(sem("relu"), 1)
            act.wait_ge(sem("acc"), 1)
            for n, (bank, h0) in enumerate(((2, 1), (3, 5), (0, 0), (1, 4))):
                act.wait_ge(sem("scores"), 3 + n)
                nc.scalar.activation(RL[:, h0:h0 + 3:2, :], M[bank].rearrange("p (a b) -> p a b", a=2), ACT.Relu).then_inc(sem("relu"), 1)
            for k in (2, 3, 4):
                project(B_Q + k, PQ[:, 0, NCOL * k:NCOL * k + NCOL], RS[:, 0:1])
                begin(B_Q + k + 1)

            groups = [0]

            def attention(work, scale, src, dst):
                for k, (t, heads) in enumerate(work):
                    g = groups[0] + k
                    ns = keys_of(work, k)
                    act.wait_ge(sem("att_max"), g + 1)
                    if k >= 2:
                        act.wait_ge(sem("att_pt"), g - 1)
                    for j, h in enumerate(heads):
                        ins = nc.scalar.activation(dst[:, g % 2, j * ns:(j + 1) * ns], src(g)[:, j * ns:(j + 1) * ns], ACT.Exp, scale=scale,
                                                   bias=NEGM[:, 4 * (g % 8) + j:4 * (g % 8) + j + 1],
                                                   accum_out=SUMS[:, 4 * (g % 8) + j:4 * (g % 8) + j + 1])
                    ins.then_inc(sem("att_exp"), 1)
                    yield k
                groups[0] += len(work)

            for k in attention(WORK_A, P ** -0.5, lambda g: LM[:, g % 2], LM):
                if k == 3:
                    project(B_Q + 5, PQ[:, 0, NCOL * 5:NCOL * 6], RS[:, 0:1])
                    begin(B_GB)

            def gate(b, dst, t, scale, after=()):
                mm_finished(b)
                for s, v in after:
                    act.wait_ge(sem(s), v)
                return nc.scalar.activation(dst, G[b % 2][t][:, :], ACT.Tanh, scale=scale)

            for e in range(12):
                act.wait_ge(sem("conv_pe"), e + 1)
                for j in range(2):
                    ct = 2 * e + j
                    ins = nc.scalar.activation(YT[:, ct, :], M[e % 4][:, SEQ * j:SEQ * j + SEQ], ACT.Copy, scale=cw[:, 3, ct:ct + 1])
                ins.then_inc(sem("conv_act"), 1)
                if e >= 1:
                    act.wait_ge(sem("conv_dve"), e)
                    if e >= 3:
                        act.wait_ge(sem("gdn_y"), e - 2)
                    nc.scalar.activation(CT[:, (e - 1) % 2], YT[:, 2 * e - 2:2 * e, :], ACT.Tanh, scale=0.5).then_inc(sem("conv_tanh"), 1)
                if e in (5, 9):
                    b = B_GB + (e == 9)
                    for t in range(NT):
                        gate(b, TMP[:, t], t, HRS[:, t:t + 1], [("gate_used", b - B_GB)] if b > B_GB else []).then_inc(sem(f"ev{t}"), 1)
                    begin(b + 1)
            act.wait_ge(sem("conv_dve"), 12)
            act.wait_ge(sem("gdn_y"), 10)
            nc.scalar.activation(CT[:, 1], YT[:, 22:24, :], ACT.Tanh, scale=0.5).then_inc(sem("conv_tanh"), 1)
            act.wait_ge(sem("gdn_y"), 12)
            nc.scalar.activation(SQ2, YT[:, 0:8, :], ACT.Square).then_inc(sem("gdn_sq"), 1)
            act.wait_ge(sem("gdn_ss"), 1)
            nc.scalar.activation(SQ2, YT[:, 8:16, :], ACT.Square).then_inc(sem("gdn_sq"), 1)
            act.wait_ge(sem("gdn_gcc"), 2)
            nc.scalar.activation(EG, GC[:, 0:16], ACT.Exp)
            nc.scalar.activation(ED, GC[:, 16:32], ACT.Exp)
            nc.scalar.activation(EL, GC[:, 32:64], ACT.Exp).then_inc(sem("gdn_e"), 1)
            for k in range(2):
                if k == 1:
                    for e in range(4):
                        act.wait_ge(sem("gdn_ktT"), e + 1)
                        nc.scalar.activation(KTN[:, 2 * e:2 * e + 2, :], M[e].rearrange("p (a b) -> p a b", a=2), ACT.Copy).then_inc(sem("gdn_kt"), 1)
                if k == 0:
                    for t in range(NT):
                        sig(gate(B_Z, ZG[:, t, 0:NCOL], t, HRS[:, t:t + 1]), "z_tanh")
                    begin(B_Z + 1)
            act.wait_ge(sem("gdn_dm0"), 1)
            nc.scalar.activation(DM, DM, ACT.Exp).then_inc(sem("gdn_dme"), 1)
            for t in range(NT):
                sig(gate(B_Z + 1, ZG[:, t, NCOL:D], t, HRS[:, t:t + 1]), "z_tanh")
            begin(B_GA)
            for lv in range(1, 6):
                for t in range(NT):
                    act.wait_ge(sem("inv_p"), NT * lv + t + 1)
                    if lv > 1:
                        act.wait_ge(sem("inv_xp"), NT * (lv - 2) + t + 1)
                    nc.scalar.activation(PS[:, 8 * t:8 * t + 8, :], M[t].rearrange("p (a b) -> p a b", a=8), ACT.Copy).then_inc(sem("inv_pc"), 1)
                if lv in (2, 4):
                    b = B_GA + (lv == 4)
                    for t in range(NT):
                        gate(b, TMP[:, t], t, HRS[:, t:t + 1], [("gate_used", 2 + (lv == 4))]).then_inc(sem(f"ev{t}"), 1)
                    begin(b + 1)
            for e in range(4):
                act.wait_ge(sem("gdn_w"), e + 1)
                c, half = e // 2, e % 2
                nc.scalar.activation(WT[:, 8 * half:8 * half + 8, 64 * c:64 * c + 64], M[e].rearrange("p (a b) -> p a b", a=8), ACT.Copy).then_inc(sem("gdn_wc"), 1)
            for e in range(4):
                act.wait_ge(sem("gdn_u"), e + 1)
                t, half = e // 2, e % 2
                nc.scalar.activation(UV[:, t, 4 * half:4 * half + 4, :], M[e].rearrange("p (a b) -> p a b", a=4), ACT.Copy).then_inc(sem("gdn_uc"), 1)
            act.wait_ge(sem("o_scaled"), 1)
            nc.scalar.activation(SQ3, O1, ACT.Square).then_inc(sem("o_sq"), 1)
            turn_hi()
            begin(B_O + 1)
            turn_hi(NORMS["mlp"])
            act.wait_ge(sem("ev0"), B_UP)
            act.wait_ge(sem("ev1"), B_UP)
            squares(1, x)

            def square_hidden(b, i=None):
                for t in range(NT):
                    act.wait_ge(sem(f"ev{t}"), at(B_UP + b + 1, 2, i))
                    ins = nc.scalar.activation(hid[:, b % 2, t], hid[:, b % 2, t], ACT.Square)
                ins.then_inc(sem("hid_sq"), 1)

            def hidden_hi(b, i=None):
                for q in range(2):
                    act.wait_ge(sem("hid_pe"), at(2 * b + q + 1, 4, i))
                    nc.scalar.activation(hT_hi[:, bass.ds(at(4 * b + 2 * q, 8, i), 2), :], M[2 * (b % 2) + q].rearrange("p (a b) -> p a b", a=2), ACT.Copy)\
                        .then_inc(sem("hid_hi"), 1)

            begin(B_UP)
            square_hidden(0)
            with act.Fori(0, 3) as i:
                for j in range(2):
                    begin(B_UP + 1 + j, i)
                    hidden_hi(j, i)
                    square_hidden(1 + j, i)
            begin(B_UP + 7)
            hidden_hi(6)
            square_hidden(7)
            hidden_hi(7)
            begin(B_DN)
            begin(B_DN + 1)
            turn_hi(NORMS["mix2"])
            act.wait_ge(sem("ev0"), B_2)
            act.wait_ge(sem("ev1"), B_2)
            act.dma_start(WR, ret_w).then_inc(sem("ret_w_in"), 16)
            act.dma_start(MEM, mem_2[0].rearrange("(t p) d -> p t d", p=P)).then_inc(sem("mem_in"), 32)
            squares(2, x)
            act.wait_ge(sem("stat_rs"), 3)
            rs2 = RS[:, 4:5]
            for k in range(4):
                begin(B_2 + k)
                project(B_2 + k, P2R[:, 0, NCOL * k:NCOL * k + NCOL], rs2)
            begin(B_2 + 4)
            for e, dst in ((0, rqT[:, 0:2, :]), (2, rkT[:, 0:2, :])):
                act.wait_ge(sem("retT"), e + 1)
                nc.scalar.activation(dst, M[e].rearrange("p (a b) -> p a b", a=2), ACT.Copy).then_inc(sem("ret_act"), 1)
            project(B_2 + 4, P2F[:, 0, 0:NCOL], rs2)
            begin(B_2 + 5)
            project(B_2 + 5, P2F[:, 0, NCOL:2 * NCOL], rs2)
            act.wait_ge(sem("ev0"), B_2 + 6)
            act.wait_ge(sem("ev1"), B_2 + 6)
            for t in range(NT):
                ins = nc.scalar.activation(SQR[:, t], P2F[:, t, 0:1024].rearrange("p (h d) -> p h d", d=64), ACT.Square)
            ins.then_inc(sem("fox_sq"), 1)
            begin(B_2 + 6)
            project(B_2 + 6, P2F[:, 0, 2 * NCOL:3 * NCOL], rs2)
            begin(B_2 + 7)
            project(B_2 + 7, P2F[:, 0, 1536:1544], rs2)
            act.wait_ge(sem("ret_o"), 1)
            act.wait_ge(sem("ev0"), B_2 + 4)
            act.wait_ge(sem("ev1"), B_2 + 4)
            nc.scalar.activation(TG, P2R[:, :, RG:RG + NCOL], ACT.Tanh, scale=0.5).then_inc(sem("rg_tanh"), 1)
            for t in range(NT):
                act.wait_ge(sem("ret_o"), t + 1)
                nc.scalar.activation(MG2[:, t, 0:NCOL], M[2 + t][:, :], ACT.Copy).then_inc(sem("ret_oc"), 1)
            act.wait_ge(sem("ret_cen"), 1)
            nc.scalar.activation(RSQ, MG2[:, :, 0:NCOL], ACT.Square).then_inc(sem("ret_sq"), 1)
            act.wait_ge(sem("f_abs"), 1)
            sig(nc.scalar.activation(SP[:, 16:32], SP[:, 0:16], ACT.Exp, scale=-1.0), "g_exp")
            own("g_exp")
            nc.scalar.activation(SP[:, 16:32], SP[:, 16:32], ACT.Ln, bias=1.0).then_inc(sem("f_ln"), 1)
            turn_hi(NORMS["mem"])
            squares(3, MEM)
            act.wait_ge(sem("stat_rs"), 4)
            rs4 = RS[:, 6:7]
            begin(B_KV)
            project(B_KV, KV[:, 0, 0:NCOL], rs4)
            begin(B_KV + 1)
            project(B_KV + 1, KV[:, 0, NCOL:D], rs4)
            for e in range(0, 8, 2):
                act.wait_ge(sem("foxT_pe"), e + 1)
                dst = (qaT if e < 4 else kaT)[0:66, 2 * (e % 4):2 * (e % 4) + 2, :]
                nc.scalar.activation(dst, M[e % 4][0:66, :].rearrange("p (a b) -> p a b", a=2), ACT.Copy).then_inc(sem("foxT_act"), 1)
            begin(B_KV + 2)
            for k in attention(WORK_A, 1.0, lambda g: LM2[:, g % 2], LM2):
                if k == 1:
                    project(B_KV + 2, KV[:, 0, D:D + NCOL], rs4)
                    begin(B_KV + 3)
                if k == 4:
                    project(B_KV + 3, KV[:, 0, D + NCOL:2 * D], rs4)
                    begin(B_O2)
            turn_hi()
            act.wait_ge(sem("ev0"), B_O2)
            act.wait_ge(sem("ev1"), B_O2)
            nc.scalar.activation(SQX, KV[:, :, 0:D], ACT.Square).then_inc(sem("x_sqk"), 1)
            begin(B_O2 + 1)
            turn_hi(NORMS["xattn"])
            act.wait_ge(sem("ev0"), B_XQ)
            act.wait_ge(sem("ev1"), B_XQ)
            squares(4, x)
            act.wait_ge(sem("stat_rs"), 5)
            for k in range(2):
                begin(B_XQ + k)
                project(B_XQ + k, XQ[:, 0, NCOL * k:NCOL * k + NCOL], RS[:, 8:9])
            for e in range(0, 8, 2):
                if e == 4:
                    act.wait_ge(sem("ev0"), B_XO)
                    act.wait_ge(sem("ev1"), B_XO)
                    act.wait_ge(sem("x_ms"), 1)
                    nc.scalar.activation(SQX, XQ, ACT.Square).then_inc(sem("x_sqq"), 1)
                act.wait_ge(sem("xT_pe"), e + 1)
                dst = (xkT if e < 4 else xqT)[:, 2 * (e % 4):2 * (e % 4) + 2, :]
                nc.scalar.activation(dst, M[e % 4].rearrange("p (a b) -> p a b", a=2), ACT.Copy).then_inc(sem("xT_act"), 1)
            for k in attention(WORK_X, 1 / 16, lambda g: M[g % 2], LM2):
                pass
            turn_hi()
            begin(B_XO)
            begin(B_XO + 1)
            turn_hi(NORMS["ffn"])
            act.wait_ge(sem("ev0"), B_GU)
            act.wait_ge(sem("ev1"), B_GU)
            squares(5, x)
            act.wait_ge(sem("stat_rs"), 6)

            def gate_tanh(p, i=None):
                b = B_GU + 2 * p
                mm_finished(b, i)
                n = blocks[b]["n"]
                for t in range(NT):
                    if i is not None or p > 0:
                        act.wait_ge(sem(f"ev{t}"), at(b - 1, 2, i))
                    nc.scalar.activation(sg2[:, 0, t, 0:n], G[b % 2][t][:, 0:n], ACT.Tanh, scale=RS5H[:, t:t + 1]).then_inc(sem("gate_tanh"), 1)

            def scale_hidden(p, i=None):
                n = blocks[B_GU + 2 * p]["n"]
                for t in range(NT):
                    act.wait_ge(sem(f"ev{t}"), at(B_GU + 2 * p + 2, 2, i))
                    ins = nc.scalar.activation(hid2[:, 0, t, 0:n], hid2[:, 0, t, 0:n], ACT.Copy, scale=RS5Q[:, t:t + 1])
                ins.then_inc(sem("hid2_sq"), 1)

            def hidden2_hi(p, i=None, q_n=2):
                for q in range(q_n):
                    act.wait_ge(sem("hid2_pe"), at(2 * p + q + 1, 2, i))
                    nc.scalar.activation(h2_hi[:, bass.ds(at(4 * p + 2 * q, 4, i), 2), :], M[q].rearrange("p (a b) -> p a b", a=2), ACT.Copy)\
                        .then_inc(sem("hid2_hi"), 1)

            act.wait_ge(sem("rs5"), 1)
            begin(B_GU)
            gate_tanh(0)
            begin(B_GU + 1)
            scale_hidden(0)
            with act.Fori(0, 3) as i:
                begin(B_GU + 2, i)
                gate_tanh(1, i)
                begin(B_GU + 3, i)
                hidden2_hi(0, i)
                scale_hidden(1, i)
            begin(B_GU + 8)
            gate_tanh(4)
            begin(B_GU + 9)
            hidden2_hi(3)
            scale_hidden(4)
            begin(B_GU + 10)
            gate_tanh(5)
            begin(B_GU + 11)
            hidden2_hi(4)
            scale_hidden(5)
            hidden2_hi(5, q_n=1)
            begin(B_D2)
            begin(B_D2 + 1)

        @block.vector
        def _(dve):
            seen = {}
            V = nc.vector

            def sig(ins, name):
                seen[name] = seen.get(name, 0) + 1
                ins.then_inc(sem(name), 1)

            def link(ins):
                sig(ins, "dve_step")
                dve.wait_ge(sem("dve_step"), seen["dve_step"])

            def split(b, c, i=None):
                n = blocks[b]["chunk0"] + c
                kn, width = chunk_shape(b, c)
                dve.wait_ge(sem("split_hi"), at(n + 1, 4, i))
                s = n % SLOTS
                V.tensor_tensor(w_lo[:, s, 0:kn, 0:width], raw[:, s, 0:kn, 0:width], w_hi[:, s, 0:kn, 0:width].bitcast(F32), ALU.subtract)\
                    .then_inc(sem("split_lo"), 1)

            def begin(b, i=None):
                for c in range(2, blocks[b]["chunks"]):
                    split(b, c, i)
                if b + 1 < B_END:
                    for c in range(2):
                        split(b + 1, c, i)

            def mm_finished(b, i=None):
                dve.wait_ge(sem("mm_done"), at(blocks[b]["chunk0"] + blocks[b]["chunks"], 4, i))

            def project(b, dst, scale, i=None):
                mm_finished(b, i)
                V.tensor_scalar(dst, G[b % 2][1][:, 0:blocks[b]["n"]], scale, None, ALU.mult).then_inc(sem("ev1"), 1)

            def residual(b, half, last=False):
                mm_finished(b)
                for t in range(NT):
                    cols = x[:, t, NCOL * half:NCOL * half + NCOL]
                    ins = V.tensor_tensor(cols, G[b % 2][t][:, :], cols, ALU.add)
                    ins.then_inc(sem("x_final") if last else sem(f"ev{t}"), 1)

            def turn_lo(norm=None):
                for q in range(4):
                    dve.wait_ge(sem("turn_hi"), seen.get("turn_lo", 0) + 1)
                    if norm is None:
                        hi = s_hi[:, 2 * q:2 * q + 2, :].bitcast(F32)
                        ins = V.tensor_tensor(s_lo[:, 2 * q:2 * q + 2, :], M[q].rearrange("p (a b) -> p a b", a=2), hi, ALU.subtract)
                    else:
                        for kk in range(2):
                            kt = 2 * q + kk
                            ins = V.scalar_tensor_tensor(s_lo[:, kt, :], M[q][:, SEQ * kk:SEQ * kk + SEQ], gains[:, norm, kt:kt + 1],
                                                         s_hi[:, kt, :].bitcast(F32), ALU.mult, ALU.subtract)
                    sig(ins, "turn_lo")

            def mean_squares(norm):
                dve.wait_ge(sem("stat_ss"), 2 * norm + 2)
                V.tensor_scalar(RS[:, 2 * norm:2 * norm + 2], SS[:, 2 * norm:2 * norm + 2], 1 / D, EPS, ALU.mult, ALU.add).then_inc(sem("stat_ms"), 1)

            def rotate(x1, x2, cos, sin, prod, eng, lnk):
                eng.tensor_tensor(prod[0], x1, cos, ALU.mult)
                eng.tensor_tensor(prod[1], x2, sin, ALU.mult)
                eng.tensor_tensor(prod[2], x2, cos, ALU.mult)
                lnk(eng.tensor_tensor(prod[3], x1, sin, ALU.mult))
                eng.tensor_tensor(x1, prod[0], prod[1], ALU.subtract)
                return eng.tensor_tensor(x2, prod[2], prod[3], ALU.add)

            dve.wait_ge(sem("vec_pe"), 1)
            sig(V.tensor_copy(gains.rearrange("p a b -> p (a b)"), M[0][:, 0:48]), "vec_dve")
            sig(V.tensor_copy(cw.rearrange("p a b -> p (a b)"), M[0][:, 128:224]), "vec_dve")
            split(0, 0)
            split(0, 1)
            turn_lo(NORMS["mix"])
            mean_squares(0)
            dve.wait_ge(sem("stat_rs"), 1)
            V.tensor_scalar(HRS, RS[:, 0:2], 0.5, None, ALU.mult)
            link(V.tensor_scalar(QRS, RS[:, 0:2], 0.25, None, ALU.mult))
            for k in range(4):
                begin(B_A + k)
                project(B_A + k, PA[:, 1, NCOL * k:NCOL * k + NCOL], RS[:, 1:2])
            begin(B_A + 4)
            project(B_A + 4, PA[:, 1, 2048:A_W], RS[:, 1:2])
            begin(B_Q)
            dve.wait_ge(sem("ev0"), 5)
            dve.wait_ge(sem("ev1"), 5)
            dve.wait_ge(sem("vec_in"), 16 * 11)
            dve.wait_ge(sem("consts_in"), 16)
            sp2 = SP[:, 0:16].rearrange("p (t h) -> p t h", t=2)
            link(V.tensor_tensor(sp2, PA[:, :, 0:8], spread(vec[:, V_DT:V_DT + 8], 1, 2), ALU.add))
            link(V.tensor_scalar(GA_, SP[:, 0:16], 0.0, None, ALU.max))
            V.scalar_tensor_tensor(SP[:, 0:16], SP[:, 0:16], -1.0, SP[:, 0:16], ALU.mult, ALU.max).then_inc(sem("g_abs"), 1)
            heads = PA[:, :, AQ:AV].rearrange("p t (h d) -> p t h d", d=P)
            dve.wait_ge(sem("att_sq"), 1)
            link(V.tensor_reduce(SSA, SQ.rearrange("p t h d -> p (t h) d"), AX_X, ALU.add))
            V.tensor_scalar(SSA, SSA, 1 / P, EPS, ALU.mult, ALU.add).then_inc(sem("att_ms"), 1)
            V.tensor_scalar(IWS.rearrange("p (t h) -> p t h", t=2), PA[:, :, IW:IW + 8], 8 ** -0.5 * 64 ** -0.5, None, ALU.mult)
            dve.wait_ge(sem("att_rn"), 1)
            for t in range(NT):
                ins = V.tensor_tensor(heads[:, t], heads[:, t], spread(RNA[:, 10 * t:10 * t + 10], 2, P), ALU.mult)
            link(ins)
            for t in range(NT):
                V.tensor_tensor(heads[:, t, 0:8], heads[:, t, 0:8], spread(vec[:, V_QG:V_QG + P], 1, 8), ALU.mult)
                ins = V.tensor_tensor(heads[:, t, 8:10], heads[:, t, 8:10], spread(vec[:, V_KG:V_KG + P], 1, 2), ALU.mult)
            link(ins)
            ca, sa = (spread(cst[:, C_ROPE_A + 32 * k:C_ROPE_A + 32 * k + 32].rearrange("p (t d) -> p t d", t=2), 2, 10) for k in range(2))
            prods = [RT[:, k].rearrange("p (t h d) -> p t h d", t=2, h=10) for k in range(4)]
            sig(rotate(heads[:, :, :, 0:16], heads[:, :, :, 16:32], ca, sa, prods, V, link), "att_rot")
            dve.wait_ge(sem("b_tanh"), 1)
            link(V.tensor_scalar(BT, BT, 0.5, 0.5, ALU.mult, ALU.add))
            V.tensor_scalar(HBT, BT, 0.5, None, ALU.mult)
            dve.wait_ge(sem("g_ln"), 1)
            link(V.tensor_tensor(GA_, GA_, SP[:, 16:32], ALU.add))
            V.scalar_tensor_tensor(GA_.rearrange("p (t h) -> p t h", t=2), GA_.rearrange("p (t h) -> p t h", t=2), -1.0,
                                   spread(SP[:, 40:48], 1, 2), ALU.mult, ALU.mult).then_inc(sem("gdn_g"), 1)
            project(B_Q, PQ[:, 1, 0:NCOL], RS[:, 1:2])
            begin(B_Q + 1)
            for e, dst in ((1, iqT[:, 2:4, :]), (3, kT), (5, qT[:, 2:4, :]), (7, qT[:, 6:8, :])):
                dve.wait_ge(sem("attT_pe"), e + 1)
                V.tensor_copy(dst, M[e % 4].rearrange("p (a b) -> p a b", a=2)).then_inc(sem("attT_dve"), 1)
            project(B_Q + 1, PQ[:, 1, NCOL:2 * NCOL], RS[:, 1:2])
            begin(B_Q + 2)
            for t in range(NT):
                ns = P * (t + 1)
                dve.wait_ge(sem("relu"), 2 if t == 0 else 6)
                link(V.tensor_scalar(SC[:, t, 0:ns], RL[:, 0, 0:ns], IWS[:, 8 * t:8 * t + 1], None, ALU.mult))
                for h in range(1, 8):
                    ins = V.scalar_tensor_tensor(SC[:, t, 0:ns], RL[:, h, 0:ns], IWS[:, 8 * t + h:8 * t + h + 1], SC[:, t, 0:ns], ALU.mult, ALU.add)
                    if h < 7:
                        link(ins)
                    elif t == 0:
                        sig(ins, "acc")
                        dve.wait_ge(sem("acc"), 1)
                    else:
                        link(ins)
                diag = SC[:, t, P * t:P * t + P]
                link(V.tensor_tensor(diag, diag, cst[:, C_TRIX:C_TRIX + P], ALU.add))
            project(B_Q + 2, PQ[:, 1, NCOL * 2:NCOL * 3], RS[:, 1:2])
            begin(B_Q + 3)

            def select(rounds):
                for _ in rounds:
                    for t in range(NT):
                        ins = V.max(MX8[:, 8 * t:8 * t + 8], SC[:, t, 0:P * (t + 1)])
                    link(ins)
                    for t in range(NT):
                        ins = V.match_replace(SC[:, t, 0:P * (t + 1)], MX8[:, 8 * t:8 * t + 8], SC[:, t, 0:P * (t + 1)], TAKEN)
                    link(ins)

            select(range(4))
            project(B_Q + 3, PQ[:, 1, NCOL * 3:NCOL * 4], RS[:, 1:2])
            begin(B_Q + 4)
            select(range(4))
            for t in range(NT):
                ns = P * (t + 1)
                link(V.tensor_scalar(BIAS[:, t, 0:ns], SC[:, t, 0:ns], BETWEEN, EXCLUDED, ALU.is_ge, ALU.mult))
                diag = BIAS[:, t, P * t:P * t + P]
                link(V.tensor_tensor(diag, diag, cst[:, C_TRI:C_TRI + P], ALU.add))
            project(B_Q + 4, PQ[:, 1, NCOL * 4:NCOL * 5], RS[:, 1:2])
            begin(B_Q + 5)

            groups = [0]

            def attention(work, scale, width, mask, lm, pts, dst):
                g0, n = groups[0], len(work)

                def greatest(k):
                    t, hs = work[k]
                    g, ns = g0 + k, keys_of(work, k)
                    a = 4 * (g % 8)
                    dve.wait_ge(sem("att_logits"), g + 1)
                    if mask is None:
                        link(V.tensor_reduce(NEGM[:, a:a + len(hs)], M[g % 2].rearrange("p (a b) -> p a b", b=ns), AX_X, ALU.max))
                    else:
                        if k >= 2:
                            dve.wait_ge(sem("att_pt"), g - 1)
                        for j in range(len(hs)):
                            ins = V.tensor_tensor_reduce(lm[:, g % 2, j * ns:(j + 1) * ns], M[g % 2][:, j * ns:(j + 1) * ns], mask(t), 1.0, -3.0e38,
                                                         ALU.add, ALU.max, NEGM[:, a + j:a + j + 1])
                        link(ins)
                    V.tensor_scalar(NEGM[:, a:a + len(hs)], NEGM[:, a:a + len(hs)], -scale, None, ALU.mult).then_inc(sem("att_max"), 1)

                def turned(k):
                    g = g0 + k
                    dve.wait_ge(sem("att_pt"), g + 1)
                    if k >= 2:
                        dve.wait_ge(sem("att_out"), g - 1)
                    V.tensor_copy(pts[:, g % 2, :], M[2][:, :]).then_inc(sem("att_ptc"), 1)

                def normed(k):
                    t, hs = work[k]
                    g = g0 + k
                    a = 4 * (g % 8)
                    link(V.reciprocal(RSUM[:, a:a + len(hs)], SUMS[:, a:a + len(hs)]))
                    dve.wait_ge(sem("att_out"), g + 1)
                    V.tensor_tensor(dst(t, hs), M[3][:, 0:width * len(hs)].rearrange("p (a b) -> p a b", b=width),
                                    spread(RSUM[:, a:a + len(hs)], 2, width), ALU.mult).then_inc(sem("att_norm"), 1)

                for k in range(n + 2):
                    if k < n:
                        greatest(k)
                    if 1 <= k <= n:
                        turned(k - 1)
                    if k >= 2:
                        normed(k - 2)
                    yield k
                groups[0] += n

            for k in attention(WORK_A, P ** -0.5, P, lambda t: BIAS[:, t, 0:P * (t + 1)], LM, PTS, lambda t, hs: OA[:, t, hs[0]:hs[-1] + 1, :]):
                if k == 4:
                    project(B_Q + 5, PQ[:, 1, NCOL * 5:NCOL * 6], RS[:, 1:2])
                    begin(B_GB)

            def silu(e):
                dve.wait_ge(sem("conv_tanh"), e + 1)
                y = YT[:, 2 * e:2 * e + 2, :]
                sig(V.scalar_tensor_tensor(y, CT[:, e % 2], 1.0, y, ALU.add, ALU.mult), "gdn_y")

            oa = OA.rearrange("p t h d -> p t (h d)")
            for e in range(12):
                dve.wait_ge(sem("conv_act"), e + 1)
                for tap in range(1, 4):
                    for j in range(2):
                        ct = 2 * e + j
                        y = YT[:, ct, tap:SEQ]
                        ins = V.scalar_tensor_tensor(y, M[e % 4][:, SEQ * j:SEQ * j + SEQ - tap], cw[:, 3 - tap, ct:ct + 1], y, ALU.mult, ALU.add)
                    if tap < 3:
                        link(ins)
                sig(ins, "conv_dve")
                if e >= 1:
                    silu(e - 1)
                if e in (5, 9):
                    b = B_GB + (e == 9)
                    cols = slice(NCOL * (e == 9), NCOL * (e == 9) + NCOL)
                    for t in range(NT):
                        dve.wait_ge(sem(f"ev{t}"), b + 1)
                        ins = V.scalar_tensor_tensor(oa[:, t, cols], TMP[:, t], 1.0, oa[:, t, cols], ALU.add, ALU.mult)
                    ins.then_inc(sem("gate_used"), 1)
                    begin(b + 1)
            silu(11)
            dve.wait_ge(sem("gdn_ss"), 2)
            V.tensor_scalar(SSK, M[0][:, 0:32], 0.25, EPS, ALU.mult, ALU.add).then_inc(sem("gdn_ms"), 1)
            dve.wait_ge(sem("gdn_gc"), 1)
            sig(V.tensor_copy(GC, M[1][:, 0:64]), "gdn_gcc")
            dve.wait_ge(sem("gdn_gcc"), 1)
            sig(V.tensor_tensor(GC[:, 16:32], GC[:, 16:32], GC[:, 0:16], ALU.subtract), "gdn_gcc")
            dve.wait_ge(sem("gdn_gcc"), 2)
            V.tensor_tensor(GU, spread(GA_, 2, 64), spread(cst[:, C_UC:C_UC + 64], 1, 16), ALU.mult)
            V.tensor_tensor(BI, spread(BT, 2, 64), spread(cst[:, C_IC:C_IC + 64], 1, 16), ALU.mult).then_inc(sem("gdn_rows"), 1)
            dve.wait_ge(sem("gdn_rq"), 1)
            link(V.tensor_scalar(RQK, RQK, 0.5, None, ALU.mult))
            for e in range(8):
                part, t, half = e // 4, e % 4 // 2, e % 2
                dve.wait_ge(sem("gdn_kvT"), e + 1)
                src = M[(e + 2) % 4].rearrange("p (a b) -> p a b", a=4)
                if part == 0:
                    f = RQK[:, 16 + 8 * t + 4 * half:][:, 0:4]
                    sig(V.tensor_tensor(KN[:, t, 4 * half:4 * half + 4, :], src, spread(f, 2, P), ALU.mult), "gdn_kv")
                else:
                    f = HBT[:, 8 * t + 4 * half:][:, 0:4]
                    sig(V.tensor_tensor(VB[:, t, 4 * half:4 * half + 4, :], src, spread(f, 2, P), ALU.mult), "gdn_kv")

            def z_block(b, half):
                for t in range(NT):
                    dve.wait_ge(sem("z_tanh"), 2 * half + t + 1)
                    cols = ZG[:, t, NCOL * half:NCOL * half + NCOL]
                    V.scalar_tensor_tensor(cols, cols, 1.0, G[b % 2][t][:, :], ALU.add, ALU.mult).then_inc(sem(f"ev{t}"), 1)

            z_block(B_Z, 0)
            begin(B_Z + 1)
            for h in range(2):
                dve.wait_ge(sem("gdn_bc"), h + 1)
                ins = V.tensor_tensor(DM[:, 8 * h:8 * h + 8, :], M[h].rearrange("p (a b) -> p a b", a=8), spread(cst[:, C_NEG:C_NEG + 64], 1, 8), ALU.add)
            ins.then_inc(sem("gdn_dm"), 1)
            dve.wait_ge(sem("gdn_dm"), 1)
            V.tensor_tensor(DM, DM, spread(GC[:, 0:16], 2, 64), ALU.subtract).then_inc(sem("gdn_dm0"), 1)
            dve.wait_ge(sem("gdn_e"), 1)
            V.tensor_tensor(BEG, BT, EG, ALU.mult).then_inc(sem("gdn_beg"), 1)
            z_block(B_Z + 1, 1)
            begin(B_GA)
            dve.wait_ge(sem("gdn_dme"), 1)
            for h in range(2):
                dve.wait_ge(sem("gdn_bc"), h + 3)
                ins = V.tensor_tensor(AT[:, 8 * h:8 * h + 8, :], M[2 + h].rearrange("p (a b) -> p a b", a=8), DM[:, 8 * h:8 * h + 8, :], ALU.mult)
            sig(ins, "gdn_db")
            dve.wait_ge(sem("gdn_db"), 1)
            for h in range(2):
                dve.wait_ge(sem("gdn_kk"), h + 1)
                sig(V.tensor_tensor(AT[:, 8 * h:8 * h + 8, :], M[h].rearrange("p (a b) -> p a b", a=8), AT[:, 8 * h:8 * h + 8, :], ALU.mult), "gdn_at")
            for h in range(2):
                dve.wait_ge(sem("gdn_kk"), h + 3)
                V.tensor_tensor(QK[:, 8 * h:8 * h + 8, :], M[2 + h].rearrange("p (a b) -> p a b", a=8), DM[:, 8 * h:8 * h + 8, :], ALU.mult).then_inc(sem("gdn_qk"), 1)

            def masked(lv, t):
                V.tensor_tensor(LT[:, 8 * t:8 * t + 8, :], AT[:, 8 * t:8 * t + 8, :],
                                spread(cst[:, C_LEV + 64 * lv:C_LEV + 64 * lv + 64], 1, 8), ALU.mult).then_inc(sem("inv_lt"), 1)

            eye = spread(cst[:, C_IC:C_IC + 64], 1, 8)
            for t in range(NT):
                dve.wait_ge(sem("gdn_at"), t + 1)
                masked(0, t)
            for lv in range(6):
                for t in range(NT):
                    tt = slice(8 * t, 8 * t + 8)
                    if lv == 0:
                        dve.wait_ge(sem("inv_lt"), t + 1)
                        dve.wait_ge(sem("inv_p"), t + 1)
                        V.tensor_tensor(XT[:, tt, :], eye, LT[:, tt, :], ALU.subtract)
                        V.tensor_tensor(XI[:, tt, :], eye, M[t].rearrange("p (a b) -> p a b", a=8), ALU.subtract).then_inc(sem("inv_x"), 1)
                        dve.wait_ge(sem("inv_x"), t + 1)
                        masked(1, t)
                        continue
                    dve.wait_ge(sem("inv_xp"), NT * (lv - 1) + t + 1)
                    if lv < 5:
                        V.tensor_tensor(XI[:, tt, :], XI[:, tt, :], M[2 + t].rearrange("p (a b) -> p a b", a=8), ALU.subtract)
                    V.tensor_tensor(XT[:, tt, :], XT[:, tt, :], M[t].rearrange("p (a b) -> p a b", a=8), ALU.subtract).then_inc(sem("inv_x"), 1)
                    if lv < 5:
                        masked(lv + 1, t)
                if lv in (2, 4):
                    b = B_GA + (lv == 4)
                    cols = slice(NCOL * (lv == 4), NCOL * (lv == 4) + NCOL)
                    for t in range(NT):
                        dve.wait_ge(sem(f"ev{t}"), b + 1)
                        ins = V.scalar_tensor_tensor(ZG[:, t, cols], TMP[:, t], 1.0, ZG[:, t, cols], ALU.add, ALU.mult)
                    ins.then_inc(sem("gate_used"), 1)
                    begin(b + 1)
            dve.wait_ge(sem("gate_used"), 4)
            zg = ZG.rearrange("p t (h d) -> p (t h) d", d=P)
            link(V.tensor_tensor(zg, zg, spread(vec[:, V_GN:V_GN + P], 1, 16), ALU.mult))
            dve.wait_ge(sem("gdn_uc"), 4)
            for n in range(4):
                t, r = n // 2, slice(64 * (n % 2), 64 * (n % 2) + 64)
                for half in range(2):
                    hh = slice(4 * half, 4 * half + 4)
                    if n > 0:
                        dve.wait_ge(sem("st_ws"), 2 * (n - 1) + half + 1)
                        V.tensor_tensor(UV[r, t, hh, :], UV[r, t, hh, :], M[half][r, :].rearrange("p (a b) -> p a b", a=4), ALU.subtract).then_inc(sem("st_v"), 1)
                if n < 3:
                    for half in range(2):
                        hh = slice(4 * half, 4 * half + 4)
                        dve.wait_ge(sem("st_kv"), 2 * n + half + 1)
                        src = M[2 + half].rearrange("p (a b) -> p a b", a=4)
                        if n == 0:
                            sig(V.tensor_copy(ST[1][:, hh, :], src), "st_new")
                        else:
                            sig(V.tensor_tensor(ST[n + 1][:, hh, :], src, SD[:, hh, :], ALU.add), "st_new")
                if n in (0, 1):
                    dve.wait_ge(sem("st_new"), 2 * (n + 1))
                    c, tt = (n + 1) % 2, (n + 1) // 2
                    f = EL[:, 16 * c + 8 * tt:][:, 0:8]
                    link(V.tensor_tensor(SD, ST[n + 1], spread(f, 2, P), ALU.mult))
            for t in range(NT):
                dve.wait_ge(sem("o_pe"), t + 1)
                for half in range(2):
                    hh = slice(4 * half, 4 * half + 4)
                    src = M[half].rearrange("p (a b) -> p a b", a=4)
                    own_ = M[2 + half].rearrange("p (a b) -> p a b", a=4)
                    f = spread(EG[:, 8 * t + 4 * half:][:, 0:4], 2, P)
                    if t == 0:
                        V.tensor_copy(O1[0:64, t, hh, :], own_[0:64])
                        link(V.tensor_tensor(O1[64:P, t, hh, :], src[64:P], f[64:P], ALU.mult))
                        ins = V.tensor_tensor(O1[64:P, t, hh, :], own_[64:P], O1[64:P, t, hh, :], ALU.add)
                    else:
                        link(V.tensor_tensor(O1[:, t, hh, :], src, f, ALU.mult))
                        ins = V.tensor_tensor(O1[:, t, hh, :], own_, O1[:, t, hh, :], ALU.add)
                if t == 0:
                    sig(ins, "o_done")
                    dve.wait_ge(sem("o_done"), 1)
                else:
                    link(ins)
            o = O1.rearrange("p t h d -> p (t h) d")
            link(V.tensor_scalar(RQK[:, 0:16], RQK[:, 0:16], P ** -0.5, None, ALU.mult))
            V.tensor_tensor(o, o, spread(RQK[:, 0:16], 2, P), ALU.mult).then_inc(sem("o_scaled"), 1)
            dve.wait_ge(sem("o_sq"), 1)
            link(V.tensor_reduce(SSO, SQ3.rearrange("p t h d -> p (t h) d"), AX_X, ALU.add))
            V.tensor_scalar(SSO, SSO, 1 / P, EPS, ALU.mult, ALU.add).then_inc(sem("o_ms"), 1)
            dve.wait_ge(sem("o_rs"), 1)
            link(V.tensor_tensor(RSO.rearrange("p (t h) -> p t h", t=2), RSO.rearrange("p (t h) -> p t h", t=2), spread(QRS, 2, 8), ALU.mult))
            link(V.tensor_tensor(o, o, spread(RSO, 2, P), ALU.mult))
            link(V.tensor_tensor(o, o, zg, ALU.mult))
            sig(V.scalar_tensor_tensor(O1.rearrange("p t h d -> p (t h d)"), OA.rearrange("p t h d -> p (t h d)"), 0.5,
                                       O1.rearrange("p t h d -> p (t h d)"), ALU.mult, ALU.add), "o_done")
            turn_lo()
            residual(B_O, 0)
            begin(B_O + 1)
            residual(B_O + 1, 1)
            turn_lo(NORMS["mlp"])
            mean_squares(1)
            dve.wait_ge(sem("stat_rs"), 2)

            def relu(b, i=None):
                mm_finished(B_UP + b, i)
                for t in range(NT):
                    if i is not None or b >= 2:
                        dve.wait_ge(sem("hid_pe"), at(2 * (b - 2) + 2, 4, i))
                    V.tensor_scalar(hid[:, b % 2, t], G[(B_UP + b) % 2][t][:, :], RS[:, 2 + t:3 + t], 0.0, ALU.mult, ALU.max).then_inc(sem(f"ev{t}"), 1)

            def hidden_lo(b, i=None):
                for q in range(2):
                    dve.wait_ge(sem("hid_hi"), at(2 * b + q + 1, 4, i))
                    kk = bass.ds(at(4 * b + 2 * q, 8, i), 2)
                    V.tensor_tensor(hT_lo[:, kk, :], M[2 * (b % 2) + q].rearrange("p (a b) -> p a b", a=2), hT_hi[:, kk, :].bitcast(F32), ALU.subtract)\
                        .then_inc(sem("hid_lo"), 1)

            begin(B_UP)
            relu(0)
            begin(B_UP + 1)
            relu(1)
            hidden_lo(0)
            begin(B_UP + 2)
            relu(2)
            hidden_lo(1)
            with dve.Fori(0, 2) as i:
                for j in range(2):
                    begin(B_UP + 3 + j, i)
                    relu(3 + j, i)
                    hidden_lo(2 + j, i)
            begin(B_UP + 7)
            relu(7)
            hidden_lo(6)
            hidden_lo(7)
            for j in range(2):
                begin(B_DN + j)
                residual(B_DN + j, j)
            turn_lo(NORMS["mix2"])
            mean_squares(2)
            dve.wait_ge(sem("stat_rs"), 3)
            rs2 = RS[:, 5:6]
            for k in range(4):
                begin(B_2 + k)
                project(B_2 + k, P2R[:, 1, NCOL * k:NCOL * k + NCOL], rs2)
                if k == 1:
                    dve.wait_ge(sem("ev0"), B_2 + 2)
                    dve.wait_ge(sem("ev1"), B_2 + 2)
                    qk = P2R[:, :, 0:1024].rearrange("p t (h d) -> p t h d", d=64)
                    cr, sr = (spread(cst[:, C_ROPE_R + 64 * n:C_ROPE_R + 64 * n + 64].rearrange("p (t d) -> p t d", t=2), 2, 16) for n in range(2))
                    pr = [RT2[:, n].rearrange("p (t h d) -> p t h d", t=2, h=16) for n in range(4)]
                    sig(rotate(qk[:, :, :, 0:32], qk[:, :, :, 32:64], cr, sr, pr, V, link), "ret_rot")
            begin(B_2 + 4)
            dve.wait_ge(sem("ret_rot"), 1)
            for e, dst in ((1, rqT[:, 2:4, :]), (3, rkT[:, 2:4, :])):
                dve.wait_ge(sem("retT"), e + 1)
                V.tensor_copy(dst, M[e].rearrange("p (a b) -> p a b", a=2)).then_inc(sem("ret_dve"), 1)
            project(B_2 + 4, P2F[:, 1, 0:NCOL], rs2)
            begin(B_2 + 5)
            dve.wait_ge(sem("ret_w_in"), 16)
            for e in range(4):
                dve.wait_ge(sem("ret_s"), e + 1)
                V.tensor_tensor(PT2[:, 512 * e:512 * e + 512], M[e][:, :], WR[:, 512 * e:512 * e + 512], ALU.mult).then_inc(sem("ret_w"), 1)
            for e in range(2):
                dve.wait_ge(sem("ret_s"), e + 5)
                V.tensor_tensor(PT2[:, 2048 + 512 * e:][:, 0:512], M[e][:, :], WR[:, 2048 + 512 * e:][:, 0:512], ALU.mult).then_inc(sem("ret_w"), 1)
            project(B_2 + 5, P2F[:, 1, NCOL:2 * NCOL], rs2)
            begin(B_2 + 6)
            dve.wait_ge(sem("fox_sq"), 1)
            link(V.tensor_reduce(SSF, SQR.rearrange("p t h d -> p (t h) d"), AX_X, ALU.add))
            V.tensor_scalar(SSF, SSF, 1 / 64, EPS, ALU.mult, ALU.add).then_inc(sem("fox_ms"), 1)
            project(B_2 + 6, P2F[:, 1, 2 * NCOL:3 * NCOL], rs2)
            begin(B_2 + 7)
            project(B_2 + 7, P2F[:, 1, 1536:1544], rs2)
            ret = [MG2[:, t, 0:NCOL].rearrange("p (h d) -> p h d", d=64) for t in range(NT)]
            for t in range(NT):
                dve.wait_ge(sem("ret_oc"), t + 1)
                ins = V.tensor_reduce(MU[:, 8 * t:8 * t + 8], ret[t], AX_X, ALU.add)
            link(ins)
            link(V.tensor_scalar(MU, MU, 1 / 64, None, ALU.mult))
            for t in range(NT):
                ins = V.tensor_tensor(ret[t], ret[t], spread(MU[:, 8 * t:8 * t + 8], 2, 64), ALU.subtract)
            ins.then_inc(sem("ret_cen"), 1)
            dve.wait_ge(sem("ev0"), B_2 + 8)
            dve.wait_ge(sem("ev1"), B_2 + 8)
            link(V.tensor_tensor(sp2, P2F[:, :, 1536:1544], spread(vec[:, V_BF:V_BF + 8], 1, 2), ALU.add))
            link(V.tensor_scalar(FL.rearrange("p t h -> p (t h)"), SP[:, 0:16], 0.0, None, ALU.min))
            V.scalar_tensor_tensor(SP[:, 0:16], SP[:, 0:16], -1.0, SP[:, 0:16], ALU.mult, ALU.max).then_inc(sem("f_abs"), 1)
            dve.wait_ge(sem("ret_sq"), 1)
            link(V.tensor_reduce(VAR, RSQ.rearrange("p t (h d) -> p (t h) d", d=64), AX_X, ALU.add))
            V.tensor_scalar(VAR, VAR, 1 / 64, EPS, ALU.mult, ALU.add).then_inc(sem("ret_ms"), 1)
            dve.wait_ge(sem("f_ln"), 1)
            V.tensor_tensor(FL.rearrange("p t h -> p (t h)"), FL.rearrange("p t h -> p (t h)"), SP[:, 16:32], ALU.subtract).then_inc(sem("fox_f"), 1)
            dve.wait_ge(sem("fox_rn"), 1)
            for n, dst in enumerate((QA, KA)):
                for t in range(NT):
                    src = P2F[:, t, NCOL * n:NCOL * n + NCOL].rearrange("p (h d) -> p h d", d=64)
                    ins = V.tensor_tensor(dst[:, t, :, 0:64], src, spread(RNF[:, 16 * t + 8 * n:][:, 0:8], 2, 64), ALU.mult)
            link(ins)
            for n, (dst, g) in enumerate(((QA, V_FQ), (KA, V_FK))):
                d = dst.rearrange("p t h d -> p (t h) d")[:, :, 0:64]
                if n == 0:
                    V.scalar_tensor_tensor(d, d, 1 / 8, spread(vec[:, g:g + 64], 1, 16), ALU.mult, ALU.mult)
                else:
                    V.tensor_tensor(d, d, spread(vec[:, g:g + 64], 1, 16), ALU.mult)
            V.memset(QA[:, :, :, 65:66], 1.0)
            V.memset(KA[:, :, :, 64:65], 1.0)
            turn_lo(NORMS["mem"])
            dve.wait_ge(sem("fox_fc"), 1)
            fc = M[0][:, 0:16].rearrange("p (t h) -> p t h", t=2)
            V.tensor_copy(QA[:, :, :, 64], fc)
            V.tensor_scalar(KA[:, :, :, 65], fc, -1.0, None, ALU.mult).then_inc(sem("fox_aug"), 1)
            dve.wait_ge(sem("rg_tanh"), 1)
            link(V.scalar_tensor_tensor(TG, TG, 1.0, P2R[:, :, RG:RG + NCOL], ALU.add, ALU.mult))
            for t in range(NT):
                ins = V.scalar_tensor_tensor(TG[:, t], TG[:, t], 0.5, vec2[:, 0:NCOL], ALU.mult, ALU.mult)
            link(ins)
            dve.wait_ge(sem("ret_rs"), 1)
            for t in range(NT):
                ins = V.tensor_tensor(ret[t], ret[t], spread(RSTD[:, 8 * t:8 * t + 8], 2, 64), ALU.mult)
            link(ins)
            sig(V.tensor_tensor(MG2[:, :, 0:NCOL], MG2[:, :, 0:NCOL], TG, ALU.mult), "ret_done")
            mean_squares(3)
            dve.wait_ge(sem("stat_rs"), 4)
            rs4 = RS[:, 7:8]
            begin(B_KV)
            project(B_KV, KV[:, 1, 0:NCOL], rs4)
            begin(B_KV + 1)
            project(B_KV + 1, KV[:, 1, NCOL:D], rs4)
            for e in range(1, 8, 2):
                dve.wait_ge(sem("foxT_pe"), e + 1)
                dst = (qaT if e < 4 else kaT)[0:66, 2 * (e % 4):2 * (e % 4) + 2, :]
                V.tensor_copy(dst, M[e % 4][0:66, :].rearrange("p (a b) -> p a b", a=2)).then_inc(sem("foxT_dve"), 1)
            begin(B_KV + 2)
            for k in attention(WORK_A, 1.0, 64, fox_mask, LM2, PTS2,
                               lambda t, hs: MG2[:, t, NCOL + 64 * hs[0]:NCOL + 64 * hs[-1] + 64].rearrange("p (a b) -> p a b", b=64)):
                if k == 1:
                    project(B_KV + 2, KV[:, 1, D:D + NCOL], rs4)
                    begin(B_KV + 3)
                if k == 5:
                    project(B_KV + 3, KV[:, 1, D + NCOL:2 * D], rs4)
                    begin(B_O2)
            turn_lo()
            dve.wait_ge(sem("x_sqk"), 1)
            link(V.tensor_reduce(SSX, SQX.rearrange("p t (h d) -> p (t h) d", d=256), AX_X, ALU.add))
            V.tensor_scalar(SSX, SSX, 1 / 256, EPS, ALU.mult, ALU.add).then_inc(sem("x_ms"), 1)
            residual(B_O2, 0)
            begin(B_O2 + 1)
            residual(B_O2 + 1, 1)
            turn_lo(NORMS["xattn"])

            def heads_norm(v, n, gain, name):
                dve.wait_ge(sem("x_rn"), n + 1)
                for t in range(NT):
                    a = v[:, t, 0:D].rearrange("p (h d) -> p h d", d=256)
                    ins = V.tensor_tensor(a, a, spread(RNX[:, 8 * n + 4 * t:][:, 0:4], 2, 256), ALU.mult)
                link(ins)
                for t in range(NT):
                    a = v[:, t, 0:D].rearrange("p (h d) -> p h d", d=256)
                    ins = V.tensor_tensor(a, a, spread(gain, 1, 4), ALU.mult)
                ins.then_inc(sem(name), 1)

            mean_squares(4)
            heads_norm(KV, 0, vec2[:, NCOL:NCOL + 256], "x_k")
            dve.wait_ge(sem("stat_rs"), 5)
            for k in range(2):
                begin(B_XQ + k)
                project(B_XQ + k, XQ[:, 1, NCOL * k:NCOL * k + NCOL], RS[:, 9:10])
            for e in range(1, 8, 2):
                if e == 5:
                    dve.wait_ge(sem("x_sqq"), 1)
                    link(V.tensor_reduce(SSX, SQX.rearrange("p t (h d) -> p (t h) d", d=256), AX_X, ALU.add))
                    V.tensor_scalar(SSX, SSX, 1 / 256, EPS, ALU.mult, ALU.add).then_inc(sem("x_ms"), 1)
                    dve.wait_ge(sem("ev0"), B_XO)
                    heads_norm(XQ, 1, vec[:, V_XQ:V_XQ + 256], "x_q")
                dve.wait_ge(sem("xT_pe"), e + 1)
                dst = (xkT if e < 4 else xqT)[:, 2 * (e % 4):2 * (e % 4) + 2, :]
                V.tensor_copy(dst, M[e % 4].rearrange("p (a b) -> p a b", a=2)).then_inc(sem("xT_dve"), 1)
            for k in attention(WORK_X, 1 / 16, 256, None, None, PTS2,
                               lambda t, hs: XO[:, t, 256 * hs[0]:256 * hs[-1] + 256].rearrange("p (a b) -> p a b", b=256)):
                pass
            turn_lo()
            for j in range(2):
                begin(B_XO + j)
                residual(B_XO + j, j)
            turn_lo(NORMS["ffn"])
            mean_squares(5)
            dve.wait_ge(sem("stat_rs"), 6)
            link(V.tensor_scalar(RS5H, RS[:, 10:12], 0.5, None, ALU.mult))
            V.tensor_tensor(RS5Q, RS5H, RS[:, 10:12], ALU.mult).then_inc(sem("rs5"), 1)

            def gate_mul(p, i=None):
                b = B_GU + 2 * p
                n = blocks[b]["n"]
                for t in range(NT):
                    dve.wait_ge(sem("gate_tanh"), at(2 * p + t + 1, 2, i))
                    V.scalar_tensor_tensor(sg2[:, 1, t, 0:n], sg2[:, 0, t, 0:n], 1.0, G[b % 2][t][:, 0:n], ALU.add, ALU.mult).then_inc(sem(f"ev{t}"), 1)

            def up_mul(p, i=None):
                b = B_GU + 2 * p + 1
                n = blocks[b]["n"]
                mm_finished(b, i)
                for t in range(NT):
                    dve.wait_ge(sem(f"ev{t}"), at(b, 2, i))
                    if i is not None or p > 0:
                        dve.wait_ge(sem("hid2_pe"), at(2 * p, 2, i))
                    V.tensor_tensor(hid2[:, 0, t, 0:n], sg2[:, 1, t, 0:n], G[b % 2][t][:, 0:n], ALU.mult).then_inc(sem(f"ev{t}"), 1)

            def hidden2_lo(p, i=None, q_n=2):
                for q in range(q_n):
                    dve.wait_ge(sem("hid2_hi"), at(2 * p + q + 1, 2, i))
                    kk = bass.ds(at(4 * p + 2 * q, 4, i), 2)
                    V.tensor_tensor(h2_lo[:, kk, :], M[q].rearrange("p (a b) -> p a b", a=2), h2_hi[:, kk, :].bitcast(F32), ALU.subtract)\
                        .then_inc(sem("hid2_lo"), 1)

            begin(B_GU)
            gate_mul(0)
            begin(B_GU + 1)
            up_mul(0)
            with dve.Fori(0, 3) as i:
                begin(B_GU + 2, i)
                gate_mul(1, i)
                begin(B_GU + 3, i)
                hidden2_lo(0, i)
                up_mul(1, i)
            begin(B_GU + 8)
            gate_mul(4)
            begin(B_GU + 9)
            hidden2_lo(3)
            up_mul(4)
            begin(B_GU + 10)
            gate_mul(5)
            begin(B_GU + 11)
            hidden2_lo(4)
            up_mul(5)
            hidden2_lo(5, q_n=1)
            begin(B_D2)
            residual(B_D2, 0)
            begin(B_D2 + 1)
            residual(B_D2 + 1, 1, last=True)

        @block.gpsimd
        def _(pool):
            def power(dst, src, n, wait, value, name):
                pool.wait_ge(sem(wait), value)
                pool.tensor_tensor(dst, src, MHALF[:, 0:n], ALU.pow).then_inc(sem(name), 1)

            for dst, src in ((vec[:, V_QG:V_QG + P], q_norm_g[0]), (vec[:, V_KG:V_KG + P], k_norm_g[0]), (vec[:, V_GN:V_GN + P], gdn_norm_g[0]),
                             (vec[:, V_DT:V_DT + 8], dt_bias[0]), (vec[:, V_AL:V_AL + 8], a_log[0]), (vec[:, V_BF:V_BF + 8], b_forget_2[0]),
                             (vec[:, V_FQ:V_FQ + 64], g_fox_q_2[0]), (vec[:, V_FK:V_FK + 64], g_fox_k_2[0]),
                             (vec[:, V_XQ:V_XQ + 256], g_xq_2[0]), (vec2[:, NCOL:NCOL + 256], g_xk_2[0]),
                             (vec2[:, 0:NCOL], g_ret_out_2[0].rearrange("h d -> (h d)"))):
                pool.dma_start(dst, src.partition_broadcast(P)).then_inc(sem("vec_in"), 16)
            pool.memset(MHALF, -0.5).then_inc(sem("pool_half"), 1)
            pool.wait_ge(sem("pool_half"), 1)

            def norm_power(k):
                power(RS[:, 2 * k:2 * k + 2], RS[:, 2 * k:2 * k + 2], 2, "stat_ms", k + 1, "stat_rs")

            norm_power(0)
            pool.wait_ge(sem("consts_in"), 16)
            pool.wait_ge(sem("ev0"), 5)
            pool.wait_ge(sem("ev1"), 5)
            idx = PA[:, :, IQ:IW].rearrange("p t (h d) -> p t h d", d=64)
            ci, si = (spread(cst[:, C_ROPE_I + 16 * k:C_ROPE_I + 16 * k + 16].rearrange("p (t d) -> p t d", t=2), 2, 9) for k in range(2))
            x1, x2 = idx[:, :, :, 0:8], idx[:, :, :, 8:16]
            pr = [RTI[:, k].rearrange("p (t h d) -> p t h d", t=2, h=9) for k in range(4)]
            for n, (a, f) in enumerate(((x1, ci), (x2, si), (x2, ci), (x1, si))):
                for t in range(NT):
                    ins = pool.tensor_tensor(pr[n][:, t], a[:, t], f[:, t], ALU.mult)
            ins.then_inc(sem("pool_step"), 1)
            pool.wait_ge(sem("pool_step"), 1)
            for t in range(NT):
                pool.tensor_tensor(x1[:, t], pr[0][:, t], pr[1][:, t], ALU.subtract)
                ins = pool.tensor_tensor(x2[:, t], pr[2][:, t], pr[3][:, t], ALU.add)
            ins.then_inc(sem("pool_step"), 1)
            pool.wait_ge(sem("pool_step"), 2)
            for n in range(2):
                ins = pool.tensor_copy(IKD[:, :, n, :], PA[:, :, IK:IW])
            ins.then_inc(sem("idx_rot"), 1)
            power(RNA, SSA, 20, "att_ms", 1, "att_rn")
            power(RQK, SSK, 32, "gdn_ms", 1, "gdn_rq")
            pool.wait_ge(sem("gdn_kv"), 8)
            pool.wait_ge(sem("gdn_e"), 1)
            kn = KN.rearrange("p t h d -> p (t h) d")
            pool.tensor_tensor(KD.rearrange("p t h d -> p (t h) d"), kn, spread(ED, 2, P), ALU.mult).then_inc(sem("gdn_kd"), 1)
            pool.wait_ge(sem("gdn_beg"), 1)
            pool.tensor_tensor(KBG.rearrange("p t h d -> p (t h) d"), kn, spread(BEG, 2, P), ALU.mult).then_inc(sem("gdn_kbg"), 1)
            power(RSO, SSO, 16, "o_ms", 1, "o_rs")
            norm_power(1)
            norm_power(2)
            power(RNF, SSF, 32, "fox_ms", 1, "fox_rn")
            power(RSTD, VAR, 16, "ret_ms", 1, "ret_rs")
            norm_power(3)
            power(RNX[:, 0:8], SSX, 8, "x_ms", 1, "x_rn")
            norm_power(4)
            power(RNX[:, 8:16], SSX, 8, "x_ms", 2, "x_rn")
            norm_power(5)


_INS = ['x', 'norm_mix_g', 'w_in', 'conv_w', 'a_log', 'dt_bias', 'gdn_norm_g', 'q_norm_g', 'k_norm_g', 'w_out', 'norm_mlp_g',
        'w_mlp_up', 'w_mlp_down', 'mem_2', 'g_mix_2', 'w_in_2', 'b_forget_2', 'g_ret_out_2', 'g_fox_q_2', 'g_fox_k_2', 'w_out_2',
        'g_xattn_2', 'w_xq_2', 'w_xkv_2', 'g_mem_2', 'g_xq_2', 'g_xk_2', 'w_xo_2', 'g_ffn_2', 'w_gate_2', 'w_up_2', 'w_down_2']


def kernel(**inputs):
    import numpy as _np
    import concourse.bacc as _bacc
    from concourse import mybir as _mybir
    from concourse.bass_utils import run_bass_kernel_spmd as _run

    nc = _bacc.Bacc("TRN2", target_bir_lowering=False, num_devices=1)
    arrays, args = {}, []
    given = [(name, _np.ascontiguousarray(inputs[name])) for name in _INS]
    given += [("constants", constants()), ("retention", retention_weights())]
    for name, a in given:
        arrays[f"in_{name}_dram"] = a
        args.append(nc.dram_tensor(f"in_{name}_dram", a.shape, _mybir.dt.from_np(a.dtype), kind="ExternalInput").ap())
    args.append(nc.dram_tensor("out_0_dram", (1, SEQ, D), _mybir.dt.float32, kind="ExternalOutput").ap())
    build(nc, *args)
    r = _run(nc, [arrays], core_ids=[0])
    return r.results[0]["out_0_dram"]
```

```python
from contextlib import ExitStack

import concourse.bass as bass
from concourse import mybir

F32 = mybir.dt.float32
F32R = mybir.dt.float32r
ALU = mybir.AluOpType
ACT = mybir.ActivationFunctionType
AX_X = mybir.AxisListType.X

P = 128
SEQ = 256
NT = SEQ // P
D = 1024
KT = D // P
EPS = 1e-6
NCOL = 512
CK = 4
SLOTS = 4
DFF = 4096
DFF2 = 2816
MEMORIES = 256

A0 = 4096
A_W = 2136
AQ, AK, AV, IQ, IK, IW = 16, 1040, 1296, 1552, 2064, 2128
RQ, RK, RV, RG, FQ, FK, FV, FG = 0, 512, 1024, 1536, 2048, 2560, 3072, 3584
W2 = 3592

EXCLUDED = -1e30
UNREACHED = -3.0e38
TAKEN = -3.4e38
BETWEEN = -3.2e38

C_ID, C_ONES, C_CUM, C_ZERO, C_TRI, C_TRIX, C_NEG, C_LEV = 0, 128, 256, 384, 512, 640, 768, 896
LEVELS = 7
C_ROPE_A = C_LEV + LEVELS * P
C_ROPE_I = C_ROPE_A + 64
C_ROPE_R = C_ROPE_I + 32
C_N = C_ROPE_R + 128

WORK_A = [(0, range(0, 4)), (0, range(4, 8))] + [(1, range(h, h + 2)) for h in range(0, 8, 2)]
WORK_X = [(t, range(h, h + 2)) for t in range(NT) for h in (0, 2)]


def keys_of(work, k):
    return NCOL // len(work[k][1])



def constants():
    import numpy as np

    c = np.zeros((P, C_N), np.float32)
    row, col = np.arange(P)[:, None], np.arange(P)[None, :]
    c[:, C_ID:C_ID + P] = row == col
    c[:, C_ONES:C_ONES + P] = 1
    c[:, C_CUM:C_CUM + P] = row <= col
    c[:, C_TRI:C_TRI + P] = np.where(col <= row, 0, EXCLUDED)
    c[:, C_TRIX:C_TRIX + P] = np.where(col <= row, 0, UNREACHED)
    c[:, C_NEG:C_NEG + P] = np.where(col >= row, 0, EXCLUDED)
    for n in range(LEVELS):
        h = 1 << n
        c[:, C_LEV + P * n:C_LEV + P * n + P] = (row // (2 * h) == col // (2 * h)) & (row // h % 2 == 0) & (col // h % 2 == 1)

    def rope(at, half, rot, theta):
        inv = np.float32(theta) ** (-np.arange(0, rot, 2, dtype=np.float32) / np.float32(rot))
        ang = np.arange(SEQ, dtype=np.float32)[:, None] * inv.astype(np.float32)[None, :]
        for t in range(NT):
            a = ang[P * t:P * t + P].astype(np.float64)
            c[:, at + t * half:at + t * half + half] = np.cos(a)
            c[:, at + (NT + t) * half:at + (NT + t) * half + half] = np.sin(a)

    rope(C_ROPE_A, 16, 32, 500000.0)
    rope(C_ROPE_I, 8, 16, 500000.0)
    rope(C_ROPE_R, 32, 64, 10000.0)
    return c


def retention_weights():
    import numpy as np

    w = np.zeros((P, 8 * 384), np.float32)
    s, t = np.arange(SEQ)[:, None], np.arange(SEQ)[None, :]
    for h in range(8):
        gamma = 1.0 - 2.0 ** (-5.0 - h)
        full = np.where(s // 64 <= t // 64, gamma ** np.abs(t - s), 0) / 8
        p, q = h % 2, h // 2
        w[:, 512 * (2 * p + q // 2) + 256 * (q % 2):][:, :256] = full[:P]
        w[:, 2048 + 512 * p + 128 * q:][:, :128] = full[P:, P:]
    return w


def build(nc, x_in, norm_mix_g, w_in, conv_w, a_log, dt_bias, gdn_norm_g, q_norm_g, k_norm_g, w_out,
          norm_mlp_g, w_mlp_up, w_mlp_down, mem_2, g_mix_2, w_in_2, b_forget_2, g_ret_out_2,
          g_fox_q_2, g_fox_k_2, w_out_2, g_xattn_2, w_xq_2, w_xkv_2, g_mem_2, g_xq_2, g_xk_2, w_xo_2,
          g_ffn_2, w_gate_2, w_up_2, w_down_2, consts, ret_w, out):
    ctx = ExitStack()
    with ctx:
        def sb(name, shape, dt=F32, stack=None):
            return (stack or ctx).enter_context(nc.sbuf_tensor(name, shape, dt))

        named = {}

        def sem(name):
            if name not in named:
                named[name] = ctx.enter_context(nc.semaphore(name))
            return named[name]

        blocks = []

        def segment(name, w, first, widths, kt=KT):
            start = len(blocks)
            for width in widths:
                chunk0 = blocks[-1]["chunk0"] + blocks[-1]["chunks"] if blocks else 0
                blocks.append(dict(seg=name, w=w, col=first, n=width, kt=kt, chunk0=chunk0, chunks=-(-kt // CK)))
                first += width
            return start

        win = w_in[0]
        B_A = segment("a", win, A0, [512] * 3 + [300] * 2)
        B_Q = segment("qkv", win, 0, [512] * 6)
        B_GB = segment("gate_b", win, 7256, [512] * 2)
        B_Z = segment("z", win, 3072, [512] * 2)
        B_GA = segment("gate_a", win, 6232, [512] * 2)
        B_O = segment("out", w_out[0], 0, [512] * 2)
        B_UP = segment("up", w_mlp_up[0], 0, [512] * 8)
        B_DN = segment("down", w_mlp_down[0], 0, [512] * 2, kt=DFF // P)
        B_2 = segment("in2", w_in_2[0], 0, [512] * 6 + [260] * 2)
        B_KV = segment("kv", w_xkv_2[0], 0, [512] * 4)
        B_O2 = segment("out2", w_out_2[0], 0, [512] * 2)
        B_XQ = segment("xq", w_xq_2[0], 0, [512] * 2)
        B_XO = segment("xo", w_xo_2[0], 0, [512] * 2)
        B_GU = len(blocks)
        for c in range(0, DFF2, 512):
            n = min(512, DFF2 - c)
            segment("gate2", w_gate_2[0], c, [n])
            segment("up2", w_up_2[0], c, [n])
        B_D2 = segment("down2", w_down_2[0], 0, [512] * 2, kt=DFF2 // P)
        B_END = len(blocks)

        with nc.sbuf_tensor("raw", [P, SLOTS, CK, NCOL], F32) as raw:
            pass
        w_lo = sb("w_lo", [P, SLOTS, CK, NCOL], F32R)
        w_hi = sb("w_hi", [P, SLOTS, CK, NCOL], F32R)
        s_hi = sb("s_hi", [P, KT, SEQ], F32R)
        s_lo = sb("s_lo", [P, KT, SEQ], F32R)
        x = sb("x", [P, NT, D])
        cst = sb("cst", [P, C_N])
        gains = sb("gains", [P, 6, KT])
        cw = sb("cw", [P, 4, 24])
        vec = sb("vec", [P, 960])
        sm = sb("sm", [P, 640])
        ident = cst[:, C_ID:C_ID + P]
        junk = sb("junk", [P, D], mybir.dt.bfloat16)

        G = [[ctx.enter_context(nc.psum_tensor(f"gemm{s}{t}", [P, NCOL], F32)) for t in range(NT)] for s in range(2)]
        M = [ctx.enter_context(nc.psum_tensor(f"mixbank{i}", [P, NCOL], F32)) for i in range(4)]

        V_QG, V_KG, V_GN, V_DT, V_AL, V_BF, V_FQ, V_FK = 0, 128, 256, 384, 392, 400, 408, 472
        V_XQ, V_XK = 536, 536 + 256
        vec2 = sb("vec2", [P, 512 + 256])
        NORMS = dict(mix=0, mlp=1, mix2=2, xattn=3, mem=4, ffn=5)

        def arena(name, words, stack):
            return sb(name, [P, words], F32, stack)

        a1 = ExitStack()
        ar = arena("mix1", 24800, a1)
        a1.close()
        a2 = ExitStack()
        hT_hi = sb("hT_hi", [P, DFF // P, SEQ], F32R, a2)
        hT_lo = sb("hT_lo", [P, DFF // P, SEQ], F32R, a2)
        hid = sb("hid", [P, 2, NT, NCOL], F32, a2)
        a2.close()
        a3 = ExitStack()
        ar2 = arena("mix2", 24800, a3)
        a3.close()
        a4 = ExitStack()
        h2_hi = sb("h2_hi", [P, DFF2 // P, SEQ], F32R, a4)
        h2_lo = sb("h2_lo", [P, DFF2 // P, SEQ], F32R, a4)
        hid2 = sb("hid2", [P, 2, NT, NCOL], F32, a4)
        sg2 = sb("sg2", [P, 2, NT, NCOL], F32, a4)
        a4.close()

        def view(base, at, *shape):
            n = 1
            for s in shape:
                n *= s
            v = base[:, at:at + n]
            if len(shape) == 1:
                return v
            names = "abcd"[:len(shape)]
            return v.rearrange(f"p ({' '.join(names)}) -> p {' '.join(names)}", **dict(zip(names, shape)))

        def spread(ap, axis, n):
            v = ap.unsqueeze(axis)
            shape = list(v.shape)
            shape[axis] = n
            return v.to_broadcast(shape)

        PA = view(ar, 0, NT, A_W)
        PQ = view(ar, 4272, NT, 3072)
        ZG = view(ar, 10416, NT, D)
        OA = view(ar, 12464, NT, 8, 128)
        TMP = view(ar, 14512, 2, NCOL)
        YT = view(ar, 15536, 24, SEQ)
        FREE1 = 21680
        SQ = view(ar, 15536, NT, 10, 128)
        qT = view(ar, 15536, 8, SEQ)
        kT = view(ar, 17584, 2, SEQ)
        iqT = view(ar, 18096, 4, SEQ)
        ikT = view(ar, 19120, SEQ)
        IKD = view(ar, 19376, NT, 2, 64)
        SC = view(ar, 19632, NT, SEQ)
        BIAS = view(ar, 20144, NT, SEQ)
        RT = view(ar, 20656, 4, NT * 160)
        RTI = view(ar, 21936, 4, NT * 72)
        RL = view(ar, 22512, 8, SEQ)
        LM = view(ar, 20656, 2, NCOL)
        PTS = view(ar, 22512, 2, NCOL)
        GU = view(ar, 0, 16, P)
        DM = view(ar, 2048, 16, P)
        KN = view(ar, 4272, NT, 8, P)
        VB = view(ar, 6320, NT, 8, P)
        KB = view(ar, 8368, NT, 8, P)
        KBT = view(ar, 19632, 8, SEQ)
        KD = view(ar, 21680, 8, P)
        KBG = view(ar, 22704, 8, P)
        AT = view(ar, 0, 16, P)
        QK = view(ar, 4272, 16, P)
        LT = view(ar, 19632, 16, P)
        XT = view(ar, 17584, 16, P)
        XI = view(ar, 8368, 16, P)
        PS = view(ar, 2048, 16, P)
        WT = view(ar, 19632, 8, P)
        UV = view(ar, 2048, NT, 8, P)
        ST = view(ar, 0, 8, P)
        O1 = view(ar, 8368, NT, 8, P)

        def st(at, n):
            return sm[:, at:at + n]

        SS, RS = st(0, 12), st(12, 12)
        HRS = st(24, 2)
        QRS = st(26, 2)
        SSA, RNA = st(28, 20), st(48, 20)
        IWS = st(68, 16)
        MX8 = st(84, 16)
        NEGM, SUMS, RSUM = st(100, 32), st(132, 32), st(164, 32)
        GA_, BT = st(196, 16), st(212, 16)
        SP = st(228, 48)
        GC = st(276, 32)
        EG, ED, KDF, BRK = st(340, 16), st(356, 16), st(372, 8), st(404, 16)
        SSK, RQK = st(420, 32), st(452, 32)
        SSO, RSO = st(484, 16), st(500, 16)
        HBT = st(516, 16)
        EXPA = st(532, 8)
        MHALF = st(540, 64)
        HALFRS2 = st(604, 4)

        FSQ, FQ = SP[:, 0:16], SP[:, 16:32]
        CT = view(ar, 21680, 2, 2, SEQ)
        hidden_rows, conv_rows = ar[:, 4272:4400], ar[:, 4400:4528]
        FL = st(608, 16).rearrange("p (t h) -> p t h", t=2)
        SSF, RNF = SSK, RQK
        SSX, RNX = st(28, 8), st(48, 16)
        MU, VAR, RSTD = GA_, BT, EG
        RS5H, RS5Q = st(624, 2), st(626, 2)

        P2R = view(ar2, 0, NT, 2048)
        P2F = view(ar2, 4096, NT, W2 - 2048)
        WR = view(ar2, 7184, 3072)
        MG2 = view(ar2, 10256, NT, D)
        MEM = view(ar2, 12304, NT, D)
        T0 = 14352
        RT2 = view(ar2, T0, 4, NT * 512)
        rqT = view(ar2, T0, 4, SEQ)
        rkT = view(ar2, T0 + 1024, 4, SEQ)
        PT2 = view(ar2, T0 + 2048, 3072)
        SQR = view(ar2, 21584, NT, 16, 64)
        TG = view(ar2, 23632, NT, NCOL)
        RSQ = view(ar2, T0 + 1024, NT, NCOL)
        QA = view(ar2, 19472, NT, 8, 66)
        KA = view(ar2, 20528, NT, 8, 66)
        qaT = view(ar2, T0, 8, SEQ)
        kaT = view(ar2, T0 + 2048, 8, SEQ)
        LM2 = view(ar2, 21584, 2, NCOL)
        PTS2 = view(ar2, 22608, 2, NCOL)
        KV = view(ar2, 0, NT, 2048)
        XQ = view(ar2, 7184, NT, D)
        XO = view(ar2, 10256, NT, D)
        SQX = view(ar2, T0 + 5120, NT, D)
        xqT = view(ar2, T0, 8, SEQ)
        xkT = view(ar2, T0 + 2048, 8, SEQ)

        block = ctx.enter_context(nc.Block())

        def at(base, step, i):
            return base if i is None else base + step * i

        def chunk_shape(b, c):
            return min(CK, blocks[b]["kt"] - CK * c), blocks[b]["n"]

        BY_POOL = set(range(B_Q + 2, B_Z + 2)) | {B_D2}

        def block_columns(b):
            first = blocks[b]["col"] - (A0 if blocks[b]["seg"] == "a" else 2048)
            return slice(first, first + blocks[b]["n"])

        def pool_chunk(b, c):
            return b in BY_POOL and c == 1

        def low_parts(b, c):
            mine = pool_chunk(b, c)
            return sum(pool_chunk(e, d) == mine for e in range(b + 1) for d in range(blocks[e]["chunks"]) if (e, d) <= (b, c))

        def fox_mask(t):
            return cst[:, C_TRI - P * t:C_TRI + P]

        @block.sync
        def _(sp):
            def load(b, c, i=None):
                n = blocks[b]["chunk0"] + c
                kn, width = chunk_shape(b, c)
                slot = n % SLOTS
                if n >= SLOTS:
                    sp.wait_ge(sem("mm_done"), at(n - SLOTS + 1, 4, i))
                rows = blocks[b]["w"][CK * P * c:CK * P * c + kn * P]
                src = rows[:, bass.ds(at(blocks[b]["col"], 2 * NCOL, i), width)]
                sp.dma_start(raw[:, slot, 0:kn, 0:width], src.rearrange("(k p) n -> p k n", p=P))\
                    .then_inc(sem(f"loaded{slot}"), 16)

            for t in range(NT):
                sp.dma_start(x[:, t, :], x_in[0, P * t:P * t + P, :]).then_inc(sem("x_in"), 16)
            b = 0
            while b < B_END:
                pairs = 0
                while (b >= 2 and b + 2 * pairs + 1 < B_END
                       and all(blocks[b + 2 * pairs + j]["seg"] == blocks[b]["seg"] and blocks[b + 2 * pairs + j]["n"] == NCOL
                               and blocks[b + 2 * pairs + j]["chunks"] == 2 for j in range(2))):
                    pairs += 1
                if pairs >= 2:
                    with sp.Fori(0, pairs) as i:
                        for j in range(2):
                            for c in range(2):
                                load(b + j, c, i)
                    b += 2 * pairs
                else:
                    for c in range(blocks[b]["chunks"]):
                        load(b, c)
                    b += 1
            for t in range(NT):
                sp.wait_ge(sem("x_final"), t + 1)
                sp.dma_start(out[0, P * t:P * t + P, :], x[:, t, :]).then_inc(sem("stored"), 16)
            sp.wait_ge(sem("stored"), 16 * NT)

        @block.tensor
        def _(pe):
            act_w = (s_hi, s_lo)

            def mm(b, i=None, stat=act_w, waits=(), only=None, turned=None):
                blk = blocks[b]
                if b >= 2 and not only:
                    pe.wait_ge(sem("ev0"), at(b - 1, 2, i))
                    pe.wait_ge(sem("ev1"), at(b - 1, 2, i))
                for s, v in waits:
                    pe.wait_ge(sem(s), v)
                for c in range(blk["chunks"]) if only is None else [only]:
                    n = blk["chunk0"] + c
                    kn, width = chunk_shape(b, c)
                    pe.wait_ge(sem("split_lo_pool" if pool_chunk(b, c) else "split_lo"), at(low_parts(b, c), 4, i))
                    for k in range(kn):
                        kt = CK * c + k
                        if turned is not None and kt % 2 == 0:
                            pe.wait_ge(sem("turn_lo"), turned - KT // 2 + kt // 2 + 1)
                        for t in range(NT):
                            o = G[b % 2][t][:, 0:width]
                            hi, lo = (s[:, kt, P * t:P * t + P] for s in stat)
                            wh, wl = (s[:, n % SLOTS, k, 0:width] for s in (w_hi, w_lo))
                            nc.tensor.matmul(o, hi, wh, start=kt == 0, stop=False)
                            nc.tensor.matmul(o, hi, wl, start=False, stop=False)
                            last = nc.tensor.matmul(o, lo, wh, start=False, stop=kt == blk["kt"] - 1)
                    last.then_inc(sem("mm_done"), 1)

            turns = [0]

            def turn(src, waits):
                for q in range(4):
                    for s, v in waits(q):
                        pe.wait_ge(sem(s), v)
                    for kk in range(2):
                        for t in range(NT):
                            last = nc.tensor.transpose(M[q][:, (2 * kk + t) * P:(2 * kk + t + 1) * P], src(2 * q + kk, t), ident)
                    last.then_inc(sem("turn_pe"), 1)
                turns[0] += 4

            def xtile(kt, t):
                return x[:, t, P * kt:P * kt + P]

            pe.wait_ge(sem("ident_in"), 32)
            nc.tensor.transpose(M[0][:, 0:8], hidden_rows[0:8, :], ident[0:8, 0:8]).then_inc(sem("vec_pe"), 1)
            pe.wait_ge(sem("x_in"), 32)
            turn(xtile, lambda q: [("vec_dve", 1)])
            mm(B_A, turned=4)
            pe.wait_ge(sem("rows_in"), 16 * 6)
            nc.tensor.transpose(M[0][:, 0:48], hidden_rows[0:48, :], ident[0:48, 0:48])
            nc.tensor.transpose(M[0][:, 128:224], conv_rows[0:96, :], ident[0:96, 0:96]).then_inc(sem("vec_pe"), 1)
            for k in range(1, 5):
                mm(B_A + k)
            mm(B_Q)

            def operands(banks):
                for e in banks:
                    if e >= 3:
                        pe.wait_ge(sem("relu"), 6)
                    if e >= 7:
                        pe.wait_ge(sem("attT_act"), 4)
                    o = M[e % 4]
                    for j in range(1 if e == 2 else 2):
                        for t in range(NT):
                            if e == 2:
                                src = IKD[:, t].rearrange("p a b -> p (a b)")
                            else:
                                c = IQ + P * (2 * e + j) if e < 2 else (AK + P * j if e == 3 else AQ + P * (2 * (e - 4) + j))
                                src = PA[:, t, c:c + P]
                            last = nc.tensor.transpose(o[:, (2 * j + t) * P:(2 * j + t + 1) * P], src, ident)
                    last.then_inc(sem("attT_pe"), 1)

            pe.wait_ge(sem("idx_rot"), 1)
            operands(range(3))
            mm(B_Q + 1)

            pe.wait_ge(sem("attT_act"), 3)
            for t in range(NT):
                for par in (0, 1) if t == 0 else (1, 0):
                    for q in range(4):
                        bank = par if t == 0 else 2 * par + q // 2
                        if t == 1 and par == 0 and q % 2 == 0:
                            pe.wait_ge(sem("relu"), 2)
                        ns = P * (t + 1)
                        o = M[bank][:, (q % (4 // (t + 1))) * ns:][:, 0:ns]
                        last = nc.tensor.matmul(o, iqT[64 * par:64 * par + 64, q, P * t:P * t + P],
                                                ikT[64 * par:64 * par + 64, 0:ns], start=True, stop=True)
                        if q == 3 or (t == 1 and q == 1):
                            last.then_inc(sem("scores"), 1)
            mm(B_Q + 2)
            pe.wait_ge(sem("att_rot"), 1)
            operands(range(3, 8))
            mm(B_Q + 3)
            mm(B_Q + 4)
            pe.wait_ge(sem("attT_act"), 6)
            pe.wait_ge(sem("attT_dve"), 2)

            groups = [0]

            def attention(work, queries, keys, values, width, mixed=None, busy=()):
                g0, n = groups[0], len(work)

                def logits(k):
                    t, heads = work[k]
                    ns = keys_of(work, k)
                    g = g0 + k
                    if k >= 2:
                        pe.wait_ge(sem("att_max"), g - 1)
                        pe.wait_ge(sem("att_exp"), g - 1)
                    for j, h in enumerate(heads):
                        parts = queries(h)
                        for e, (qq, kk) in enumerate(zip(parts, keys(h))):
                            last = nc.tensor.matmul(M[g % 2][:, j * ns:(j + 1) * ns], qq[:, P * t:P * t + P], kk[:, 0:ns],
                                                    start=e == 0, stop=e == len(parts) - 1)
                    last.then_inc(sem("att_logits"), 1)

                def turned(k, buf):
                    t, heads = work[k]
                    ns = keys_of(work, k)
                    g = g0 + k
                    pe.wait_ge(sem("att_exp"), g + 1)
                    if k >= 1:
                        pe.wait_ge(sem("att_ptc"), g)
                    for c in range(4):
                        last = nc.tensor.transpose(M[2][:, c * P:(c + 1) * P], buf[:, g % 2, c * P:(c + 1) * P], ident)
                    last.then_inc(sem("att_pt"), 1)

                def weighed(k, pts):
                    t, heads = work[k]
                    ns = keys_of(work, k)
                    g = g0 + k
                    pe.wait_ge(sem("att_ptc"), g + 1)
                    if k >= 1:
                        pe.wait_ge(sem("att_norm"), g)
                    per = ns // P
                    for j, h in enumerate(heads):
                        for s in range(per):
                            last = nc.tensor.matmul(M[3][:, j * width:(j + 1) * width], pts[:, g % 2, (j * per + s) * P:][:, 0:P],
                                                    values(h, s), start=s == 0, stop=s == per - 1)
                    last.then_inc(sem("att_out"), 1)

                buf, pts = mixed
                for s, v in busy:
                    pe.wait_ge(sem(s), v)
                for k in range(n + 2):
                    if k < n:
                        logits(k)
                    yield k
                    if 1 <= k <= n:
                        turned(k - 1, buf)
                    if k >= 2:
                        weighed(k - 2, pts)
                groups[0] += n

            for k in attention(WORK_A, lambda h: [qT[:, h, :]], lambda h: [kT[:, h // 4, :]],
                               lambda h, s: PA[:, s, AV + P * (h // 4):AV + P * (h // 4) + P], P,
                               mixed=(LM, PTS), busy=[("relu", 6)]):
                if k in (1, 2):
                    mm(B_Q + 5, only=k - 1)

            pe.wait_ge(sem("att_norm"), 6)
            pe.wait_ge(sem("ev0"), B_Q + 6)
            pe.wait_ge(sem("ev1"), B_Q + 6)
            pe.wait_ge(sem("gdn_g"), 1)
            nc.tensor.matmul(M[2][:, 0:16], cst[:, C_CUM:C_CUM + P], GA_, start=True, stop=True)
            nc.tensor.matmul(M[2][:, 16:32], cst[:, C_ONES:C_ONES + P], GA_, start=True, stop=True).then_inc(sem("gdn_gc"), 1)

            def conv_in(e):
                if e >= 2:
                    pe.wait_ge(sem("conv_dve"), e - 1)
                for j in range(2):
                    for t in range(NT):
                        c = P * (2 * e + j)
                        last = nc.tensor.transpose(M[e % 2][:, (2 * j + t) * P:(2 * j + t + 1) * P], PQ[:, t, c:c + P], ident)
                last.then_inc(sem("conv_pe"), 1)

            def conv_back(e):
                pe.wait_ge(sem("gdn_y"), e + 1)
                if e == 0:
                    pe.wait_ge(sem("gdn_gcc"), 1)
                elif e >= 10:
                    pe.wait_ge(sem("gdn_vb"), e - 9)
                elif e >= 2:
                    pe.wait_ge(sem("back_act"), e - 1)
                for j in range(2):
                    for t in range(NT):
                        last = nc.tensor.transpose(M[2 + e % 2][:, (2 * j + t) * P:(2 * j + t + 1) * P], YT[:, 2 * e + j, P * t:P * t + P], ident)
                last.then_inc(sem("back_pe"), 1)

            def decay_rows(u):
                if u < 2:
                    pe.wait_ge(sem("conv_dve"), 11 + u)
                    pe.wait_ge(sem("gdn_gu"), 1)
                else:
                    pe.wait_ge(sem("gdn_dm"), u - 1)
                src = GU[:, 4 * u:4 * u + 4, :].rearrange("p a b -> p (a b)")
                nc.tensor.matmul(M[u % 2][:, :], cst[:, C_ONES:C_ONES + P], src, start=True, stop=True).then_inc(sem("gdn_bc"), 1)

            FILL = {1: ([B_GB], 0), 2: ([B_GB], 1), 4: ([B_GB + 1], 0), 5: ([B_GB + 1], 1), 7: ([B_Z], 0), 8: ([B_Z], 1), 11: ([B_Z + 1], 0)}
            for e in range(14):
                if e < 12:
                    conv_in(e)
                else:
                    decay_rows(e - 12)
                if e >= 2:
                    conv_back(e - 2)
                if e in FILL:
                    mm(*FILL[e][0], only=FILL[e][1])
            decay_rows(2)
            decay_rows(3)

            for u in range(4):
                if u < 2:
                    pe.wait_ge(sem("gdn_vb"), 3 + u)
                else:
                    pe.wait_ge(sem("gdn_dm"), 1 + u)
                for q in range(4):
                    h, tok = 4 * (u % 2) + q, slice(P * (u // 2), P * (u // 2) + P)
                    last = nc.tensor.matmul(M[(u + 2) % 4][:, P * q:P * q + P], YT[:, 8 + h, tok], YT[:, h, tok], start=True, stop=True)
                last.then_inc(sem("gdn_kq"), 1)
            mm(B_Z + 1, only=1)
            pe.wait_ge(sem("gdn_kb"), 2)
            for e in range(4):
                pe.wait_ge(sem("gdn_qk"), e + 1)
                for j in range(2):
                    for t in range(NT):
                        last = nc.tensor.transpose(M[(e + 2) % 4][:, (2 * j + t) * P:(2 * j + t + 1) * P], KB[:, t, 2 * e + j, :], ident)
                last.then_inc(sem("gdn_ktT"), 1)
            pe.wait_ge(sem("gdn_kt"), 4)
            for u in range(4):
                for q in range(4):
                    h, tok = 4 * (u % 2) + q, slice(P * (u // 2), P * (u // 2) + P)
                    last = nc.tensor.matmul(M[u][:, P * q:P * q + P], YT[:, 8 + h, tok], KBT[:, h, tok], start=True, stop=True)
                last.then_inc(sem("gdn_kk"), 1)
            mm(B_GA, only=0)

            def unit(u, lhsT, rhs):
                for q in range(4):
                    last = nc.tensor.matmul(M[u][:, P * q:P * q + P], lhsT[:, 4 * u + q, :], rhs[:, 4 * u + q, :], start=True, stop=True)
                return last

            for u in range(4):
                pe.wait_ge(sem("inv_lt"), u + 1)
                for q in range(4):
                    last = nc.tensor.transpose(M[u][:, P * q:P * q + P], LT[:, 4 * u + q, :], ident)
                last.then_inc(sem("inv_p"), 1)
            for lv in range(1, LEVELS):
                for u in range(4):
                    pe.wait_ge(sem("inv_lt"), 4 * lv + u + 1)
                    pe.wait_ge(sem("inv_x"), 4 * (lv - 1) + u + 1)
                    unit(u, LT, XI).then_inc(sem("inv_p"), 1)
                if lv == 3:
                    mm(B_GA, only=1)
                if lv < LEVELS - 1:
                    for u in range(4):
                        pe.wait_ge(sem("inv_pc"), 4 * (lv - 1) + u + 1)
                        unit(u, XT, PS).then_inc(sem("inv_xp"), 1)
                for u in range(4):
                    if lv < LEVELS - 1:
                        pe.wait_ge(sem("inv_xi"), 4 * (lv - 1) + u + 1)
                    else:
                        pe.wait_ge(sem("inv_pc"), 4 * (lv - 1) + u + 1)
                    unit(u, PS, XT).then_inc(sem("inv_tp"), 1)

            pe.wait_ge(sem("inv_x"), 4 * LEVELS)
            for half in range(2):
                for q in range(4):
                    h = 4 * half + q
                    last = nc.tensor.matmul(M[half][:, P * q:P * q + P], KBG[:, h, :], XT[:, 8 + h, :], start=True, stop=True)
                last.then_inc(sem("gdn_w"), 1)
            for half in range(2):
                for q in range(4):
                    h = 4 * half + q
                    last = nc.tensor.matmul(M[2 + half][:, P * q:P * q + P], XT[:, h, :], VB[:, 0, h, :], start=True, stop=True)
                last.then_inc(sem("gdn_u"), 1)
            mm(B_GA + 1, only=0)
            for half in range(2):
                pe.wait_ge(sem("gdn_uc"), half + 1)
                for q in range(4):
                    h = 4 * half + q
                    last = nc.tensor.matmul(M[2 + half][:, P * q:P * q + P], KD[:, h, :], UV[:, 0, h, :], start=True, stop=True)
                last.then_inc(sem("st_kv"), 1)
            for half in range(2):
                pe.wait_ge(sem("gdn_wc"), half + 1)
                pe.wait_ge(sem("st_new"), half + 1)
                for q in range(4):
                    h = 4 * half + q
                    nc.tensor.matmul(M[half][:, P * q:P * q + P], XT[:, 8 + h, :], VB[:, 1, h, :], start=True, stop=False)
                    last = nc.tensor.matmul(M[half][:, P * q:P * q + P], WT[:, h, :], ST[:, h, :], start=False, stop=True)
                last.then_inc(sem("st_ws"), 1)
            for half in range(2):
                for q in range(4):
                    h = 4 * half + q
                    last = nc.tensor.matmul(M[2 + half][:, P * q:P * q + P], QK[:, h, :], UV[:, 0, h, :], start=True, stop=True)
                last.then_inc(sem("o_pe"), 1)
            for half in range(2):
                pe.wait_ge(sem("st_v"), half + 1)
                pe.wait_ge(sem("o_copied"), half + 1)
                for q in range(4):
                    h = 4 * half + q
                    nc.tensor.matmul(M[half][:, P * q:P * q + P], YT[:, h, P:2 * P], ST[:, h, :], start=True, stop=True)
                    last = nc.tensor.matmul(M[2 + half][:, P * q:P * q + P], QK[:, 8 + h, :], UV[:, 1, h, :], start=True, stop=True)
                last.then_inc(sem("o_pe"), 1)
            mm(B_GA + 1, only=1)

            turn(lambda kt, t: O1[:, t, kt, :], lambda q: [("o_done", 1 + q // 2)])
            for j in range(2):
                mm(B_O + j, turned=None if j else 8)

            turn(xtile, lambda q: [("ev0", B_O + 1 + q // 2), ("ev1", B_O + 1 + q // 2), ("turn_lo", 8)])

            def hidden(b, i, mlp):
                pe.wait_ge(sem(mlp["ready"]), at(b + 1, 2, i))
                for q in range(2):
                    bank = M[2 * (b % 2) + q]
                    if b >= 2 or i is not None:
                        pe.wait_ge(sem(mlp["lo"]), at(2 * (b - 2) + q + 1, 4, i))
                    for kk in range(2):
                        for t in range(NT):
                            c = P * (2 * q + kk)
                            last = nc.tensor.transpose(bank[:, (2 * kk + t) * P:(2 * kk + t + 1) * P], mlp["hid"][:, b % 2, t, c:c + P], ident)
                    last.then_inc(sem(mlp["pe"]), 1)

            mlp1 = dict(ready="hid_sq", lo="hid_lo", pe="hid_pe", hid=hid)
            mm(B_UP, turned=12)
            mm(B_UP + 1)
            hidden(0, None, mlp1)
            mm(B_UP + 2)
            hidden(1, None, mlp1)
            with pe.Fori(0, 2) as i:
                for j in range(2):
                    mm(B_UP + 3 + j, i)
                    hidden(2 + j, i, mlp1)
            mm(B_UP + 7)
            hidden(6, None, mlp1)
            hidden(7, None, mlp1)
            for j in range(2):
                mm(B_DN + j, stat=(hT_hi, hT_lo), waits=[("hid_lo", 16)])

            turn(xtile, lambda q: [("ev0", B_DN + 1 + q // 2), ("ev1", B_DN + 1 + q // 2), ("hid_lo", 16)])
            for j in range(4):
                mm(B_2 + j, turned=None if j else 16)
            pe.wait_ge(sem("ret_rot"), 1)
            for e in range(4):
                for j in range(2):
                    for t in range(NT):
                        c = (RQ if e < 2 else RK) + P * (2 * (e % 2) + j)
                        last = nc.tensor.transpose(M[e][:, (2 * j + t) * P:(2 * j + t + 1) * P], P2R[:, t, c:c + P], ident)
                last.then_inc(sem("retT"), 1)
            mm(B_2 + 4)
            mm(B_2 + 5)
            pe.wait_ge(sem("ret_act"), 2)
            pe.wait_ge(sem("ret_dve"), 2)
            for par in range(2):
                for half in range(2):
                    e = 2 * par + half
                    for j in range(2):
                        q = 2 * half + j
                        last = nc.tensor.matmul(M[e][:, 256 * j:256 * j + 256], rkT[64 * par:64 * par + 64, q, 0:P],
                                                rqT[64 * par:64 * par + 64, q, :], start=True, stop=True)
                    last.then_inc(sem("ret_s"), 1)
            for par in range(2):
                pe.wait_ge(sem("ret_w"), par + 1)
                for q in range(4):
                    last = nc.tensor.matmul(M[par][:, P * q:P * q + P], rkT[64 * par:64 * par + 64, q, P:2 * P],
                                            rqT[64 * par:64 * par + 64, q, P:2 * P], start=True, stop=True)
                last.then_inc(sem("ret_s"), 1)
            mm(B_2 + 6)
            mm(B_2 + 7)
            pe.wait_ge(sem("ret_w"), 6)
            for t in range(NT):
                for h in range(8):
                    par, q = h % 2, h // 2
                    o = M[2 + t][:, 64 * h:64 * h + 64]
                    early = PT2[:, 512 * (2 * par + q // 2) + 256 * (q % 2) + P * t:][:, 0:P]
                    v = [P2R[:, s, RV + 64 * h:RV + 64 * h + 64] for s in range(2)]
                    last = nc.tensor.matmul(o, early, v[0], start=True, stop=t == 0)
                    if t == 1:
                        late = PT2[:, 2048 + 512 * par + P * q:][:, 0:P]
                        last = nc.tensor.matmul(o, late, v[1], start=False, stop=True)
                last.then_inc(sem("ret_o"), 1)

            pe.wait_ge(sem("mem_in"), 32)
            turn(lambda kt, t: MEM[:, t, P * kt:P * kt + P], lambda q: [("ret_oc", 2)])
            mm(B_KV, turned=20)
            pe.wait_ge(sem("fox_f"), 1)
            nc.tensor.matmul(M[0][:, 0:8], cst[:, C_CUM:C_CUM + P], FL[:, 0, :], start=True, stop=True)
            nc.tensor.matmul(M[0][:, 8:16], cst[:, C_ONES:C_ONES + P], FL[:, 0, :], start=True, stop=False)
            nc.tensor.matmul(M[0][:, 8:16], cst[:, C_CUM:C_CUM + P], FL[:, 1, :], start=False, stop=True).then_inc(sem("fox_fc"), 1)
            mm(B_KV + 1)
            pe.wait_ge(sem("fox_aug"), 1)
            for e in range(8):
                src = QA if e < 4 else KA
                if e >= 4:
                    pe.wait_ge(sem("foxT_act" if e % 2 == 0 else "foxT_dve"), (e - 4) // 2 + 1)
                for j in range(2):
                    for t in range(NT):
                        last = nc.tensor.transpose(M[e % 4][0:66, (2 * j + t) * P:(2 * j + t + 1) * P], src[:, t, 2 * (e % 4) + j, :], ident)
                last.then_inc(sem("foxT_pe"), 1)
            pe.wait_ge(sem("foxT_act"), 4)
            pe.wait_ge(sem("foxT_dve"), 4)
            for k in attention(WORK_A, lambda h: [qaT[0:66, h, :]], lambda h: [kaT[0:66, h, :]],
                               lambda h, s: P2F[:, s, FV - 2048 + 64 * h:FV - 2048 + 64 * h + 64], 64, mixed=(LM2, PTS2)):
                if 1 <= k <= 4:
                    mm(B_KV + 2 + (k - 1) // 2, only=(k - 1) % 2)
            turn(lambda kt, t: MG2[:, t, P * kt:P * kt + P], lambda q: [("att_norm", 12), ("ret_done", 1)])
            for j in range(2):
                mm(B_O2 + j, turned=None if j else 24)

            turn(xtile, lambda q: [("ev0", B_O2 + 1 + q // 2), ("ev1", B_O2 + 1 + q // 2), ("turn_lo", 24)])
            for j in range(2):
                mm(B_XQ + j, turned=None if j else 28)
            for e in range(8):
                pe.wait_ge(sem("x_k" if e < 4 else "x_q"), 1)
                if e >= 4:
                    pe.wait_ge(sem("xT_act" if e % 2 == 0 else "xT_dve"), (e - 4) // 2 + 1)
                for j in range(2):
                    for t in range(NT):
                        c = P * (2 * (e % 4) + j)
                        src = (KV if e < 4 else XQ)[:, t, c:c + P]
                        last = nc.tensor.transpose(M[e % 4][:, (2 * j + t) * P:(2 * j + t + 1) * P], src, ident)
                last.then_inc(sem("xT_pe"), 1)
            pe.wait_ge(sem("xT_act"), 4)
            pe.wait_ge(sem("xT_dve"), 4)
            for k in attention(WORK_X, lambda h: [xqT[:, 2 * h + e, :] for e in range(2)],
                               lambda h: [xkT[:, 2 * h + e, :] for e in range(2)],
                               lambda h, s: KV[:, s, D + 256 * h:D + 256 * h + 256], 256, mixed=(LM2, PTS2)):
                pass
            turn(lambda kt, t: XO[:, t, P * kt:P * kt + P], lambda q: [("att_norm", 16)])
            for j in range(2):
                mm(B_XO + j, turned=None if j else 32)

            turn(xtile, lambda q: [("ev0", B_XO + 1 + q // 2), ("ev1", B_XO + 1 + q // 2), ("turn_lo", 32)])
            mlp2 = dict(ready="hid2_sq", lo="hid2_lo", pe="hid2_pe", hid=hid2)

            def hidden2(p, i=None, q_n=2):
                pe.wait_ge(sem("hid2_sq"), at(p + 1, 1, i))
                for q in range(q_n):
                    if p >= 1 or i is not None:
                        pe.wait_ge(sem("hid2_lo"), at(2 * (p - 1) + q + 1, 2, i))
                    for kk in range(2):
                        for t in range(NT):
                            c = P * (2 * q + kk)
                            last = nc.tensor.transpose(M[q][:, (2 * kk + t) * P:(2 * kk + t + 1) * P], hid2[:, 0, t, c:c + P], ident)
                    last.then_inc(sem("hid2_pe"), 1)

            for j in range(2):
                mm(B_GU + j, turned=None if j else 36)
            mm(B_GU + 2)
            hidden2(0)
            with pe.Fori(0, 3) as i:
                mm(B_GU + 3, i)
                mm(B_GU + 4, i)
                hidden2(1, i)
            mm(B_GU + 9)
            mm(B_GU + 10)
            hidden2(4)
            mm(B_GU + 11)
            hidden2(5, q_n=1)
            for j in range(2):
                mm(B_D2 + j, stat=(h2_hi, h2_lo), waits=[("hid2_lo", 11)])

        @block.scalar
        def _(act):
            seen = {}

            def sig(ins, name):
                seen[name] = seen.get(name, 0) + 1
                ins.then_inc(sem(name), 1)

            def own(name):
                act.wait_ge(sem(name), seen[name])

            def split(b, c, i=None):
                n = blocks[b]["chunk0"] + c
                kn, width = chunk_shape(b, c)
                act.wait_ge(sem(f"loaded{n % SLOTS}"), at(16 * (n // SLOTS + 1), 16, i))
                nc.scalar.activation(w_hi[:, n % SLOTS, 0:kn, 0:width], raw[:, n % SLOTS, 0:kn, 0:width], ACT.Copy)\
                    .then_inc(sem("split_hi"), 1)

            def begin(b, i=None):
                for c in range(2, blocks[b]["chunks"]):
                    split(b, c, i)
                if b + 1 < B_END:
                    for c in range(2):
                        split(b + 1, c, i)

            def mm_finished(b, i=None):
                act.wait_ge(sem("mm_done"), at(blocks[b]["chunk0"] + blocks[b]["chunks"], 4, i))

            def project(b, dst, scale, i=None):
                mm_finished(b, i)
                nc.scalar.activation(dst, G[b % 2][0][:, 0:blocks[b]["n"]], ACT.Copy, scale=scale).then_inc(sem("ev0"), 1)

            def turn_hi(norm=None):
                for q in range(4):
                    act.wait_ge(sem("turn_pe"), seen.get("turn_hi", 0) + 1)
                    if norm is None:
                        ins = nc.scalar.activation(s_hi[:, 2 * q:2 * q + 2, :], M[q].rearrange("p (a b) -> p a b", a=2), ACT.Copy)
                    else:
                        for kk in range(2):
                            ins = nc.scalar.activation(s_hi[:, 2 * q + kk, :], M[q][:, SEQ * kk:SEQ * kk + SEQ], ACT.Copy,
                                                       scale=gains[:, norm, 2 * q + kk:2 * q + kk + 1])
                    sig(ins, "turn_hi")

            def squares(norm, src):
                for t in range(NT):
                    if norm + t > 0:
                        act.wait_ge(sem("stat_ss"), 2 * norm + t)
                    nc.scalar.activation(junk[:, :], src[:, t, :], ACT.Square, accum_out=SS[:, 2 * norm + t:2 * norm + t + 1])\
                        .then_inc(sem("stat_ss"), 1)

            act.dma_start(ident, consts[:, C_ID:C_ID + P]).then_inc(sem("ident_in"), 16)
            act.dma_start(hidden_rows[0:8, :], norm_mix_g[0].rearrange("(k p) -> k p", p=P)).then_inc(sem("ident_in"), 16)
            turn_hi(NORMS["mix"])
            split(0, 0)
            split(0, 1)
            act.dma_start(cst[:, P:], consts[:, P:]).then_inc(sem("consts_in"), 16)
            act.wait_ge(sem("x_in"), 32)
            squares(0, x)
            act.wait_ge(sem("stat_rs"), 1)
            for k in range(5):
                begin(B_A + k)
                project(B_A + k, PA[:, 0, block_columns(B_A + k)], RS[:, 0:1])
            begin(B_Q)
            act.wait_ge(sem("ev1"), 5)
            act.wait_ge(sem("ev0"), 5)
            for t in range(NT):
                ins = nc.scalar.activation(SQ[:, t], PA[:, t, AQ:AV].rearrange("p (h d) -> p h d", d=P), ACT.Square)
            ins.then_inc(sem("att_sq"), 1)
            act.wait_ge(sem("vec_in"), 16 * 11)
            nc.scalar.activation(SP[:, 40:48], vec[:, V_AL:V_AL + 8], ACT.Exp)
            act.wait_ge(sem("g_abs"), 1)
            sig(nc.scalar.activation(SP[:, 16:32], SP[:, 0:16], ACT.Exp, scale=-1.0), "g_exp")
            sig(nc.scalar.activation(BT.rearrange("p (t h) -> p t h", t=2), PA[:, :, 8:16], ACT.Tanh, scale=0.5), "b_tanh")
            own("g_exp")
            nc.scalar.activation(SP[:, 16:32], SP[:, 16:32], ACT.Ln, bias=1.0).then_inc(sem("g_ln"), 1)
            def operand(e, dst):
                act.wait_ge(sem("attT_pe"), e + 1)
                if e == 2:
                    ins = nc.scalar.activation(dst, M[2][:, 0:SEQ], ACT.Copy)
                else:
                    ins = nc.scalar.activation(dst, M[e % 4].rearrange("p (a b) -> p a b", a=2), ACT.Copy)
                sig(ins, "attT_act")

            project(B_Q, PQ[:, 0, 0:NCOL], RS[:, 0:1])
            for e, dst in enumerate((iqT[:, 0:2, :], iqT[:, 2:4, :], ikT)):
                operand(e, dst)
            begin(B_Q + 1)
            project(B_Q + 1, PQ[:, 0, NCOL:2 * NCOL], RS[:, 0:1])
            act.wait_ge(sem("scores"), 1)
            nc.scalar.activation(RL[:, 0:8:2, 0:P], M[0].rearrange("p (a b) -> p a b", a=4), ACT.Relu).then_inc(sem("relu"), 1)
            act.wait_ge(sem("scores"), 2)
            nc.scalar.activation(RL[:, 1:8:2, 0:P], M[1].rearrange("p (a b) -> p a b", a=4), ACT.Relu).then_inc(sem("relu"), 1)
            act.wait_ge(sem("acc"), 1)
            for n, (bank, h0) in enumerate(((2, 1), (3, 5), (0, 0), (1, 4))):
                act.wait_ge(sem("scores"), 3 + n)
                nc.scalar.activation(RL[:, h0:h0 + 3:2, :], M[bank].rearrange("p (a b) -> p a b", a=2), ACT.Relu).then_inc(sem("relu"), 1)
            begin(B_Q + 2)
            project(B_Q + 2, PQ[:, 0, NCOL * 2:NCOL * 3], RS[:, 0:1])
            for e, dst in ((3, kT), (5, qT[:, 2:4, :]), (7, qT[:, 6:8, :])):
                operand(e, dst)
            begin(B_Q + 3)
            for k in (3, 4):
                project(B_Q + k, PQ[:, 0, NCOL * k:NCOL * k + NCOL], RS[:, 0:1])
                begin(B_Q + k + 1)

            groups = [0]

            def attention(work, scale, src, dst):
                for k, (t, heads) in enumerate(work):
                    g = groups[0] + k
                    ns = keys_of(work, k)
                    act.wait_ge(sem("att_max"), g + 1)
                    if k >= 2:
                        act.wait_ge(sem("att_pt"), g - 1)
                    for j, h in enumerate(heads):
                        ins = nc.scalar.activation(dst[:, g % 2, j * ns:(j + 1) * ns], src(g)[:, j * ns:(j + 1) * ns], ACT.Exp, scale=scale,
                                                   bias=NEGM[:, 4 * (g % 8) + j:4 * (g % 8) + j + 1],
                                                   accum_out=SUMS[:, 4 * (g % 8) + j:4 * (g % 8) + j + 1])
                    ins.then_inc(sem("att_exp"), 1)
                    yield k
                groups[0] += len(work)

            for k in attention(WORK_A, P ** -0.5, lambda g: LM[:, g % 2], LM):
                if k == 3:
                    project(B_Q + 5, PQ[:, 0, NCOL * 5:NCOL * 6], RS[:, 0:1])
                    begin(B_GB)

            def gate(b, dst, t, scale, after=()):
                mm_finished(b)
                for s, v in after:
                    act.wait_ge(sem(s), v)
                return nc.scalar.activation(dst, G[b % 2][t][:, :], ACT.Tanh, scale=scale)

            act.wait_ge(sem("gdn_gcc"), 2)
            nc.scalar.activation(EG, GC[:, 0:16], ACT.Exp)
            nc.scalar.activation(ED, GC[:, 16:32], ACT.Exp).then_inc(sem("gdn_e"), 1)
            act.wait_ge(sem("stat_ss"), 2)

            def taken_back(e):
                act.wait_ge(sem("back_pe"), e + 1)
                if e >= 2:
                    act.wait_ge(sem("back_act"), e - 1)
                bank = M[2 + e % 2]
                for j in range(2):
                    for t in range(NT):
                        n = 2 * j + t
                        c = 16 * (e // 4) + 8 * t + 2 * (e % 4) + j
                        ins = nc.scalar.activation(junk[:, P * (4 * (e % 2) + n):][:, 0:P], bank[:, P * n:P * n + P], ACT.Square, accum_out=SSK[:, c:c + 1])
                if e >= 4:
                    h = 2 * (e % 4)
                    ins = nc.scalar.activation(KN[:, :, h:h + 2, :].rearrange("p t j d -> p j t d"), bank.rearrange("p (j t d) -> p j t d", j=2, t=2), ACT.Copy)
                ins.then_inc(sem("back_act"), 1)

            for e in range(13):
                if e < 12:
                    act.wait_ge(sem("conv_pe"), e + 1)
                    for j in range(2):
                        ct = 2 * e + j
                        ins = nc.scalar.activation(YT[:, ct, :], M[e % 2][:, SEQ * j:SEQ * j + SEQ], ACT.Copy, scale=cw[:, 3, ct:ct + 1])
                    ins.then_inc(sem("conv_act"), 1)
                if e >= 1:
                    act.wait_ge(sem("conv_dve"), e)
                    if e >= 3:
                        act.wait_ge(sem("gdn_y"), e - 2)
                    nc.scalar.activation(CT[:, (e - 1) % 2], YT[:, 2 * e - 2:2 * e, :], ACT.Tanh, scale=0.5).then_inc(sem("conv_tanh"), 1)
                if 3 <= e < 11:
                    taken_back(e - 3)
                if e in (3, 6):
                    b = B_GB + (e == 6)
                    for t in range(NT):
                        gate(b, TMP[:, t], t, HRS[:, t:t + 1], [("gate_used", b - B_GB)] if b > B_GB else []).then_inc(sem(f"ev{t}"), 1)
                    begin(b + 1)
                if e == 9:
                    for t in range(NT):
                        sig(gate(B_Z, ZG[:, t, 0:NCOL], t, HRS[:, t:t + 1]), "z_tanh")
                    begin(B_Z + 1)
            for u in range(4):
                act.wait_ge(sem("gdn_dm"), u + 1)
                nc.scalar.activation(DM[:, 4 * u:4 * u + 4, :], DM[:, 4 * u:4 * u + 4, :], ACT.Exp).then_inc(sem("gdn_dme"), 1)
            for t in range(NT):
                sig(gate(B_Z + 1, ZG[:, t, NCOL:D], t, HRS[:, t:t + 1]), "z_tanh")
            for e in range(4):
                act.wait_ge(sem("gdn_ktT"), e + 1)
                nc.scalar.activation(KBT[:, 2 * e:2 * e + 2, :], M[(e + 2) % 4].rearrange("p (a b) -> p a b", a=2), ACT.Copy).then_inc(sem("gdn_kt"), 1)
            begin(B_GA)
            for lv in range(1, LEVELS):
                for u in range(4):
                    act.wait_ge(sem("inv_p"), 4 * lv + u + 1)
                    nc.scalar.activation(PS[:, 4 * u:4 * u + 4, :], M[u].rearrange("p (a b) -> p a b", a=4), ACT.Copy).then_inc(sem("inv_pc"), 1)
                if lv == 3:
                    for t in range(NT):
                        gate(B_GA, TMP[:, t], t, HRS[:, t:t + 1], [("gate_used", 2)]).then_inc(sem(f"ev{t}"), 1)
                    begin(B_GA + 1)
            for half in range(2):
                act.wait_ge(sem("gdn_w"), half + 1)
                nc.scalar.activation(WT[:, 4 * half:4 * half + 4, :], M[half].rearrange("p (a b) -> p a b", a=4), ACT.Copy, scale=-1.0).then_inc(sem("gdn_wc"), 1)
            for half in range(2):
                act.wait_ge(sem("st_kv"), half + 1)
                nc.scalar.activation(ST[:, 4 * half:4 * half + 4, :], M[2 + half].rearrange("p (a b) -> p a b", a=4), ACT.Copy).then_inc(sem("st_new"), 1)

            def output_squares(t):
                for h in range(8):
                    ins = nc.scalar.activation(junk[:, P * h:P * h + P], O1[:, t, h, :], ACT.Square, accum_out=SSO[:, 8 * t + h:8 * t + h + 1])
                ins.then_inc(sem("o_sq"), 1)

            for half in range(2):
                act.wait_ge(sem("o_pe"), half + 1)
                sig(nc.scalar.activation(O1[:, 0, 4 * half:4 * half + 4, :], M[2 + half].rearrange("p (a b) -> p a b", a=4), ACT.Copy), "o_copied")
            own("o_copied")
            act.wait_ge(sem("back_act"), 8)
            output_squares(0)
            act.wait_ge(sem("o_sq"), 1)
            act.wait_ge(sem("o_raw"), 2)
            output_squares(1)
            for t in range(NT):
                gate(B_GA + 1, TMP[:, t], t, HRS[:, t:t + 1], [("gate_used", 3)]).then_inc(sem(f"ev{t}"), 1)
            act.wait_ge(sem("o_sq"), 2)
            turn_hi()
            begin(B_O)
            begin(B_O + 1)
            turn_hi(NORMS["mlp"])
            act.wait_ge(sem("ev0"), B_UP)
            act.wait_ge(sem("ev1"), B_UP)
            squares(1, x)

            def square_hidden(b, i=None):
                for t in range(NT):
                    act.wait_ge(sem(f"ev{t}"), at(B_UP + b + 1, 2, i))
                    ins = nc.scalar.activation(hid[:, b % 2, t], hid[:, b % 2, t], ACT.Square)
                ins.then_inc(sem("hid_sq"), 1)

            def hidden_hi(b, i=None):
                for q in range(2):
                    act.wait_ge(sem("hid_pe"), at(2 * b + q + 1, 4, i))
                    nc.scalar.activation(hT_hi[:, bass.ds(at(4 * b + 2 * q, 8, i), 2), :], M[2 * (b % 2) + q].rearrange("p (a b) -> p a b", a=2), ACT.Copy)\
                        .then_inc(sem("hid_hi"), 1)

            begin(B_UP)
            square_hidden(0)
            with act.Fori(0, 3) as i:
                for j in range(2):
                    begin(B_UP + 1 + j, i)
                    hidden_hi(j, i)
                    square_hidden(1 + j, i)
            begin(B_UP + 7)
            hidden_hi(6)
            square_hidden(7)
            hidden_hi(7)
            begin(B_DN)
            begin(B_DN + 1)
            turn_hi(NORMS["mix2"])
            act.wait_ge(sem("ev0"), B_2)
            act.wait_ge(sem("ev1"), B_2)
            act.dma_start(WR, ret_w).then_inc(sem("ret_w_in"), 16)
            act.dma_start(MEM, mem_2[0].rearrange("(t p) d -> p t d", p=P)).then_inc(sem("mem_in"), 32)
            squares(2, x)
            act.wait_ge(sem("stat_rs"), 3)
            rs2 = RS[:, 4:5]
            for k in range(4):
                begin(B_2 + k)
                project(B_2 + k, P2R[:, 0, NCOL * k:NCOL * k + NCOL], rs2)
            begin(B_2 + 4)
            for e, dst in ((0, rqT[:, 0:2, :]), (2, rkT[:, 0:2, :])):
                act.wait_ge(sem("retT"), e + 1)
                nc.scalar.activation(dst, M[e].rearrange("p (a b) -> p a b", a=2), ACT.Copy).then_inc(sem("ret_act"), 1)
            project(B_2 + 4, P2F[:, 0, 0:NCOL], rs2)
            begin(B_2 + 5)
            project(B_2 + 5, P2F[:, 0, NCOL:2 * NCOL], rs2)
            act.wait_ge(sem("ev0"), B_2 + 6)
            act.wait_ge(sem("ev1"), B_2 + 6)
            for t in range(NT):
                ins = nc.scalar.activation(SQR[:, t], P2F[:, t, 0:1024].rearrange("p (h d) -> p h d", d=64), ACT.Square)
            ins.then_inc(sem("fox_sq"), 1)
            begin(B_2 + 6)
            project(B_2 + 6, P2F[:, 0, block_columns(B_2 + 6)], rs2)
            begin(B_2 + 7)
            project(B_2 + 7, P2F[:, 0, block_columns(B_2 + 7)], rs2)
            act.wait_ge(sem("ev0"), B_2 + 4)
            act.wait_ge(sem("ev1"), B_2 + 4)
            nc.scalar.activation(TG, P2R[:, :, RG:RG + NCOL], ACT.Tanh, scale=0.5).then_inc(sem("rg_tanh"), 1)
            act.wait_ge(sem("mem_in"), 32)
            squares(3, MEM)
            for t in range(NT):
                act.wait_ge(sem("ret_o"), t + 1)
                nc.scalar.activation(MG2[:, t, 0:NCOL], M[2 + t][:, :], ACT.Copy).then_inc(sem("ret_oc"), 1)
            turn_hi(NORMS["mem"])
            begin(B_KV)
            act.wait_ge(sem("ret_cen"), 1)
            nc.scalar.activation(RSQ, MG2[:, :, 0:NCOL], ACT.Square).then_inc(sem("ret_sq"), 1)
            act.wait_ge(sem("f_abs"), 1)
            sig(nc.scalar.activation(SP[:, 16:32], SP[:, 0:16], ACT.Exp, scale=-1.0), "g_exp")
            own("g_exp")
            nc.scalar.activation(SP[:, 16:32], SP[:, 16:32], ACT.Ln, bias=1.0).then_inc(sem("f_ln"), 1)
            act.wait_ge(sem("stat_rs"), 4)
            rs4 = RS[:, 6:7]
            project(B_KV, KV[:, 0, 0:NCOL], rs4)
            begin(B_KV + 1)
            project(B_KV + 1, KV[:, 0, NCOL:D], rs4)
            for e in range(0, 8, 2):
                act.wait_ge(sem("foxT_pe"), e + 1)
                dst = (qaT if e < 4 else kaT)[0:66, 2 * (e % 4):2 * (e % 4) + 2, :]
                nc.scalar.activation(dst, M[e % 4][0:66, :].rearrange("p (a b) -> p a b", a=2), ACT.Copy).then_inc(sem("foxT_act"), 1)
            begin(B_KV + 2)
            for k in attention(WORK_A, 1.0, lambda g: LM2[:, g % 2], LM2):
                if k == 1:
                    project(B_KV + 2, KV[:, 0, D:D + NCOL], rs4)
                    begin(B_KV + 3)
                if k == 4:
                    project(B_KV + 3, KV[:, 0, D + NCOL:2 * D], rs4)
                    begin(B_O2)
            turn_hi()
            act.wait_ge(sem("ev0"), B_O2)
            act.wait_ge(sem("ev1"), B_O2)
            nc.scalar.activation(SQX, KV[:, :, 0:D], ACT.Square).then_inc(sem("x_sqk"), 1)
            begin(B_O2 + 1)
            turn_hi(NORMS["xattn"])
            act.wait_ge(sem("ev0"), B_XQ)
            act.wait_ge(sem("ev1"), B_XQ)
            squares(4, x)
            act.wait_ge(sem("stat_rs"), 5)
            for k in range(2):
                begin(B_XQ + k)
                project(B_XQ + k, XQ[:, 0, NCOL * k:NCOL * k + NCOL], RS[:, 8:9])
            for e in range(0, 8, 2):
                if e == 4:
                    act.wait_ge(sem("ev0"), B_XO)
                    act.wait_ge(sem("ev1"), B_XO)
                    act.wait_ge(sem("x_ms"), 1)
                    nc.scalar.activation(SQX, XQ, ACT.Square).then_inc(sem("x_sqq"), 1)
                act.wait_ge(sem("xT_pe"), e + 1)
                dst = (xkT if e < 4 else xqT)[:, 2 * (e % 4):2 * (e % 4) + 2, :]
                nc.scalar.activation(dst, M[e % 4].rearrange("p (a b) -> p a b", a=2), ACT.Copy).then_inc(sem("xT_act"), 1)
            for k in attention(WORK_X, 1 / 16, lambda g: M[g % 2], LM2):
                pass
            turn_hi()
            begin(B_XO)
            begin(B_XO + 1)
            turn_hi(NORMS["ffn"])
            act.wait_ge(sem("ev0"), B_GU)
            act.wait_ge(sem("ev1"), B_GU)
            squares(5, x)
            act.wait_ge(sem("stat_rs"), 6)

            def gate_tanh(p, i=None):
                b = B_GU + 2 * p
                mm_finished(b, i)
                n = blocks[b]["n"]
                for t in range(NT):
                    if i is not None or p > 0:
                        act.wait_ge(sem(f"ev{t}"), at(b - 1, 2, i))
                    nc.scalar.activation(sg2[:, 0, t, 0:n], G[b % 2][t][:, 0:n], ACT.Tanh, scale=RS5H[:, t:t + 1]).then_inc(sem("gate_tanh"), 1)

            def scale_hidden(p, i=None):
                n = blocks[B_GU + 2 * p]["n"]
                for t in range(NT):
                    act.wait_ge(sem(f"ev{t}"), at(B_GU + 2 * p + 2, 2, i))
                    ins = nc.scalar.activation(hid2[:, 0, t, 0:n], hid2[:, 0, t, 0:n], ACT.Copy, scale=RS5Q[:, t:t + 1])
                ins.then_inc(sem("hid2_sq"), 1)

            def hidden2_hi(p, i=None, q_n=2):
                for q in range(q_n):
                    act.wait_ge(sem("hid2_pe"), at(2 * p + q + 1, 2, i))
                    nc.scalar.activation(h2_hi[:, bass.ds(at(4 * p + 2 * q, 4, i), 2), :], M[q].rearrange("p (a b) -> p a b", a=2), ACT.Copy)\
                        .then_inc(sem("hid2_hi"), 1)

            act.wait_ge(sem("rs5"), 1)
            begin(B_GU)
            gate_tanh(0)
            begin(B_GU + 1)
            scale_hidden(0)
            with act.Fori(0, 3) as i:
                begin(B_GU + 2, i)
                gate_tanh(1, i)
                begin(B_GU + 3, i)
                hidden2_hi(0, i)
                scale_hidden(1, i)
            begin(B_GU + 8)
            gate_tanh(4)
            begin(B_GU + 9)
            hidden2_hi(3)
            scale_hidden(4)
            begin(B_GU + 10)
            gate_tanh(5)
            hidden2_hi(4)
            begin(B_GU + 11)
            scale_hidden(5)
            hidden2_hi(5, q_n=1)
            begin(B_D2)
            begin(B_D2 + 1)

        @block.vector
        def _(dve):
            seen = {}
            V = nc.vector

            def sig(ins, name):
                seen[name] = seen.get(name, 0) + 1
                ins.then_inc(sem(name), 1)

            def link(ins):
                sig(ins, "dve_step")
                dve.wait_ge(sem("dve_step"), seen["dve_step"])

            def split(b, c, i=None):
                if pool_chunk(b, c):
                    return
                n = blocks[b]["chunk0"] + c
                kn, width = chunk_shape(b, c)
                dve.wait_ge(sem("split_hi"), at(n + 1, 4, i))
                s = n % SLOTS
                V.tensor_tensor(w_lo[:, s, 0:kn, 0:width], raw[:, s, 0:kn, 0:width], w_hi[:, s, 0:kn, 0:width].bitcast(F32), ALU.subtract)\
                    .then_inc(sem("split_lo"), 1)

            def begin(b, i=None):
                for c in range(2, blocks[b]["chunks"]):
                    split(b, c, i)
                if b + 1 < B_END:
                    for c in range(2):
                        split(b + 1, c, i)

            def mm_finished(b, i=None):
                dve.wait_ge(sem("mm_done"), at(blocks[b]["chunk0"] + blocks[b]["chunks"], 4, i))

            def project(b, dst, scale, i=None):
                mm_finished(b, i)
                V.tensor_scalar(dst, G[b % 2][1][:, 0:blocks[b]["n"]], scale, None, ALU.mult).then_inc(sem("ev1"), 1)

            def residual(b, half, last=False):
                mm_finished(b)
                for t in range(NT):
                    cols = x[:, t, NCOL * half:NCOL * half + NCOL]
                    ins = V.tensor_tensor(cols, G[b % 2][t][:, :], cols, ALU.add)
                    ins.then_inc(sem("x_final") if last else sem(f"ev{t}"), 1)

            def turn_lo(norm=None):
                for q in range(4):
                    dve.wait_ge(sem("turn_hi"), seen.get("turn_lo", 0) + 1)
                    if norm is None:
                        hi = s_hi[:, 2 * q:2 * q + 2, :].bitcast(F32)
                        ins = V.tensor_tensor(s_lo[:, 2 * q:2 * q + 2, :], M[q].rearrange("p (a b) -> p a b", a=2), hi, ALU.subtract)
                    else:
                        for kk in range(2):
                            kt = 2 * q + kk
                            ins = V.scalar_tensor_tensor(s_lo[:, kt, :], M[q][:, SEQ * kk:SEQ * kk + SEQ], gains[:, norm, kt:kt + 1],
                                                         s_hi[:, kt, :].bitcast(F32), ALU.mult, ALU.subtract)
                    sig(ins, "turn_lo")

            def mean_squares(norm):
                dve.wait_ge(sem("stat_ss"), 2 * norm + 2)
                V.tensor_scalar(RS[:, 2 * norm:2 * norm + 2], SS[:, 2 * norm:2 * norm + 2], 1 / D, EPS, ALU.mult, ALU.add).then_inc(sem("stat_ms"), 1)

            def rotate(x1, x2, cos, sin, prod, eng, lnk):
                eng.tensor_tensor(prod[0], x1, cos, ALU.mult)
                eng.tensor_tensor(prod[1], x2, sin, ALU.mult)
                eng.tensor_tensor(prod[2], x2, cos, ALU.mult)
                lnk(eng.tensor_tensor(prod[3], x1, sin, ALU.mult))
                eng.tensor_tensor(x1, prod[0], prod[1], ALU.subtract)
                return eng.tensor_tensor(x2, prod[2], prod[3], ALU.add)

            dve.wait_ge(sem("vec_pe"), 1)
            sig(V.tensor_copy(gains[:, 0, :], M[0][:, 0:8]), "vec_dve")
            turn_lo(NORMS["mix"])
            split(0, 0)
            split(0, 1)
            mean_squares(0)
            dve.wait_ge(sem("stat_rs"), 1)
            V.tensor_scalar(HRS, RS[:, 0:2], 0.5, None, ALU.mult)
            link(V.tensor_scalar(QRS, RS[:, 0:2], 0.25, None, ALU.mult))
            for k in range(5):
                begin(B_A + k)
                project(B_A + k, PA[:, 1, block_columns(B_A + k)], RS[:, 1:2])
                if k == 0:
                    dve.wait_ge(sem("vec_pe"), 2)
                    V.tensor_copy(gains[:, 1:6, :].rearrange("p a b -> p (a b)"), M[0][:, 8:48])
                    V.tensor_copy(cw.rearrange("p a b -> p (a b)"), M[0][:, 128:224]).then_inc(sem("vec_dve"), 1)
            begin(B_Q)
            dve.wait_ge(sem("ev0"), 5)
            dve.wait_ge(sem("ev1"), 5)
            dve.wait_ge(sem("vec_in"), 16 * 11)
            dve.wait_ge(sem("consts_in"), 16)
            sp2 = SP[:, 0:16].rearrange("p (t h) -> p t h", t=2)
            link(V.tensor_tensor(sp2, PA[:, :, 0:8], spread(vec[:, V_DT:V_DT + 8], 1, 2), ALU.add))
            link(V.tensor_scalar(GA_, SP[:, 0:16], 0.0, None, ALU.max))
            V.scalar_tensor_tensor(SP[:, 0:16], SP[:, 0:16], -1.0, SP[:, 0:16], ALU.mult, ALU.max).then_inc(sem("g_abs"), 1)
            heads = PA[:, :, AQ:AV].rearrange("p t (h d) -> p t h d", d=P)
            dve.wait_ge(sem("att_sq"), 1)
            link(V.tensor_reduce(SSA, SQ.rearrange("p t h d -> p (t h) d"), AX_X, ALU.add))
            V.tensor_scalar(SSA, SSA, 1 / P, EPS, ALU.mult, ALU.add).then_inc(sem("att_ms"), 1)
            V.tensor_scalar(IWS.rearrange("p (t h) -> p t h", t=2), PA[:, :, IW:IW + 8], 8 ** -0.5 * 64 ** -0.5, None, ALU.mult)
            project(B_Q, PQ[:, 1, 0:NCOL], RS[:, 1:2])
            dve.wait_ge(sem("att_rn"), 1)
            for t in range(NT):
                ins = V.tensor_tensor(heads[:, t], heads[:, t], spread(RNA[:, 10 * t:10 * t + 10], 2, P), ALU.mult)
            link(ins)
            for t in range(NT):
                V.tensor_tensor(heads[:, t, 0:8], heads[:, t, 0:8], spread(vec[:, V_QG:V_QG + P], 1, 8), ALU.mult)
                ins = V.tensor_tensor(heads[:, t, 8:10], heads[:, t, 8:10], spread(vec[:, V_KG:V_KG + P], 1, 2), ALU.mult)
            link(ins)
            ca, sa = (spread(cst[:, C_ROPE_A + 32 * k:C_ROPE_A + 32 * k + 32].rearrange("p (t d) -> p t d", t=2), 2, 10) for k in range(2))
            prods = [RT[:, k].rearrange("p (t h d) -> p t h d", t=2, h=10) for k in range(4)]
            sig(rotate(heads[:, :, :, 0:16], heads[:, :, :, 16:32], ca, sa, prods, V, link), "att_rot")
            begin(B_Q + 1)
            project(B_Q + 1, PQ[:, 1, NCOL:2 * NCOL], RS[:, 1:2])
            for t in range(NT):
                ns = P * (t + 1)
                dve.wait_ge(sem("relu"), 2 if t == 0 else 6)
                link(V.tensor_scalar(SC[:, t, 0:ns], RL[:, 0, 0:ns], IWS[:, 8 * t:8 * t + 1], None, ALU.mult))
                for h in range(1, 8):
                    ins = V.scalar_tensor_tensor(SC[:, t, 0:ns], RL[:, h, 0:ns], IWS[:, 8 * t + h:8 * t + h + 1], SC[:, t, 0:ns], ALU.mult, ALU.add)
                    if h < 7:
                        link(ins)
                    elif t == 0:
                        sig(ins, "acc")
                        dve.wait_ge(sem("acc"), 1)
                    else:
                        link(ins)
                diag = SC[:, t, P * t:P * t + P]
                link(V.tensor_tensor(diag, diag, cst[:, C_TRIX:C_TRIX + P], ALU.add))
            begin(B_Q + 2)
            dve.wait_ge(sem("b_tanh"), 1)
            link(V.tensor_scalar(BT, BT, 0.5, 0.5, ALU.mult, ALU.add))
            V.tensor_scalar(HBT, BT, 0.5, None, ALU.mult)
            dve.wait_ge(sem("g_ln"), 1)
            link(V.tensor_tensor(GA_, GA_, SP[:, 16:32], ALU.add))
            V.scalar_tensor_tensor(GA_.rearrange("p (t h) -> p t h", t=2), GA_.rearrange("p (t h) -> p t h", t=2), -1.0,
                                   spread(SP[:, 40:48], 1, 2), ALU.mult, ALU.mult).then_inc(sem("gdn_g"), 1)
            project(B_Q + 2, PQ[:, 1, NCOL * 2:NCOL * 3], RS[:, 1:2])
            for e, dst in ((4, qT[:, 0:2, :]), (6, qT[:, 4:6, :])):
                dve.wait_ge(sem("attT_pe"), e + 1)
                V.tensor_copy(dst, M[e % 4].rearrange("p (a b) -> p a b", a=2)).then_inc(sem("attT_dve"), 1)

            def select(rounds):
                for _ in rounds:
                    for t in range(NT):
                        ins = V.max(MX8[:, 8 * t:8 * t + 8], SC[:, t, 0:P * (t + 1)])
                    link(ins)
                    for t in range(NT):
                        ins = V.match_replace(SC[:, t, 0:P * (t + 1)], MX8[:, 8 * t:8 * t + 8], SC[:, t, 0:P * (t + 1)], TAKEN)
                    link(ins)

            select(range(4))
            begin(B_Q + 3)
            project(B_Q + 3, PQ[:, 1, NCOL * 3:NCOL * 4], RS[:, 1:2])
            begin(B_Q + 4)
            select(range(4))
            for t in range(NT):
                ns = P * (t + 1)
                link(V.tensor_scalar(BIAS[:, t, 0:ns], SC[:, t, 0:ns], BETWEEN, EXCLUDED, ALU.is_ge, ALU.mult))
                diag = BIAS[:, t, P * t:P * t + P]
                link(V.tensor_tensor(diag, diag, cst[:, C_TRI:C_TRI + P], ALU.add))
            project(B_Q + 4, PQ[:, 1, NCOL * 4:NCOL * 5], RS[:, 1:2])
            begin(B_Q + 5)

            groups = [0]

            def attention(work, scale, width, mask, lm, pts, dst):
                g0, n = groups[0], len(work)

                def greatest(k):
                    t, hs = work[k]
                    g, ns = g0 + k, keys_of(work, k)
                    a = 4 * (g % 8)
                    dve.wait_ge(sem("att_logits"), g + 1)
                    if mask is None:
                        link(V.tensor_reduce(NEGM[:, a:a + len(hs)], M[g % 2].rearrange("p (a b) -> p a b", b=ns), AX_X, ALU.max))
                    else:
                        if k >= 2:
                            dve.wait_ge(sem("att_pt"), g - 1)
                        for j in range(len(hs)):
                            ins = V.tensor_tensor_reduce(lm[:, g % 2, j * ns:(j + 1) * ns], M[g % 2][:, j * ns:(j + 1) * ns], mask(t), 1.0, -3.0e38,
                                                         ALU.add, ALU.max, NEGM[:, a + j:a + j + 1])
                        link(ins)
                    V.tensor_scalar(NEGM[:, a:a + len(hs)], NEGM[:, a:a + len(hs)], -scale, None, ALU.mult).then_inc(sem("att_max"), 1)

                def turned(k):
                    g = g0 + k
                    dve.wait_ge(sem("att_pt"), g + 1)
                    if k >= 2:
                        dve.wait_ge(sem("att_out"), g - 1)
                    V.tensor_copy(pts[:, g % 2, :], M[2][:, :]).then_inc(sem("att_ptc"), 1)

                def normed(k):
                    t, hs = work[k]
                    g = g0 + k
                    a = 4 * (g % 8)
                    link(V.reciprocal(RSUM[:, a:a + len(hs)], SUMS[:, a:a + len(hs)]))
                    dve.wait_ge(sem("att_out"), g + 1)
                    V.tensor_tensor(dst(t, hs), M[3][:, 0:width * len(hs)].rearrange("p (a b) -> p a b", b=width),
                                    spread(RSUM[:, a:a + len(hs)], 2, width), ALU.mult).then_inc(sem("att_norm"), 1)

                for k in range(n + 2):
                    if k < n:
                        greatest(k)
                    if 1 <= k <= n:
                        turned(k - 1)
                    if k >= 2:
                        normed(k - 2)
                    yield k
                groups[0] += n

            for k in attention(WORK_A, P ** -0.5, P, lambda t: BIAS[:, t, 0:P * (t + 1)], LM, PTS, lambda t, hs: OA[:, t, hs[0]:hs[-1] + 1, :]):
                if k == 4:
                    project(B_Q + 5, PQ[:, 1, NCOL * 5:NCOL * 6], RS[:, 1:2])
                    begin(B_GB)

            def silu(e):
                dve.wait_ge(sem("conv_tanh"), e + 1)
                y = YT[:, 2 * e:2 * e + 2, :]
                sig(V.scalar_tensor_tensor(y, CT[:, e % 2], 1.0, y, ALU.add, ALU.mult), "gdn_y")

            def z_block(b, half):
                for t in range(NT):
                    dve.wait_ge(sem("z_tanh"), 2 * half + t + 1)
                    cols = ZG[:, t, NCOL * half:NCOL * half + NCOL]
                    V.scalar_tensor_tensor(cols, cols, 1.0, G[b % 2][t][:, :], ALU.add, ALU.mult).then_inc(sem(f"ev{t}"), 1)

            def decays(u):
                dve.wait_ge(sem("gdn_bc"), u + 1)
                for q in range(4):
                    n = 4 * u + q
                    ins = V.scalar_tensor_tensor(DM[:, n, :], M[u % 2][:, P * q:P * q + P], GC[:, n:n + 1], cst[:, C_NEG:C_NEG + P], ALU.subtract, ALU.add)
                ins.then_inc(sem("gdn_dm"), 1)

            dve.wait_ge(sem("gdn_gc"), 1)
            sig(V.tensor_copy(GC, M[2][:, 0:32]), "gdn_gcc")
            dve.wait_ge(sem("gdn_gcc"), 1)
            sig(V.tensor_tensor(GC[:, 16:32], GC[:, 16:32], GC[:, 0:16], ALU.subtract), "gdn_gcc")
            oa = OA.rearrange("p t h d -> p t (h d)")
            for e in range(15):
                if e < 12:
                    dve.wait_ge(sem("conv_act"), e + 1)
                    for tap in range(1, 4):
                        for j in range(2):
                            ct = 2 * e + j
                            y = YT[:, ct, tap:SEQ]
                            ins = V.scalar_tensor_tensor(y, M[e % 2][:, SEQ * j:SEQ * j + SEQ - tap], cw[:, 3 - tap, ct:ct + 1], y, ALU.mult, ALU.add)
                        if tap < 3:
                            link(ins)
                    sig(ins, "conv_dve")
                if 1 <= e <= 12:
                    silu(e - 1)
                if e >= 11:
                    dve.wait_ge(sem("back_pe"), e - 2)
                    h = 2 * (e - 11)
                    f = HBT.rearrange("p (t h) -> p h t", t=2)[:, h:h + 2, :]
                    sig(V.tensor_tensor(VB[:, :, h:h + 2, :].rearrange("p t j d -> p j t d"), M[2 + (e - 3) % 2].rearrange("p (j t d) -> p j t d", j=2, t=2),
                                        spread(f, 3, P), ALU.mult), "gdn_vb")
                if e in (3, 6):
                    b = B_GB + (e == 6)
                    cols = slice(NCOL * (e == 6), NCOL * (e == 6) + NCOL)
                    for t in range(NT):
                        dve.wait_ge(sem(f"ev{t}"), b + 1)
                        ins = V.scalar_tensor_tensor(oa[:, t, cols], TMP[:, t], 1.0, oa[:, t, cols], ALU.add, ALU.mult)
                    ins.then_inc(sem("gate_used"), 1)
                    begin(b + 1)
                if e == 9:
                    z_block(B_Z, 0)
                    begin(B_Z + 1)
                if e == 11:
                    dve.wait_ge(sem("back_act"), 8)
                    V.tensor_scalar(SSK, SSK, 0.25, EPS, ALU.mult, ALU.add).then_inc(sem("gdn_ms"), 1)
                if 12 <= e < 14:
                    decays(e - 12)
            decays(2)
            decays(3)
            dve.wait_ge(sem("gdn_rq"), 1)
            dve.wait_ge(sem("gdn_e"), 1)
            link(V.tensor_scalar(RQK, RQK, 0.5, None, ALU.mult))
            V.tensor_tensor(KDF, RQK[:, 16:24], ED[:, 0:8], ALU.mult).then_inc(sem("gdn_kdf"), 1)
            link(V.tensor_tensor(BRK, RQK[:, 16:32], BT, ALU.mult))
            for t in range(NT):
                V.tensor_tensor(KB[:, t], KN[:, t], spread(BRK[:, 8 * t:8 * t + 8], 2, P), ALU.mult).then_inc(sem("gdn_kb"), 1)
            link(V.tensor_scalar(RQK[:, 0:16], RQK[:, 0:16], P ** -0.5, None, ALU.mult))
            V.scalar_tensor_tensor(FSQ, RQK[:, 0:16], 1 / P, RQK[:, 0:16], ALU.mult, ALU.mult)
            link(V.tensor_tensor(FQ.rearrange("p (t h) -> p t h", t=2), RQK[:, 0:16].rearrange("p (t h) -> p t h", t=2), spread(QRS, 2, 8), ALU.mult))

            def decayed(dst, bank, u, name):
                for q in range(4):
                    n = 4 * u + q
                    ins = V.scalar_tensor_tensor(dst[:, n, :], bank[:, P * q:P * q + P], RQK[:, 16 + n:17 + n], DM[:, n, :], ALU.mult, ALU.mult)
                ins.then_inc(sem(name), 1)

            dve.wait_ge(sem("gdn_kd"), 1)
            dve.wait_ge(sem("gdn_kb"), 2)
            for u in range(4):
                dve.wait_ge(sem("gdn_kq"), u + 1)
                dve.wait_ge(sem("gdn_dme"), u + 1)
                decayed(QK, M[(u + 2) % 4], u, "gdn_qk")
            z_block(B_Z + 1, 1)
            begin(B_GA)
            for u in range(4):
                dve.wait_ge(sem("gdn_kk"), u + 1)
                decayed(AT, M[u], u, "gdn_at")

            eye = spread(ident, 1, 4)
            dve.wait_ge(sem("gdn_kbg"), 1)
            for u in range(4):
                n = slice(4 * u, 4 * u + 4)
                dve.wait_ge(sem("inv_p"), u + 1)
                V.tensor_tensor(XT[:, n, :], eye, LT[:, n, :], ALU.subtract)
                V.tensor_tensor(XI[:, n, :], eye, M[u].rearrange("p (a b) -> p a b", a=4), ALU.subtract).then_inc(sem("inv_x"), 1)

            def gate_a(b, half):
                cols = slice(NCOL * half, NCOL * half + NCOL)
                for t in range(NT):
                    dve.wait_ge(sem(f"ev{t}"), b + 1)
                    ins = V.scalar_tensor_tensor(ZG[:, t, cols], TMP[:, t], 1.0, ZG[:, t, cols], ALU.add, ALU.mult)
                sig(ins, "gate_used")

            for lv in range(1, LEVELS):
                if lv < LEVELS - 1:
                    for u in range(4):
                        n = slice(4 * u, 4 * u + 4)
                        dve.wait_ge(sem("inv_xp"), 4 * (lv - 1) + u + 1)
                        V.tensor_tensor(XI[:, n, :], XI[:, n, :], M[u].rearrange("p (a b) -> p a b", a=4), ALU.subtract).then_inc(sem("inv_xi"), 1)
                for u in range(4):
                    n = slice(4 * u, 4 * u + 4)
                    dve.wait_ge(sem("inv_tp"), 4 * (lv - 1) + u + 1)
                    V.tensor_tensor(XT[:, n, :], XT[:, n, :], M[u].rearrange("p (a b) -> p a b", a=4), ALU.subtract).then_inc(sem("inv_x"), 1)
                if lv == 1:
                    zg = ZG.rearrange("p t (h d) -> p (t h) d", d=P)
                    link(V.tensor_tensor(zg, zg, spread(vec[:, V_GN:V_GN + P], 1, 16), ALU.mult))
                if lv == 3:
                    gate_a(B_GA, 0)
                    begin(B_GA + 1)
            for half in range(2):
                dve.wait_ge(sem("gdn_u"), half + 1)
                V.tensor_copy(UV[:, 0, 4 * half:4 * half + 4, :], M[2 + half].rearrange("p (a b) -> p a b", a=4)).then_inc(sem("gdn_uc"), 1)
            for half in range(2):
                dve.wait_ge(sem("st_ws"), half + 1)
                V.tensor_copy(UV[:, 1, 4 * half:4 * half + 4, :], M[half].rearrange("p (a b) -> p a b", a=4)).then_inc(sem("st_v"), 1)

            def output_norm(t):
                c = slice(8 * t, 8 * t + 8)
                dve.wait_ge(sem("o_sq"), t + 1)
                link(V.tensor_tensor(SSO[:, c], SSO[:, c], FSQ[:, c], ALU.mult))
                V.tensor_scalar(SSO[:, c], SSO[:, c], EPS, None, ALU.add).then_inc(sem("o_ms"), 1)

            def output_factors(t):
                c = slice(8 * t, 8 * t + 8)
                dve.wait_ge(sem("o_rs"), t + 1)
                link(V.tensor_tensor(RSO[:, c], RSO[:, c], FQ[:, c], ALU.mult))
                link(V.tensor_tensor(O1[:, t], O1[:, t], spread(RSO[:, c], 2, P), ALU.mult))

            output_norm(0)
            for half in range(2):
                hh = slice(4 * half, 4 * half + 4)
                dve.wait_ge(sem("o_pe"), 3 + half)
                link(V.tensor_tensor(O1[:, 1, hh, :], M[half].rearrange("p (a b) -> p a b", a=4), spread(EG[:, 8 + 4 * half:12 + 4 * half], 2, P), ALU.mult))
                sig(V.tensor_tensor(O1[:, 1, hh, :], M[2 + half].rearrange("p (a b) -> p a b", a=4), O1[:, 1, hh, :], ALU.add), "o_raw")
            output_factors(0)
            output_norm(1)
            output_factors(1)
            for half in range(2):
                if half == 1:
                    gate_a(B_GA + 1, 1)
                dve.wait_ge(sem("gate_used"), 3 + half)
                hh = slice(4 * half, 4 * half + 4)
                o = O1[:, :, hh, :].rearrange("p t h d -> p t (h d)")
                cols = slice(NCOL * half, NCOL * half + NCOL)
                link(V.tensor_tensor(o, o, ZG[:, :, cols], ALU.mult))
                sig(V.scalar_tensor_tensor(o, oa[:, :, cols], 0.5, o, ALU.mult, ALU.add), "o_done")
            turn_lo()
            begin(B_O)
            residual(B_O, 0)
            begin(B_O + 1)
            residual(B_O + 1, 1)
            turn_lo(NORMS["mlp"])
            mean_squares(1)
            dve.wait_ge(sem("stat_rs"), 2)

            def relu(b, i=None):
                mm_finished(B_UP + b, i)
                for t in range(NT):
                    if i is not None or b >= 2:
                        dve.wait_ge(sem("hid_pe"), at(2 * (b - 2) + 2, 4, i))
                    V.tensor_scalar(hid[:, b % 2, t], G[(B_UP + b) % 2][t][:, :], RS[:, 2 + t:3 + t], 0.0, ALU.mult, ALU.max).then_inc(sem(f"ev{t}"), 1)

            def hidden_lo(b, i=None):
                for q in range(2):
                    dve.wait_ge(sem("hid_hi"), at(2 * b + q + 1, 4, i))
                    kk = bass.ds(at(4 * b + 2 * q, 8, i), 2)
                    V.tensor_tensor(hT_lo[:, kk, :], M[2 * (b % 2) + q].rearrange("p (a b) -> p a b", a=2), hT_hi[:, kk, :].bitcast(F32), ALU.subtract)\
                        .then_inc(sem("hid_lo"), 1)

            begin(B_UP)
            relu(0)
            begin(B_UP + 1)
            relu(1)
            hidden_lo(0)
            begin(B_UP + 2)
            relu(2)
            hidden_lo(1)
            with dve.Fori(0, 2) as i:
                for j in range(2):
                    begin(B_UP + 3 + j, i)
                    relu(3 + j, i)
                    hidden_lo(2 + j, i)
            begin(B_UP + 7)
            relu(7)
            hidden_lo(6)
            hidden_lo(7)
            for j in range(2):
                begin(B_DN + j)
                residual(B_DN + j, j)
            turn_lo(NORMS["mix2"])
            mean_squares(2)
            dve.wait_ge(sem("stat_rs"), 3)
            rs2 = RS[:, 5:6]
            for k in range(4):
                begin(B_2 + k)
                project(B_2 + k, P2R[:, 1, NCOL * k:NCOL * k + NCOL], rs2)
                if k == 1:
                    dve.wait_ge(sem("ev0"), B_2 + 2)
                    dve.wait_ge(sem("ev1"), B_2 + 2)
                    qk = P2R[:, :, 0:1024].rearrange("p t (h d) -> p t h d", d=64)
                    cr, sr = (spread(cst[:, C_ROPE_R + 64 * n:C_ROPE_R + 64 * n + 64].rearrange("p (t d) -> p t d", t=2), 2, 16) for n in range(2))
                    pr = [RT2[:, n].rearrange("p (t h d) -> p t h d", t=2, h=16) for n in range(4)]
                    sig(rotate(qk[:, :, :, 0:32], qk[:, :, :, 32:64], cr, sr, pr, V, link), "ret_rot")
            begin(B_2 + 4)
            dve.wait_ge(sem("ret_rot"), 1)
            for e, dst in ((1, rqT[:, 2:4, :]), (3, rkT[:, 2:4, :])):
                dve.wait_ge(sem("retT"), e + 1)
                V.tensor_copy(dst, M[e].rearrange("p (a b) -> p a b", a=2)).then_inc(sem("ret_dve"), 1)
            project(B_2 + 4, P2F[:, 1, 0:NCOL], rs2)
            begin(B_2 + 5)
            dve.wait_ge(sem("ret_w_in"), 16)
            for e in range(4):
                dve.wait_ge(sem("ret_s"), e + 1)
                V.tensor_tensor(PT2[:, 512 * e:512 * e + 512], M[e][:, :], WR[:, 512 * e:512 * e + 512], ALU.mult).then_inc(sem("ret_w"), 1)
            for e in range(2):
                dve.wait_ge(sem("ret_s"), e + 5)
                V.tensor_tensor(PT2[:, 2048 + 512 * e:][:, 0:512], M[e][:, :], WR[:, 2048 + 512 * e:][:, 0:512], ALU.mult).then_inc(sem("ret_w"), 1)
            project(B_2 + 5, P2F[:, 1, NCOL:2 * NCOL], rs2)
            begin(B_2 + 6)
            dve.wait_ge(sem("fox_sq"), 1)
            link(V.tensor_reduce(SSF, SQR.rearrange("p t h d -> p (t h) d"), AX_X, ALU.add))
            V.tensor_scalar(SSF, SSF, 1 / 64, EPS, ALU.mult, ALU.add).then_inc(sem("fox_ms"), 1)
            project(B_2 + 6, P2F[:, 1, block_columns(B_2 + 6)], rs2)
            begin(B_2 + 7)
            project(B_2 + 7, P2F[:, 1, block_columns(B_2 + 7)], rs2)
            mean_squares(3)
            ret = [MG2[:, t, 0:NCOL].rearrange("p (h d) -> p h d", d=64) for t in range(NT)]
            for t in range(NT):
                dve.wait_ge(sem("ret_oc"), t + 1)
                ins = V.tensor_reduce(MU[:, 8 * t:8 * t + 8], ret[t], AX_X, ALU.add)
            link(ins)
            turn_lo(NORMS["mem"])
            begin(B_KV)
            link(V.tensor_scalar(MU, MU, 1 / 64, None, ALU.mult))
            for t in range(NT):
                ins = V.tensor_tensor(ret[t], ret[t], spread(MU[:, 8 * t:8 * t + 8], 2, 64), ALU.subtract)
            ins.then_inc(sem("ret_cen"), 1)
            dve.wait_ge(sem("ev0"), B_2 + 8)
            dve.wait_ge(sem("ev1"), B_2 + 8)
            link(V.tensor_tensor(sp2, P2F[:, :, 1536:1544], spread(vec[:, V_BF:V_BF + 8], 1, 2), ALU.add))
            link(V.tensor_scalar(FL.rearrange("p t h -> p (t h)"), SP[:, 0:16], 0.0, None, ALU.min))
            V.scalar_tensor_tensor(SP[:, 0:16], SP[:, 0:16], -1.0, SP[:, 0:16], ALU.mult, ALU.max).then_inc(sem("f_abs"), 1)
            dve.wait_ge(sem("ret_sq"), 1)
            link(V.tensor_reduce(VAR, RSQ.rearrange("p t (h d) -> p (t h) d", d=64), AX_X, ALU.add))
            V.tensor_scalar(VAR, VAR, 1 / 64, EPS, ALU.mult, ALU.add).then_inc(sem("ret_ms"), 1)
            dve.wait_ge(sem("f_ln"), 1)
            V.tensor_tensor(FL.rearrange("p t h -> p (t h)"), FL.rearrange("p t h -> p (t h)"), SP[:, 16:32], ALU.subtract).then_inc(sem("fox_f"), 1)
            dve.wait_ge(sem("fox_rn"), 1)
            for n, dst in enumerate((QA, KA)):
                for t in range(NT):
                    src = P2F[:, t, NCOL * n:NCOL * n + NCOL].rearrange("p (h d) -> p h d", d=64)
                    ins = V.tensor_tensor(dst[:, t, :, 0:64], src, spread(RNF[:, 16 * t + 8 * n:][:, 0:8], 2, 64), ALU.mult)
            link(ins)
            for n, (dst, g) in enumerate(((QA, V_FQ), (KA, V_FK))):
                d = dst.rearrange("p t h d -> p (t h) d")[:, :, 0:64]
                if n == 0:
                    V.scalar_tensor_tensor(d, d, 1 / 8, spread(vec[:, g:g + 64], 1, 16), ALU.mult, ALU.mult)
                else:
                    V.tensor_tensor(d, d, spread(vec[:, g:g + 64], 1, 16), ALU.mult)
            V.memset(QA[:, :, :, 65:66], 1.0)
            V.memset(KA[:, :, :, 64:65], 1.0)
            dve.wait_ge(sem("stat_rs"), 4)
            rs4 = RS[:, 7:8]
            project(B_KV, KV[:, 1, 0:NCOL], rs4)
            dve.wait_ge(sem("fox_fc"), 1)
            fc = M[0][:, 0:16].rearrange("p (t h) -> p t h", t=2)
            V.tensor_copy(QA[:, :, :, 64], fc)
            V.tensor_scalar(KA[:, :, :, 65], fc, -1.0, None, ALU.mult).then_inc(sem("fox_aug"), 1)
            begin(B_KV + 1)
            dve.wait_ge(sem("rg_tanh"), 1)
            link(V.scalar_tensor_tensor(TG, TG, 1.0, P2R[:, :, RG:RG + NCOL], ALU.add, ALU.mult))
            for t in range(NT):
                ins = V.scalar_tensor_tensor(TG[:, t], TG[:, t], 0.5, vec2[:, 0:NCOL], ALU.mult, ALU.mult)
            link(ins)
            dve.wait_ge(sem("ret_rs"), 1)
            for t in range(NT):
                ins = V.tensor_tensor(ret[t], ret[t], spread(RSTD[:, 8 * t:8 * t + 8], 2, 64), ALU.mult)
            link(ins)
            sig(V.tensor_tensor(MG2[:, :, 0:NCOL], MG2[:, :, 0:NCOL], TG, ALU.mult), "ret_done")
            project(B_KV + 1, KV[:, 1, NCOL:D], rs4)
            for e in range(1, 8, 2):
                dve.wait_ge(sem("foxT_pe"), e + 1)
                dst = (qaT if e < 4 else kaT)[0:66, 2 * (e % 4):2 * (e % 4) + 2, :]
                V.tensor_copy(dst, M[e % 4][0:66, :].rearrange("p (a b) -> p a b", a=2)).then_inc(sem("foxT_dve"), 1)
            begin(B_KV + 2)
            for k in attention(WORK_A, 1.0, 64, fox_mask, LM2, PTS2,
                               lambda t, hs: MG2[:, t, NCOL + 64 * hs[0]:NCOL + 64 * hs[-1] + 64].rearrange("p (a b) -> p a b", b=64)):
                if k == 1:
                    project(B_KV + 2, KV[:, 1, D:D + NCOL], rs4)
                    begin(B_KV + 3)
                if k == 5:
                    project(B_KV + 3, KV[:, 1, D + NCOL:2 * D], rs4)
                    begin(B_O2)
            turn_lo()
            dve.wait_ge(sem("x_sqk"), 1)
            link(V.tensor_reduce(SSX, SQX.rearrange("p t (h d) -> p (t h) d", d=256), AX_X, ALU.add))
            V.tensor_scalar(SSX, SSX, 1 / 256, EPS, ALU.mult, ALU.add).then_inc(sem("x_ms"), 1)
            residual(B_O2, 0)
            begin(B_O2 + 1)
            residual(B_O2 + 1, 1)
            turn_lo(NORMS["xattn"])

            def heads_norm(v, n, gain, name):
                dve.wait_ge(sem("x_rn"), n + 1)
                for t in range(NT):
                    a = v[:, t, 0:D].rearrange("p (h d) -> p h d", d=256)
                    ins = V.tensor_tensor(a, a, spread(RNX[:, 8 * n + 4 * t:][:, 0:4], 2, 256), ALU.mult)
                link(ins)
                for t in range(NT):
                    a = v[:, t, 0:D].rearrange("p (h d) -> p h d", d=256)
                    ins = V.tensor_tensor(a, a, spread(gain, 1, 4), ALU.mult)
                ins.then_inc(sem(name), 1)

            mean_squares(4)
            heads_norm(KV, 0, vec2[:, NCOL:NCOL + 256], "x_k")
            dve.wait_ge(sem("stat_rs"), 5)
            for k in range(2):
                begin(B_XQ + k)
                project(B_XQ + k, XQ[:, 1, NCOL * k:NCOL * k + NCOL], RS[:, 9:10])
            for e in range(1, 8, 2):
                if e == 5:
                    dve.wait_ge(sem("x_sqq"), 1)
                    link(V.tensor_reduce(SSX, SQX.rearrange("p t (h d) -> p (t h) d", d=256), AX_X, ALU.add))
                    V.tensor_scalar(SSX, SSX, 1 / 256, EPS, ALU.mult, ALU.add).then_inc(sem("x_ms"), 1)
                    dve.wait_ge(sem("ev0"), B_XO)
                    heads_norm(XQ, 1, vec[:, V_XQ:V_XQ + 256], "x_q")
                dve.wait_ge(sem("xT_pe"), e + 1)
                dst = (xkT if e < 4 else xqT)[:, 2 * (e % 4):2 * (e % 4) + 2, :]
                V.tensor_copy(dst, M[e % 4].rearrange("p (a b) -> p a b", a=2)).then_inc(sem("xT_dve"), 1)
            for k in attention(WORK_X, 1 / 16, 256, None, None, PTS2,
                               lambda t, hs: XO[:, t, 256 * hs[0]:256 * hs[-1] + 256].rearrange("p (a b) -> p a b", b=256)):
                pass
            turn_lo()
            for j in range(2):
                begin(B_XO + j)
                residual(B_XO + j, j)
            turn_lo(NORMS["ffn"])
            mean_squares(5)
            dve.wait_ge(sem("stat_rs"), 6)
            link(V.tensor_scalar(RS5H, RS[:, 10:12], 0.5, None, ALU.mult))
            V.tensor_tensor(RS5Q, RS5H, RS[:, 10:12], ALU.mult).then_inc(sem("rs5"), 1)

            def gate_mul(p, i=None):
                b = B_GU + 2 * p
                n = blocks[b]["n"]
                for t in range(NT):
                    dve.wait_ge(sem("gate_tanh"), at(2 * p + t + 1, 2, i))
                    V.scalar_tensor_tensor(sg2[:, 1, t, 0:n], sg2[:, 0, t, 0:n], 1.0, G[b % 2][t][:, 0:n], ALU.add, ALU.mult).then_inc(sem(f"ev{t}"), 1)

            def up_mul(p, i=None):
                b = B_GU + 2 * p + 1
                n = blocks[b]["n"]
                mm_finished(b, i)
                for t in range(NT):
                    dve.wait_ge(sem(f"ev{t}"), at(b, 2, i))
                    if i is not None or p > 0:
                        dve.wait_ge(sem("hid2_pe"), at(2 * p, 2, i))
                    V.tensor_tensor(hid2[:, 0, t, 0:n], sg2[:, 1, t, 0:n], G[b % 2][t][:, 0:n], ALU.mult).then_inc(sem(f"ev{t}"), 1)

            def hidden2_lo(p, i=None, q_n=2):
                for q in range(q_n):
                    dve.wait_ge(sem("hid2_hi"), at(2 * p + q + 1, 2, i))
                    kk = bass.ds(at(4 * p + 2 * q, 4, i), 2)
                    V.tensor_tensor(h2_lo[:, kk, :], M[q].rearrange("p (a b) -> p a b", a=2), h2_hi[:, kk, :].bitcast(F32), ALU.subtract)\
                        .then_inc(sem("hid2_lo"), 1)

            begin(B_GU)
            gate_mul(0)
            begin(B_GU + 1)
            up_mul(0)
            with dve.Fori(0, 3) as i:
                begin(B_GU + 2, i)
                gate_mul(1, i)
                begin(B_GU + 3, i)
                hidden2_lo(0, i)
                up_mul(1, i)
            begin(B_GU + 8)
            gate_mul(4)
            begin(B_GU + 9)
            hidden2_lo(3)
            up_mul(4)
            begin(B_GU + 10)
            gate_mul(5)
            hidden2_lo(4)
            begin(B_GU + 11)
            up_mul(5)
            hidden2_lo(5, q_n=1)
            begin(B_D2)
            residual(B_D2, 0)
            begin(B_D2 + 1)
            residual(B_D2 + 1, 1, last=True)

        @block.gpsimd
        def _(pool):
            def split(b, c):
                n = blocks[b]["chunk0"] + c
                kn, width = chunk_shape(b, c)
                pool.wait_ge(sem("split_hi"), n + 1)
                s = n % SLOTS
                pool.tensor_tensor(w_lo[:, s, 0:kn, 0:width], raw[:, s, 0:kn, 0:width], w_hi[:, s, 0:kn, 0:width].bitcast(F32), ALU.subtract)\
                    .then_inc(sem("split_lo_pool"), 1)

            def power(dst, src, n, wait, value, name):
                pool.wait_ge(sem(wait), value)
                pool.tensor_tensor(dst, src, MHALF[:, 0:n], ALU.pow).then_inc(sem(name), 1)

            for n, g in enumerate((norm_mlp_g, g_mix_2, g_xattn_2, g_mem_2, g_ffn_2)):
                pool.dma_start(hidden_rows[8 * n + 8:8 * n + 16, :], g[0].rearrange("(k p) -> k p", p=P)).then_inc(sem("rows_in"), 16)
            pool.dma_start(conv_rows[0:96, :], conv_w[0].rearrange("j (k p) -> (j k) p", p=P)).then_inc(sem("rows_in"), 16)
            for dst, src in ((vec[:, V_QG:V_QG + P], q_norm_g[0]), (vec[:, V_KG:V_KG + P], k_norm_g[0]), (vec[:, V_GN:V_GN + P], gdn_norm_g[0]),
                             (vec[:, V_DT:V_DT + 8], dt_bias[0]), (vec[:, V_AL:V_AL + 8], a_log[0]), (vec[:, V_BF:V_BF + 8], b_forget_2[0]),
                             (vec[:, V_FQ:V_FQ + 64], g_fox_q_2[0]), (vec[:, V_FK:V_FK + 64], g_fox_k_2[0]),
                             (vec[:, V_XQ:V_XQ + 256], g_xq_2[0]), (vec2[:, NCOL:NCOL + 256], g_xk_2[0]),
                             (vec2[:, 0:NCOL], g_ret_out_2[0].rearrange("h d -> (h d)"))):
                pool.dma_start(dst, src.partition_broadcast(P)).then_inc(sem("vec_in"), 16)
            pool.memset(MHALF, -0.5).then_inc(sem("pool_half"), 1)
            pool.wait_ge(sem("pool_half"), 1)

            def norm_power(k):
                power(RS[:, 2 * k:2 * k + 2], RS[:, 2 * k:2 * k + 2], 2, "stat_ms", k + 1, "stat_rs")

            norm_power(0)
            pool.wait_ge(sem("consts_in"), 16)
            pool.wait_ge(sem("ev0"), 5)
            pool.wait_ge(sem("ev1"), 5)
            idx = PA[:, :, IQ:IW].rearrange("p t (h d) -> p t h d", d=64)
            ci, si = (spread(cst[:, C_ROPE_I + 16 * k:C_ROPE_I + 16 * k + 16].rearrange("p (t d) -> p t d", t=2), 2, 9) for k in range(2))
            x1, x2 = idx[:, :, :, 0:8], idx[:, :, :, 8:16]
            pr = [RTI[:, k].rearrange("p (t h d) -> p t h d", t=2, h=9) for k in range(4)]
            for n, (a, f) in enumerate(((x1, ci), (x2, si), (x2, ci), (x1, si))):
                for t in range(NT):
                    ins = pool.tensor_tensor(pr[n][:, t], a[:, t], f[:, t], ALU.mult)
            ins.then_inc(sem("pool_step"), 1)
            pool.wait_ge(sem("pool_step"), 1)
            for t in range(NT):
                pool.tensor_tensor(x1[:, t], pr[0][:, t], pr[1][:, t], ALU.subtract)
                ins = pool.tensor_tensor(x2[:, t], pr[2][:, t], pr[3][:, t], ALU.add)
            ins.then_inc(sem("pool_step"), 1)
            pool.wait_ge(sem("pool_step"), 2)
            for n in range(2):
                ins = pool.tensor_copy(IKD[:, :, n, :], PA[:, :, IK:IW])
            ins.then_inc(sem("idx_rot"), 1)
            power(RNA, SSA, 20, "att_ms", 1, "att_rn")
            for b in range(B_Q + 2, B_GB + 2):
                split(b, 1)
            pool.wait_ge(sem("gdn_g"), 1)
            pool.wait_ge(sem("att_norm"), 6)
            pool.tensor_tensor(GU, spread(GA_, 2, P), spread(cst[:, C_CUM:C_CUM + P], 1, 16), ALU.mult).then_inc(sem("gdn_gu"), 1)
            for b in (B_Z, B_Z + 1):
                split(b, 1)
            power(RQK, SSK, 32, "gdn_ms", 1, "gdn_rq")
            pool.wait_ge(sem("gdn_y"), 12)
            pool.wait_ge(sem("gdn_kdf"), 1)
            pool.tensor_tensor(KD, KN[:, 0], spread(KDF, 2, P), ALU.mult).then_inc(sem("gdn_kd"), 1)
            pool.wait_ge(sem("gdn_kb"), 2)
            pool.tensor_tensor(KBG, KB[:, 1], spread(EG[:, 8:16], 2, P), ALU.mult).then_inc(sem("gdn_kbg"), 1)
            for lv in range(LEVELS):
                for u in range(4):
                    if lv == 0:
                        pool.wait_ge(sem("gdn_kk"), 4)
                        pool.wait_ge(sem("gdn_at"), u + 1)
                    else:
                        pool.wait_ge(sem("inv_p"), 4 * (lv - 1) + u + 1)
                        if lv == 1:
                            pool.wait_ge(sem("inv_x"), u + 1)
                    n = slice(4 * u, 4 * u + 4)
                    pool.tensor_tensor(LT[:, n, :], AT[:, n, :], spread(cst[:, C_LEV + P * lv:C_LEV + P * lv + P], 1, 4), ALU.mult).then_inc(sem("inv_lt"), 1)
            for t in range(NT):
                power(RSO[:, 8 * t:8 * t + 8], SSO[:, 8 * t:8 * t + 8], 8, "o_ms", t + 1, "o_rs")
            norm_power(1)
            norm_power(2)
            power(RNF, SSF, 32, "fox_ms", 1, "fox_rn")
            norm_power(3)
            power(RSTD, VAR, 16, "ret_ms", 1, "ret_rs")
            power(RNX[:, 0:8], SSX, 8, "x_ms", 1, "x_rn")
            norm_power(4)
            power(RNX[:, 8:16], SSX, 8, "x_ms", 2, "x_rn")
            norm_power(5)
            split(B_D2, 1)


_INS = ['x', 'norm_mix_g', 'w_in', 'conv_w', 'a_log', 'dt_bias', 'gdn_norm_g', 'q_norm_g', 'k_norm_g', 'w_out', 'norm_mlp_g',
        'w_mlp_up', 'w_mlp_down', 'mem_2', 'g_mix_2', 'w_in_2', 'b_forget_2', 'g_ret_out_2', 'g_fox_q_2', 'g_fox_k_2', 'w_out_2',
        'g_xattn_2', 'w_xq_2', 'w_xkv_2', 'g_mem_2', 'g_xq_2', 'g_xk_2', 'w_xo_2', 'g_ffn_2', 'w_gate_2', 'w_up_2', 'w_down_2']


def kernel(**inputs):
    import numpy as _np
    import concourse.bacc as _bacc
    from concourse import mybir as _mybir
    from concourse.bass_utils import run_bass_kernel_spmd as _run

    nc = _bacc.Bacc("TRN2", target_bir_lowering=False, num_devices=1)
    arrays, args = {}, []
    given = [(name, _np.ascontiguousarray(inputs[name])) for name in _INS]
    given += [("constants", constants()), ("retention", retention_weights())]
    for name, a in given:
        arrays[f"in_{name}_dram"] = a
        args.append(nc.dram_tensor(f"in_{name}_dram", a.shape, _mybir.dt.from_np(a.dtype), kind="ExternalInput").ap())
    args.append(nc.dram_tensor("out_0_dram", (1, SEQ, D), _mybir.dt.float32, kind="ExternalOutput").ap())
    build(nc, *args)
    r = _run(nc, [arrays], core_ids=[0])
    return r.results[0]["out_0_dram"]
```

```python
from contextlib import ExitStack

import concourse.bass as bass
from concourse import mybir

F32 = mybir.dt.float32
F32R = mybir.dt.float32r
ALU = mybir.AluOpType
ACT = mybir.ActivationFunctionType
AX_X = mybir.AxisListType.X

P = 128
SEQ = 256
NT = SEQ // P
D = 1024
KT = D // P
EPS = 1e-6
NCOL = 512
CK = 4
SLOTS = 4
DFF = 4096
DFF2 = 2816
MEMORIES = 256

A0 = 4096
A_W = 2136
AQ, AK, AV, IQ, IK, IW = 16, 1040, 1296, 1552, 2064, 2128
RQ, RK, RV, RG, FQ, FK, FV, FG = 0, 512, 1024, 1536, 2048, 2560, 3072, 3584
W2 = 3592

EXCLUDED = -1e30
UNREACHED = -3.0e38
TAKEN = -3.4e38
BETWEEN = -3.2e38

C_ID, C_ONES, C_CUM, C_ZERO, C_TRI, C_TRIX, C_NEG, C_LEV = 0, 128, 256, 384, 512, 640, 768, 896
LEVELS = 7
C_ROPE_A = C_LEV + LEVELS * P
C_ROPE_I = C_ROPE_A + 64
C_ROPE_R = C_ROPE_I + 32
C_EVEN = C_ROPE_R + 128
C_N = C_EVEN + LEVELS

WORK_A = [(0, range(0, 4)), (0, range(4, 8))] + [(1, range(h, h + 2)) for h in range(0, 8, 2)]
WORK_X = [(t, range(h, h + 2)) for t in range(NT) for h in (0, 2)]


def keys_of(work, k):
    return NCOL // len(work[k][1])


def constants():
    import numpy as np

    c = np.zeros((P, C_N), np.float32)
    row, col = np.arange(P)[:, None], np.arange(P)[None, :]
    c[:, C_ID:C_ID + P] = row == col
    c[:, C_ONES:C_ONES + P] = 1
    c[:, C_CUM:C_CUM + P] = row <= col
    c[:, C_TRI:C_TRI + P] = np.where(col <= row, 0, EXCLUDED)
    c[:, C_TRIX:C_TRIX + P] = np.where(col <= row, 0, UNREACHED)
    c[:, C_NEG:C_NEG + P] = np.where(col >= row, 0, EXCLUDED)
    for n in range(LEVELS):
        h = 1 << n
        c[:, C_LEV + P * n:C_LEV + P * n + P] = (row // (2 * h) == col // (2 * h)) & (row // h % 2 == 0) & (col // h % 2 == 1)
        c[:, C_EVEN + n:C_EVEN + n + 1] = -(row // h % 2 == 0).astype(np.float32)

    def rope(at, half, rot, theta):
        inv = np.float32(theta) ** (-np.arange(0, rot, 2, dtype=np.float32) / np.float32(rot))
        ang = np.arange(SEQ, dtype=np.float32)[:, None] * inv.astype(np.float32)[None, :]
        for t in range(NT):
            a = ang[P * t:P * t + P].astype(np.float64)
            c[:, at + t * half:at + t * half + half] = np.cos(a)
            c[:, at + (NT + t) * half:at + (NT + t) * half + half] = np.sin(a)

    rope(C_ROPE_A, 16, 32, 500000.0)
    rope(C_ROPE_I, 8, 16, 500000.0)
    rope(C_ROPE_R, 32, 64, 10000.0)
    return c


def retention_weights():
    import numpy as np

    w = np.zeros((P, 8 * 384), np.float32)
    s, t = np.arange(SEQ)[:, None], np.arange(SEQ)[None, :]
    for h in range(8):
        gamma = 1.0 - 2.0 ** (-5.0 - h)
        full = np.where(s // 64 <= t // 64, gamma ** np.abs(t - s), 0) / 8
        p, q = h % 2, h // 2
        w[:, 512 * (2 * p + q // 2) + 256 * (q % 2):][:, :256] = full[:P]
        w[:, 2048 + 512 * p + 128 * q:][:, :128] = full[P:, P:]
    return w


def build(nc, x_in, norm_mix_g, w_in, conv_w, a_log, dt_bias, gdn_norm_g, q_norm_g, k_norm_g, w_out,
          norm_mlp_g, w_mlp_up, w_mlp_down, mem_2, g_mix_2, w_in_2, b_forget_2, g_ret_out_2,
          g_fox_q_2, g_fox_k_2, w_out_2, g_xattn_2, w_xq_2, w_xkv_2, g_mem_2, g_xq_2, g_xk_2, w_xo_2,
          g_ffn_2, w_gate_2, w_up_2, w_down_2, consts, ret_w, out):
    ctx = ExitStack()
    with ctx:
        def sb(name, shape, dt=F32, stack=None):
            return (stack or ctx).enter_context(nc.sbuf_tensor(name, shape, dt))

        named = {}

        def sem(name):
            if name not in named:
                named[name] = ctx.enter_context(nc.semaphore(name))
            return named[name]

        blocks = []

        def segment(name, w, first, widths, kt=KT):
            start = len(blocks)
            for width in widths:
                chunk0 = blocks[-1]["chunk0"] + blocks[-1]["chunks"] if blocks else 0
                blocks.append(dict(seg=name, w=w, col=first, n=width, kt=kt, chunk0=chunk0, chunks=-(-kt // CK)))
                first += width
            return start

        win = w_in[0]
        B_A = segment("a", win, A0, [512] * 3 + [300] * 2)
        B_Q = segment("qkv", win, 0, [512] * 6)
        B_GB = segment("gate_b", win, 7256, [512] * 2)
        B_Z = segment("z", win, 3072, [512] * 2)
        B_GA = segment("gate_a", win, 6232, [512] * 2)
        B_O = segment("out", w_out[0], 0, [512] * 2)
        B_UP = segment("up", w_mlp_up[0], 0, [512] * 8)
        B_DN = segment("down", w_mlp_down[0], 0, [512] * 2, kt=DFF // P)
        B_2 = segment("in2", w_in_2[0], 0, [512] * 6 + [260] * 2)
        B_KV = segment("kv", w_xkv_2[0], 0, [512] * 4)
        B_O2 = segment("out2", w_out_2[0], 0, [512] * 2)
        B_XQ = segment("xq", w_xq_2[0], 0, [512] * 2)
        B_XO = segment("xo", w_xo_2[0], 0, [512] * 2)
        B_GU = len(blocks)
        for c in range(0, DFF2, 512):
            n = min(512, DFF2 - c)
            segment("gate2", w_gate_2[0], c, [n])
            segment("up2", w_up_2[0], c, [n])
        B_D2 = segment("down2", w_down_2[0], 0, [512] * 2, kt=DFF2 // P)
        B_END = len(blocks)
        EARLY = [B_O + 1, B_DN + 1, B_O2 + 1, B_XO + 1, B_D2 + 1]

        V_QG, V_KG, V_GN, V_DT, V_AL, V_BF, V_FQ, V_FK, V_XQ, V_XK, V_RO = 0, 128, 256, 384, 392, 400, 408, 472, 536, 792, 1048
        V_N = V_RO + NCOL
        with nc.sbuf_tensor("raw", [P, SLOTS, CK, NCOL], F32) as raw:
            pass
        w_lo = sb("w_lo", [P, SLOTS, CK, NCOL], F32R)
        w_hi = sb("w_hi", [P, SLOTS, CK, NCOL], F32R)
        s_hi = sb("s_hi", [P, KT, SEQ], F32R)
        s_lo = sb("s_lo", [P, KT, SEQ], F32R)
        x = sb("x", [P, NT, D])
        cst = sb("cst", [P, C_N])
        gains = sb("gains", [P, 6, KT])
        cw = sb("cw", [P, 4, 24])
        vec = sb("vec", [P, V_N])
        sm = sb("sm", [P, 640])
        ident = cst[:, C_ID:C_ID + P]
        junk = sb("junk", [P, D], mybir.dt.bfloat16)

        G = [[ctx.enter_context(nc.psum_tensor(f"gemm{s}{t}", [P, NCOL], F32)) for t in range(NT)] for s in range(2)]
        M = [ctx.enter_context(nc.psum_tensor(f"mixbank{i}", [P, NCOL], F32)) for i in range(4)]

        NORMS = dict(mix=0, mlp=1, mix2=2, xattn=3, mem=4, ffn=5)

        MIXER = 24800
        a1 = ExitStack()
        ar = sb("mix1", [P, MIXER], F32, a1)
        a1.close()
        a2 = ExitStack()
        hT_hi = sb("hT_hi", [P, DFF // P, SEQ], F32R, a2)
        hT_lo = sb("hT_lo", [P, DFF // P, SEQ], F32R, a2)
        hid = sb("hid", [P, 2, NT, NCOL], F32, a2)
        a2.close()
        a3 = ExitStack()
        ar2 = sb("mix2", [P, MIXER], F32, a3)
        a3.close()
        a4 = ExitStack()
        h2_hi = sb("h2_hi", [P, DFF2 // P, SEQ], F32R, a4)
        h2_lo = sb("h2_lo", [P, DFF2 // P, SEQ], F32R, a4)
        hid2 = sb("hid2", [P, NT, NCOL], F32, a4)
        sg2 = sb("sg2", [P, 2, NT, NCOL], F32, a4)
        a4.close()

        def view(base, at, *shape):
            n = 1
            for s in shape:
                n *= s
            v = base[:, at:at + n]
            if len(shape) == 1:
                return v
            names = "abcd"[:len(shape)]
            return v.rearrange(f"p ({' '.join(names)}) -> p {' '.join(names)}", **dict(zip(names, shape)))

        def spread(ap, axis, n):
            v = ap.unsqueeze(axis)
            shape = list(v.shape)
            shape[axis] = n
            return v.to_broadcast(shape)

        PA = view(ar, 0, NT, A_W)
        PQ = view(ar, 4272, NT, 3072)
        ZG = view(ar, 10416, NT, D)
        OA = view(ar, 12464, NT, 8, 128)
        TMP = view(ar, 14512, 2, NCOL)
        YT = view(ar, 15536, 24, SEQ)
        CT = view(ar, 21680, 2, 2, SEQ)
        hidden_rows, conv_rows = ar[:, 4272:4400], ar[:, 4400:4528]
        SQ = view(ar, 15536, NT, 10, 128)
        qT = view(ar, 15536, 8, SEQ)
        kT = view(ar, 17584, 2, SEQ)
        iqT = view(ar, 18096, 4, SEQ)
        ikT = view(ar, 19120, SEQ)
        IKD = view(ar, 19376, NT, 2, 64)
        SC = view(ar, 19632, NT, SEQ)
        BIAS = view(ar, 20144, NT, SEQ)
        RT = view(ar, 20656, 4, NT * 160)
        RTI = view(ar, 21936, 4, NT * 72)
        RL = view(ar, 22512, 8, SEQ)
        LM = view(ar, 20656, 2, NCOL)
        PTS = view(ar, 22512, 2, NCOL)
        GU = view(ar, 0, 16, P)
        DM = view(ar, 2048, 16, P)
        KN = view(ar, 4272, NT, 8, P)
        VB = view(ar, 6320, NT, 8, P)
        KB = view(ar, 8368, NT, 8, P)
        KBT = view(ar, 19632, 8, SEQ)
        KD = view(ar, 21680, 8, P)
        KBG = view(ar, 22704, 8, P)
        AT = view(ar, 0, 16, P)
        QK = view(ar, 4272, 16, P)
        LT = view(ar, 19632, 16, P)
        XT = view(ar, 17584, 16, P)
        XI = view(ar, 8368, 16, P)
        PS = view(ar, 2048, 16, P)
        WT = view(ar, 19632, 8, P)
        UV = view(ar, 2048, NT, 8, P)
        ST = view(ar, 0, 8, P)
        O1 = view(ar, 8368, NT, 8, P)

        def st(at, n):
            return sm[:, at:at + n]

        SS, RS = st(0, 12), st(12, 12)
        HRS, QRS = st(24, 2), st(26, 2)
        SSA, RNA = st(28, 20), st(48, 20)
        IWS = st(68, 16)
        MX8 = st(84, 16)
        NEGM, SUMS, RSUM = st(100, 32), st(132, 32), st(164, 32)
        GA_, BT, HBT = st(196, 16), st(212, 16), st(516, 16)
        SP = st(228, 48)
        GC = st(276, 32)
        EG, ED = st(340, 16), st(356, 16)
        KDF, BRK = st(372, 8), st(404, 16)
        SSK, RQK = st(420, 32), st(452, 32)
        SSO, RSO = st(484, 16), st(500, 16)
        FSQ, FQ = SP[:, 0:16], SP[:, 16:32]
        MHALF = st(540, 64)
        FL = st(608, 16).rearrange("p (t h) -> p t h", t=2)
        SSF, RNF = SSK, RQK
        SSX, RNX = st(28, 8), st(48, 16)
        XSC = st(68, 8)
        MU, VAR, RSTD = GA_, BT, EG
        RS5H, RS5Q = st(624, 2), st(626, 2)

        P2R = view(ar2, 0, NT, 2048)
        P2F = view(ar2, 4096, NT, W2 - 2048)
        WR = view(ar2, 7184, 3072)
        MG2 = view(ar2, 10256, NT, D)
        MEM = view(ar2, 12304, NT, D)
        T0 = 14352
        RT2 = view(ar2, T0, 4, NT * 512)
        rqT = view(ar2, T0, 4, SEQ)
        rkT = view(ar2, T0 + 1024, 4, SEQ)
        PT2 = view(ar2, T0 + 2048, 3072)
        RSQ = view(ar2, T0 + 1024, NT, NCOL)
        TG = view(ar2, 23632, NT, NCOL)
        SQR = view(ar2, 21584, NT, 16, 64)
        QA = view(ar2, 19472, NT, 8, 66)
        KA = view(ar2, 20528, NT, 8, 66)
        qaT = view(ar2, T0, 8, SEQ)
        kaT = view(ar2, T0 + 2048, 8, SEQ)
        LM2 = view(ar2, 21584, 2, NCOL)
        PTS2 = view(ar2, 22608, 2, NCOL)
        KV = view(ar2, 0, NT, 2048)
        XQ = view(ar2, 7184, NT, D)
        XO = view(ar2, 10256, NT, D)
        SQX = view(ar2, T0 + 5120, NT, D)
        xqT = view(ar2, T0, 8, SEQ)
        xkT = view(ar2, T0 + 2048, 8, SEQ)

        block = ctx.enter_context(nc.Block())

        def at(base, step, i):
            return base if i is None else base + step * i

        def chunk_shape(b, c):
            return min(CK, blocks[b]["kt"] - CK * c), blocks[b]["n"]

        BY_POOL = {(b, 1) for b in range(B_Q + 2, B_Z + 2)} | {(b, 0) for b in range(B_GB + 1, B_Z + 2)} | {(B_D2, 1)}

        assert all(c < blocks[b]["chunks"] for b, c in BY_POOL)

        def block_columns(b):
            first = blocks[b]["col"] - (A0 if blocks[b]["seg"] == "a" else 2048)
            return slice(first, first + blocks[b]["n"])

        def pool_chunk(b, c):
            return (b, c) in BY_POOL

        def low_parts(b, c):
            mine = pool_chunk(b, c)
            return sum(pool_chunk(e, d) == mine for e in range(b + 1) for d in range(blocks[e]["chunks"]) if (e, d) <= (b, c))

        def blocks_of(v, lv, odd):
            if len(v.shape) == 2:
                return v.rearrange("p (m two h) -> p m two h", two=2, h=1 << lv)[:, :, odd, :]
            return v.rearrange("p a (m two h) -> p a m two h", two=2, h=1 << lv)[:, :, :, odd, :]

        def half_bank(bank, lv):
            return bank[:, 0:SEQ].rearrange("p (a m h) -> p a m h", a=4, h=1 << lv)

        def fox_mask(t):
            return cst[:, C_TRI - P * t:C_TRI + P]

        @block.sync
        def _(sp):
            def load(b, c, i=None):
                n = blocks[b]["chunk0"] + c
                kn, width = chunk_shape(b, c)
                slot = n % SLOTS
                if n >= SLOTS:
                    sp.wait_ge(sem("mm_done"), at(n - SLOTS + 1, 4, i))
                rows = blocks[b]["w"][CK * P * c:CK * P * c + kn * P]
                src = rows[:, bass.ds(at(blocks[b]["col"], 2 * NCOL, i), width)]
                sp.dma_start(raw[:, slot, 0:kn, 0:width], src.rearrange("(k p) n -> p k n", p=P))\
                    .then_inc(sem(f"loaded{slot}"), 16)

            load(0, 0)
            for c in range(2):
                cols = slice(NCOL * c, NCOL * c + NCOL)
                sp.dma_start(x[:, :, cols], x_in[0].rearrange("(t p) d -> p t d", p=P)[:, :, cols]).then_inc(sem(f"x_in{c}"), 16)
            b = 0
            while b < B_END:
                pairs = 0
                while (b >= 2 and b + 2 * pairs + 1 < B_END
                       and all(blocks[b + 2 * pairs + j]["seg"] == blocks[b]["seg"] and blocks[b + 2 * pairs + j]["n"] == NCOL
                               and blocks[b + 2 * pairs + j]["chunks"] == 2 for j in range(2))):
                    pairs += 1
                if pairs >= 2:
                    with sp.Fori(0, pairs) as i:
                        for j in range(2):
                            for c in range(2):
                                load(b + j, c, i)
                    b += 2 * pairs
                else:
                    for c in range(1 if b == 0 else 0, blocks[b]["chunks"]):
                        load(b, c)
                    b += 1
            for t in range(NT):
                sp.wait_ge(sem("x_final"), t + 1)
                sp.dma_start(out[0, P * t:P * t + P, :], x[:, t, :]).then_inc(sem("stored"), 16)
            sp.wait_ge(sem("stored"), 16 * NT)

        @block.tensor
        def _(pe):
            act_w = (s_hi, s_lo)

            def mm(b, i=None, stat=act_w, turned=None, hidden=None, quarters=None):
                blk = blocks[b]
                pairs = range(blk["kt"] // 2) if quarters is None else quarters
                if b >= 2 and pairs[0] == 0:
                    pe.wait_ge(sem("ev0"), at(b - 1, 2, i))
                    pe.wait_ge(sem("ev1"), at(b - 1, 2, i))
                for pair in pairs:
                    c = 2 * pair // CK
                    n = blk["chunk0"] + c
                    kn, width = chunk_shape(b, c)
                    if 2 * pair == CK * c:
                        pe.wait_ge(sem("split_lo_pool" if pool_chunk(b, c) else "split_lo"), at(low_parts(b, c), 4, i))
                    if turned is not None:
                        pe.wait_ge(sem("turn_lo"), turned - KT // 2 + pair + 1)
                    if hidden is not None:
                        pe.wait_ge(sem(hidden), pair + 1)
                    early = b in EARLY and 2 * pair == blk["kt"] - 2
                    tiles = [(kt, t) for kt in (2 * pair, 2 * pair + 1) for t in range(NT)]
                    for kt, t in sorted(tiles, key=lambda tile: tile[1]) if early else tiles:
                        o = G[b % 2][t][:, 0:width]
                        hi, lo = (s[:, kt, P * t:P * t + P] for s in stat)
                        wh, wl = (s[:, n % SLOTS, kt - CK * c, 0:width] for s in (w_hi, w_lo))
                        nc.tensor.matmul(o, hi, wh, start=kt == 0, stop=False)
                        nc.tensor.matmul(o, hi, wl, start=False, stop=False)
                        last = nc.tensor.matmul(o, lo, wh, start=False, stop=kt == blk["kt"] - 1)
                        if early and t == 0 and kt == blk["kt"] - 1:
                            last.then_inc(sem("first_tile"), 1)
                    if kt == CK * c + kn - 1:
                        last.then_inc(sem("mm_done"), 1)

            def turn(src, waits, banks=range(4)):
                for q in banks:
                    for s, v in waits(q):
                        pe.wait_ge(sem(s), v)
                    for kk in range(2):
                        for t in range(NT):
                            last = nc.tensor.transpose(M[q][:, (2 * kk + t) * P:(2 * kk + t + 1) * P], src(2 * q + kk, t), ident)
                    last.then_inc(sem("turn_pe"), 1)

            def xtile(kt, t):
                return x[:, t, P * kt:P * kt + P]

            pe.wait_ge(sem("ident_in"), 32)
            nc.tensor.transpose(M[0][:, 0:8], hidden_rows[0:8, :], ident[0:8, 0:8]).then_inc(sem("vec_pe"), 1)
            turn(xtile, lambda q: [(f"x_in{q // 2}", 16), ("vec_dve", 1)])
            mm(B_A, turned=4)
            pe.wait_ge(sem("rows_in"), 16 * 6)
            nc.tensor.transpose(M[0][:, 0:48], hidden_rows[0:48, :], ident[0:48, 0:48])
            nc.tensor.transpose(M[0][:, 128:224], conv_rows[0:96, :], ident[0:96, 0:96]).then_inc(sem("vec_pe"), 1)
            for k in range(1, 5):
                mm(B_A + k)
            mm(B_Q)

            def operands(banks):
                for e in banks:
                    if e >= 3:
                        pe.wait_ge(sem("relu"), 6)
                    if e >= 7:
                        pe.wait_ge(sem("attT_act"), 4)
                    o = M[e % 4]
                    for j in range(1 if e == 2 else 2):
                        for t in range(NT):
                            if e == 2:
                                src = IKD[:, t].rearrange("p a b -> p (a b)")
                            else:
                                c = IQ + P * (2 * e + j) if e < 2 else (AK + P * j if e == 3 else AQ + P * (2 * (e - 4) + j))
                                src = PA[:, t, c:c + P]
                            last = nc.tensor.transpose(o[:, (2 * j + t) * P:(2 * j + t + 1) * P], src, ident)
                    last.then_inc(sem("attT_pe"), 1)

            pe.wait_ge(sem("idx_rot"), 1)
            operands(range(3))
            mm(B_Q + 1)

            pe.wait_ge(sem("attT_act"), 3)
            for t in range(NT):
                for par in (0, 1) if t == 0 else (1, 0):
                    for q in range(4):
                        bank = par if t == 0 else 2 * par + q // 2
                        if t == 1 and par == 0 and q % 2 == 0:
                            pe.wait_ge(sem("relu"), 2)
                        ns = P * (t + 1)
                        o = M[bank][:, (q % (4 // (t + 1))) * ns:][:, 0:ns]
                        last = nc.tensor.matmul(o, iqT[64 * par:64 * par + 64, q, P * t:P * t + P],
                                                ikT[64 * par:64 * par + 64, 0:ns], start=True, stop=True)
                        if q == 3 or (t == 1 and q == 1):
                            last.then_inc(sem("scores"), 1)
            mm(B_Q + 2)
            pe.wait_ge(sem("att_rot"), 1)
            operands(range(3, 8))
            mm(B_Q + 3)
            mm(B_Q + 4)
            pe.wait_ge(sem("attT_act"), 6)
            pe.wait_ge(sem("attT_dve"), 2)

            groups = [0]

            def attention(work, queries, keys, values, width, exps, exps_turned):
                g0, n = groups[0], len(work)

                def logits(k):
                    t, heads = work[k]
                    ns = keys_of(work, k)
                    g = g0 + k
                    if k >= 2:
                        pe.wait_ge(sem("att_max"), g - 1)
                        pe.wait_ge(sem("att_exp"), g - 1)
                    for j, h in enumerate(heads):
                        parts = queries(h)
                        for e, (qq, kk) in enumerate(zip(parts, keys(h))):
                            last = nc.tensor.matmul(M[g % 2][:, j * ns:(j + 1) * ns], qq[:, P * t:P * t + P], kk[:, 0:ns],
                                                    start=e == 0, stop=e == len(parts) - 1)
                    last.then_inc(sem("att_logits"), 1)

                def turned(k):
                    g = g0 + k
                    pe.wait_ge(sem("att_exp"), g + 1)
                    if k >= 1:
                        pe.wait_ge(sem("att_ptc"), g)
                    for c in range(4):
                        last = nc.tensor.transpose(M[2][:, c * P:(c + 1) * P], exps[:, g % 2, c * P:(c + 1) * P], ident)
                    last.then_inc(sem("att_pt"), 1)

                def weighed(k):
                    t, heads = work[k]
                    ns = keys_of(work, k)
                    g = g0 + k
                    pe.wait_ge(sem("att_ptc"), g + 1)
                    if k >= 1:
                        pe.wait_ge(sem("att_norm"), g)
                    per = ns // P
                    for j, h in enumerate(heads):
                        for s in range(per):
                            last = nc.tensor.matmul(M[3][:, j * width:(j + 1) * width], exps_turned[:, g % 2, (j * per + s) * P:][:, 0:P],
                                                    values(h, s), start=s == 0, stop=s == per - 1)
                    last.then_inc(sem("att_out"), 1)

                for k in range(n + 2):
                    if k < n:
                        logits(k)
                    yield k
                    if 1 <= k <= n:
                        turned(k - 1)
                    if k >= 2:
                        weighed(k - 2)
                groups[0] += n

            pe.wait_ge(sem("relu"), 6)
            for k in attention(WORK_A, lambda h: [qT[:, h, :]], lambda h: [kT[:, h // 4, :]],
                               lambda h, s: PA[:, s, AV + P * (h // 4):AV + P * (h // 4) + P], P,
                               LM, PTS):
                if 1 <= k <= 4:
                    mm(B_Q + 5, quarters=[k - 1])

            pe.wait_ge(sem("att_ptc"), 6)
            pe.wait_ge(sem("ev0"), B_Q + 6)
            pe.wait_ge(sem("ev1"), B_Q + 6)
            pe.wait_ge(sem("gdn_g"), 1)
            nc.tensor.matmul(M[2][:, 0:16], cst[:, C_CUM:C_CUM + P], GA_, start=True, stop=True)
            nc.tensor.matmul(M[2][:, 16:32], cst[:, C_ONES:C_ONES + P], GA_, start=True, stop=True).then_inc(sem("gdn_gc"), 1)

            def conv_in(e):
                if e >= 2:
                    pe.wait_ge(sem("conv_dve"), e - 1)
                for j in range(2):
                    for t in range(NT):
                        c = P * (2 * e + j)
                        last = nc.tensor.transpose(M[e % 2][:, (2 * j + t) * P:(2 * j + t + 1) * P], PQ[:, t, c:c + P], ident)
                last.then_inc(sem("conv_pe"), 1)

            def conv_back(e):
                pe.wait_ge(sem("gdn_y"), e + 1)
                if e == 0:
                    pe.wait_ge(sem("gdn_gcc"), 1)
                elif e == 1:
                    pe.wait_ge(sem("att_norm"), 6)
                elif e >= 10:
                    pe.wait_ge(sem("gdn_vb"), e - 9)
                elif e >= 2:
                    pe.wait_ge(sem("back_act"), e - 1)
                for j in range(2):
                    for t in range(NT):
                        last = nc.tensor.transpose(M[2 + e % 2][:, (2 * j + t) * P:(2 * j + t + 1) * P], YT[:, 2 * e + j, P * t:P * t + P], ident)
                last.then_inc(sem("back_pe"), 1)

            def decay_rows(u):
                if u < 2:
                    pe.wait_ge(sem("conv_dve"), 11 + u)
                    pe.wait_ge(sem("gdn_gu"), 1)
                else:
                    pe.wait_ge(sem("gdn_dm"), u - 1)
                src = GU[:, 4 * u:4 * u + 4, :].rearrange("p a b -> p (a b)")
                nc.tensor.matmul(M[u % 2][:, :], cst[:, C_ONES:C_ONES + P], src, start=True, stop=True).then_inc(sem("gdn_bc"), 1)

            for e in range(15):
                if e < 12:
                    conv_in(e)
                elif e < 14:
                    decay_rows(e - 12)
                if e >= 3:
                    conv_back(e - 3)
                mm(B_GB + e // 4, quarters=[e % 4])
            decay_rows(2)
            decay_rows(3)

            for u in range(4):
                if u < 2:
                    pe.wait_ge(sem("gdn_vb"), 3 + u)
                else:
                    pe.wait_ge(sem("gdn_dm"), 1 + u)
                for q in range(4):
                    h, tok = 4 * (u % 2) + q, slice(P * (u // 2), P * (u // 2) + P)
                    last = nc.tensor.matmul(M[(u + 2) % 4][:, P * q:P * q + P], YT[:, 8 + h, tok], YT[:, h, tok], start=True, stop=True)
                last.then_inc(sem("gdn_kq"), 1)
            mm(B_Z + 1, quarters=[3])
            mm(B_GA, quarters=[0])
            pe.wait_ge(sem("gdn_kb"), 2)
            for e in range(4):
                pe.wait_ge(sem("gdn_qk"), e + 1)
                for j in range(2):
                    for t in range(NT):
                        last = nc.tensor.transpose(M[(e + 2) % 4][:, (2 * j + t) * P:(2 * j + t + 1) * P], KB[:, t, 2 * e + j, :], ident)
                last.then_inc(sem("gdn_ktT"), 1)
            pe.wait_ge(sem("gdn_kt"), 4)
            for u in range(4):
                for q in range(4):
                    h, tok = 4 * (u % 2) + q, slice(P * (u // 2), P * (u // 2) + P)
                    last = nc.tensor.matmul(M[u][:, P * q:P * q + P], YT[:, 8 + h, tok], KBT[:, h, tok], start=True, stop=True)
                last.then_inc(sem("gdn_kk"), 1)
            mm(B_GA, quarters=[1, 2])

            def unit(u, lhsT, rhs, lv, odd):
                for q in range(4):
                    o = M[u][:, 64 * q:64 * q + 64].rearrange("p (m h) -> p m h", h=1 << lv)
                    last = nc.tensor.matmul(o, lhsT[:, 4 * u + q, :], blocks_of(rhs[:, 4 * u + q, :], lv, odd), start=True, stop=True)
                return last

            for u in range(4):
                pe.wait_ge(sem("inv_lt"), u + 1)
                for q in range(4):
                    last = nc.tensor.transpose(M[u][:, P * q:P * q + P], LT[:, 4 * u + q, :], ident)
                last.then_inc(sem("inv_p"), 1)
            mm(B_GA, quarters=[3])
            for lv in range(1, LEVELS):
                for u in range(4):
                    pe.wait_ge(sem("inv_lt"), 4 * lv + u + 1)
                    pe.wait_ge(sem("inv_x"), 4 * (lv - 1) + u + 1)
                    unit(u, LT, XI, lv, 0).then_inc(sem("inv_p"), 1)
                for u in range(4):
                    pe.wait_ge(sem("inv_pc"), 4 * (lv - 1) + u + 1)
                    if lv == 1:
                        pe.wait_ge(sem("inv_xt"), u + 1)
                    unit(u, PS, XT, lv, 1).then_inc(sem("inv_tp"), 1)
                if lv < LEVELS - 1:
                    for u in range(4):
                        pe.wait_ge(sem("inv_xt"), 4 * lv + u + 1)
                        for q in range(4):
                            last = nc.tensor.transpose(M[u][:, P * q:P * q + P], XT[:, 4 * u + q, :], ident)
                        last.then_inc(sem("inv_xp"), 1)

            pe.wait_ge(sem("inv_xt"), 4 * LEVELS)
            for half in range(2):
                for q in range(4):
                    h = 4 * half + q
                    last = nc.tensor.matmul(M[half][:, P * q:P * q + P], KBG[:, h, :], XT[:, 8 + h, :], start=True, stop=True)
                last.then_inc(sem("gdn_w"), 1)
            for half in range(2):
                for q in range(4):
                    h = 4 * half + q
                    last = nc.tensor.matmul(M[2 + half][:, P * q:P * q + P], XT[:, h, :], VB[:, 0, h, :], start=True, stop=True)
                last.then_inc(sem("gdn_u"), 1)
            mm(B_GA + 1, quarters=[0])
            for half in range(2):
                pe.wait_ge(sem("gdn_uc"), half + 1)
                for q in range(4):
                    h = 4 * half + q
                    last = nc.tensor.matmul(M[2 + half][:, P * q:P * q + P], KD[:, h, :], UV[:, 0, h, :], start=True, stop=True)
                last.then_inc(sem("st_kv"), 1)
            for half in range(2):
                pe.wait_ge(sem("gdn_wc"), half + 1)
                for q in range(4):
                    h = 4 * half + q
                    last = nc.tensor.matmul(M[half][:, P * q:P * q + P], QK[:, h, :], UV[:, 0, h, :], start=True, stop=True)
                last.then_inc(sem("o_pe"), 1)
            for half in range(2):
                pe.wait_ge(sem("st_new"), half + 1)
                for q in range(4):
                    h = 4 * half + q
                    nc.tensor.matmul(M[2 + half][:, P * q:P * q + P], XT[:, 8 + h, :], VB[:, 1, h, :], start=True, stop=False)
                    last = nc.tensor.matmul(M[2 + half][:, P * q:P * q + P], WT[:, h, :], ST[:, h, :], start=False, stop=True)
                last.then_inc(sem("st_ws"), 1)
            for half in range(2):
                pe.wait_ge(sem("o_copied"), half + 1)
                for q in range(4):
                    h = 4 * half + q
                    last = nc.tensor.matmul(M[half][:, P * q:P * q + P], YT[:, h, P:2 * P], ST[:, h, :], start=True, stop=True)
                last.then_inc(sem("o_pe"), 1)
            for half in range(2):
                pe.wait_ge(sem("st_v"), half + 1)
                for q in range(4):
                    h = 4 * half + q
                    last = nc.tensor.matmul(M[2 + half][:, P * q:P * q + P], QK[:, 8 + h, :], UV[:, 1, h, :], start=True, stop=True)
                last.then_inc(sem("o_pe"), 1)
            mm(B_GA + 1, quarters=[1, 2, 3])

            for half in range(2):
                turn(lambda kt, t: O1[:, t, kt, :], lambda q: [("o_done", 1 + q // 2)], banks=range(2 * half, 2 * half + 2))
                mm(B_O, turned=8, quarters=range(1) if half == 0 else range(1, 4))
            mm(B_O + 1)

            turn(xtile, lambda q: [("ev0", B_O + 1 + q // 2), ("ev1", B_O + 1 + q // 2), ("turn_lo", 8)])

            def hidden(b, i=None):
                pe.wait_ge(sem("hid_sq"), at(b + 1, 2, i))
                for q in range(2):
                    bank = M[2 * (b % 2) + q]
                    if b >= 2 or i is not None:
                        pe.wait_ge(sem("hid_lo"), at(2 * (b - 2) + q + 1, 4, i))
                    for kk in range(2):
                        for t in range(NT):
                            c = P * (2 * q + kk)
                            last = nc.tensor.transpose(bank[:, (2 * kk + t) * P:(2 * kk + t + 1) * P], hid[:, b % 2, t, c:c + P], ident)
                    last.then_inc(sem("hid_pe"), 1)

            mm(B_UP, turned=12)
            mm(B_UP + 1)
            hidden(0)
            mm(B_UP + 2)
            hidden(1)
            with pe.Fori(0, 2) as i:
                for j in range(2):
                    mm(B_UP + 3 + j, i)
                    hidden(2 + j, i)
            mm(B_UP + 7)
            hidden(6)
            mm(B_DN, stat=(hT_hi, hT_lo), hidden="hid_lo", quarters=[0, 1])
            hidden(7)
            mm(B_DN, stat=(hT_hi, hT_lo), hidden="hid_lo", quarters=range(2, DFF // P // 2))
            mm(B_DN + 1, stat=(hT_hi, hT_lo))

            turn(xtile, lambda q: [("ev0", B_DN + 1 + q // 2), ("ev1", B_DN + 1 + q // 2), ("hid_lo", 16)])
            for j in range(4):
                mm(B_2 + j, turned=None if j else 16)
            pe.wait_ge(sem("ret_rot"), 1)
            for e in range(4):
                for j in range(2):
                    for t in range(NT):
                        c = (RQ if e < 2 else RK) + P * (2 * (e % 2) + j)
                        last = nc.tensor.transpose(M[e][:, (2 * j + t) * P:(2 * j + t + 1) * P], P2R[:, t, c:c + P], ident)
                last.then_inc(sem("retT"), 1)
            mm(B_2 + 4)
            mm(B_2 + 5)
            pe.wait_ge(sem("ret_act"), 2)
            pe.wait_ge(sem("ret_dve"), 2)
            for par in range(2):
                for half in range(2):
                    e = 2 * par + half
                    for j in range(2):
                        q = 2 * half + j
                        last = nc.tensor.matmul(M[e][:, 256 * j:256 * j + 256], rkT[64 * par:64 * par + 64, q, 0:P],
                                                rqT[64 * par:64 * par + 64, q, :], start=True, stop=True)
                    last.then_inc(sem("ret_s"), 1)
            for par in range(2):
                pe.wait_ge(sem("ret_w"), par + 1)
                for q in range(4):
                    last = nc.tensor.matmul(M[par][:, P * q:P * q + P], rkT[64 * par:64 * par + 64, q, P:2 * P],
                                            rqT[64 * par:64 * par + 64, q, P:2 * P], start=True, stop=True)
                last.then_inc(sem("ret_s"), 1)
            mm(B_2 + 6)
            mm(B_2 + 7)
            pe.wait_ge(sem("ret_w"), 6)
            for t in range(NT):
                for h in range(8):
                    par, q = h % 2, h // 2
                    o = M[2 + t][:, 64 * h:64 * h + 64]
                    early = PT2[:, 512 * (2 * par + q // 2) + 256 * (q % 2) + P * t:][:, 0:P]
                    v = [P2R[:, s, RV + 64 * h:RV + 64 * h + 64] for s in range(2)]
                    last = nc.tensor.matmul(o, early, v[0], start=True, stop=t == 0)
                    if t == 1:
                        late = PT2[:, 2048 + 512 * par + P * q:][:, 0:P]
                        last = nc.tensor.matmul(o, late, v[1], start=False, stop=True)
                last.then_inc(sem("ret_o"), 1)

            pe.wait_ge(sem("mem_in"), 16)
            turn(lambda kt, t: MEM[:, t, P * kt:P * kt + P], lambda q: [("ret_oc", q - 1)] if q >= 2 else [])
            mm(B_KV, turned=20)
            mm(B_KV + 1, quarters=[0])
            pe.wait_ge(sem("fox_f"), 1)
            nc.tensor.matmul(M[0][:, 0:8], cst[:, C_CUM:C_CUM + P], FL[:, 0, :], start=True, stop=True)
            nc.tensor.matmul(M[0][:, 8:16], cst[:, C_ONES:C_ONES + P], FL[:, 0, :], start=True, stop=False)
            nc.tensor.matmul(M[0][:, 8:16], cst[:, C_CUM:C_CUM + P], FL[:, 1, :], start=False, stop=True).then_inc(sem("fox_fc"), 1)
            mm(B_KV + 1, quarters=[1, 2, 3])
            pe.wait_ge(sem("fox_aug"), 1)
            for e in range(8):
                src = QA if e < 4 else KA
                if e >= 4:
                    pe.wait_ge(sem("foxT_act" if e % 2 == 0 else "foxT_dve"), (e - 4) // 2 + 1)
                for j in range(2):
                    for t in range(NT):
                        last = nc.tensor.transpose(M[e % 4][0:66, (2 * j + t) * P:(2 * j + t + 1) * P], src[:, t, 2 * (e % 4) + j, :], ident)
                last.then_inc(sem("foxT_pe"), 1)
            pe.wait_ge(sem("foxT_act"), 3)
            pe.wait_ge(sem("foxT_dve"), 3)
            for k in attention(WORK_A, lambda h: [qaT[0:66, h, :]], lambda h: [kaT[0:66, h, :]],
                               lambda h, s: P2F[:, s, FV - 2048 + 64 * h:FV - 2048 + 64 * h + 64], 64, LM2, PTS2):
                if k == 0:
                    pe.wait_ge(sem("foxT_act"), 4)
                    pe.wait_ge(sem("foxT_dve"), 4)
                if k == 7:
                    turn(lambda kt, t: MG2[:, t, P * kt:P * kt + P], lambda q: [("ret_done", 1), ("att_max", 12)], banks=range(2))
                mm(B_KV + 2 + k // 4, quarters=[k % 4])
            mm(B_O2, turned=24, quarters=[0])
            turn(lambda kt, t: MG2[:, t, P * kt:P * kt + P], lambda q: [("att_norm", 12)], banks=range(2, 4))
            mm(B_O2, turned=24, quarters=[1, 2, 3])
            mm(B_O2 + 1)

            turn(xtile, lambda q: [("ev0", B_O2 + 1 + q // 2), ("ev1", B_O2 + 1 + q // 2), ("turn_lo", 24)])
            def cross_operands(banks):
                for e in banks:
                    if e >= 4:
                        pe.wait_ge(sem("xT_act" if e % 2 == 0 else "xT_dve"), (e - 4) // 2 + 1)
                        pe.wait_ge(sem("ev0"), B_XQ + 1 + (e - 4) // 2)
                        pe.wait_ge(sem("ev1"), B_XQ + 1 + (e - 4) // 2)
                    for j in range(2):
                        for t in range(NT):
                            c = P * (2 * (e % 4) + j)
                            src = (KV if e < 4 else XQ)[:, t, c:c + P]
                            last = nc.tensor.transpose(M[e % 4][:, (2 * j + t) * P:(2 * j + t + 1) * P], src, ident)
                    last.then_inc(sem("xT_pe"), 1)

            mm(B_XQ, turned=28)
            pe.wait_ge(sem("x_k"), 1)
            cross_operands(range(4))
            mm(B_XQ + 1)
            cross_operands(range(4, 8))
            pe.wait_ge(sem("xT_act"), 3)
            pe.wait_ge(sem("xT_dve"), 3)
            for k in attention(WORK_X, lambda h: [xqT[:, 2 * h + e, :] for e in range(2)],
                               lambda h: [xkT[:, 2 * h + e, :] for e in range(2)],
                               lambda h, s: KV[:, s, D + 256 * h:D + 256 * h + 256], 256, LM2, PTS2):
                if k == 0:
                    pe.wait_ge(sem("xT_act"), 4)
                    pe.wait_ge(sem("xT_dve"), 4)
                if k == 5:
                    turn(lambda kt, t: XO[:, t, P * kt:P * kt + P], lambda q: [("att_norm", 15), ("att_exp", 16)], banks=range(2))
            mm(B_XO, turned=32, quarters=[0])
            turn(lambda kt, t: XO[:, t, P * kt:P * kt + P], lambda q: [("att_norm", 16)], banks=range(2, 4))
            mm(B_XO, turned=32, quarters=[1, 2, 3])
            mm(B_XO + 1)

            turn(xtile, lambda q: [("ev0", B_XO + 1 + q // 2), ("ev1", B_XO + 1 + q // 2), ("turn_lo", 32)])
            def hidden2(p, i=None, q_n=2):
                pe.wait_ge(sem("hid2_sq"), at(p + 1, 1, i))
                for q in range(q_n):
                    if p >= 1 or i is not None:
                        pe.wait_ge(sem("hid2_lo"), at(2 * (p - 1) + q + 1, 2, i))
                    for kk in range(2):
                        for t in range(NT):
                            c = P * (2 * q + kk)
                            last = nc.tensor.transpose(M[q][:, (2 * kk + t) * P:(2 * kk + t + 1) * P], hid2[:, t, c:c + P], ident)
                    last.then_inc(sem("hid2_pe"), 1)

            for j in range(2):
                mm(B_GU + j, turned=None if j else 36)
            mm(B_GU + 2)
            hidden2(0)
            with pe.Fori(0, 3) as i:
                mm(B_GU + 3, i)
                mm(B_GU + 4, i)
                hidden2(1, i)
            mm(B_GU + 9)
            mm(B_GU + 10)
            hidden2(4)
            mm(B_GU + 11)
            mm(B_D2, stat=(h2_hi, h2_lo), hidden="hid2_lo", quarters=[0, 1])
            hidden2(5, q_n=1)
            mm(B_D2, stat=(h2_hi, h2_lo), hidden="hid2_lo", quarters=range(2, DFF2 // P // 2))
            mm(B_D2 + 1, stat=(h2_hi, h2_lo))

        @block.scalar
        def _(act):
            seen = {}

            def sig(ins, name):
                seen[name] = seen.get(name, 0) + 1
                ins.then_inc(sem(name), 1)

            def own(name):
                act.wait_ge(sem(name), seen[name])


            def split(b, c, i=None):
                n = blocks[b]["chunk0"] + c
                kn, width = chunk_shape(b, c)
                act.wait_ge(sem(f"loaded{n % SLOTS}"), at(16 * (n // SLOTS + 1), 16, i))
                nc.scalar.activation(w_hi[:, n % SLOTS, 0:kn, 0:width], raw[:, n % SLOTS, 0:kn, 0:width], ACT.Copy)\
                    .then_inc(sem("split_hi"), 1)

            def begin(b, i=None):
                for c in range(2, blocks[b]["chunks"]):
                    split(b, c, i)
                if b + 1 < B_END:
                    for c in range(2):
                        split(b + 1, c, i)

            def mm_finished(b, i=None):
                act.wait_ge(sem("mm_done"), at(blocks[b]["chunk0"] + blocks[b]["chunks"], 4, i))

            def project(b, dst, scale, i=None):
                mm_finished(b, i)
                nc.scalar.activation(dst, G[b % 2][0][:, 0:blocks[b]["n"]], ACT.Copy, scale=scale).then_inc(sem("ev0"), 1)

            def turn_hi(norm=None, banks=range(4)):
                for q in banks:
                    act.wait_ge(sem("turn_pe"), seen.get("turn_hi", 0) + 1)
                    if norm is None:
                        ins = nc.scalar.activation(s_hi[:, 2 * q:2 * q + 2, :], M[q].rearrange("p (a b) -> p a b", a=2), ACT.Copy)
                    else:
                        for kk in range(2):
                            ins = nc.scalar.activation(s_hi[:, 2 * q + kk, :], M[q][:, SEQ * kk:SEQ * kk + SEQ], ACT.Copy,
                                                       scale=gains[:, norm, 2 * q + kk:2 * q + kk + 1])
                    sig(ins, "turn_hi")

            def squares(norm, src):
                for t in range(NT):
                    if norm + t > 0:
                        act.wait_ge(sem("stat_ss"), 2 * norm + t)
                    nc.scalar.activation(junk[:, :], src[:, t, :], ACT.Square, accum_out=SS[:, 2 * norm + t:2 * norm + t + 1])\
                        .then_inc(sem("stat_ss"), 1)

            act.dma_start(ident, consts[:, C_ID:C_ID + P]).then_inc(sem("ident_in"), 16)
            act.dma_start(hidden_rows[0:8, :], norm_mix_g[0].rearrange("(k p) -> k p", p=P)).then_inc(sem("ident_in"), 16)
            split(0, 0)
            turn_hi(NORMS["mix"])
            split(0, 1)
            act.dma_start(cst[:, P:], consts[:, P:]).then_inc(sem("consts_in"), 16)
            act.wait_ge(sem("x_in0"), 16)
            act.wait_ge(sem("x_in1"), 16)
            squares(0, x)
            act.wait_ge(sem("stat_rs"), 1)
            for k in range(5):
                begin(B_A + k)
                project(B_A + k, PA[:, 0, block_columns(B_A + k)], RS[:, 0:1])
            begin(B_Q)
            act.wait_ge(sem("ev1"), 5)
            act.wait_ge(sem("ev0"), 5)
            for t in range(NT):
                ins = nc.scalar.activation(SQ[:, t], PA[:, t, AQ:AV].rearrange("p (h d) -> p h d", d=P), ACT.Square)
            ins.then_inc(sem("att_sq"), 1)
            act.wait_ge(sem("vec_in"), 16 * 11)
            nc.scalar.activation(SP[:, 40:48], vec[:, V_AL:V_AL + 8], ACT.Exp)
            act.wait_ge(sem("g_abs"), 1)
            sig(nc.scalar.activation(SP[:, 16:32], SP[:, 0:16], ACT.Exp, scale=-1.0), "g_exp")
            sig(nc.scalar.activation(BT.rearrange("p (t h) -> p t h", t=2), PA[:, :, 8:16], ACT.Tanh, scale=0.5), "b_tanh")
            own("g_exp")
            nc.scalar.activation(SP[:, 16:32], SP[:, 16:32], ACT.Ln, bias=1.0).then_inc(sem("g_ln"), 1)
            def operand(e, dst):
                act.wait_ge(sem("attT_pe"), e + 1)
                if e == 2:
                    ins = nc.scalar.activation(dst, M[2][:, 0:SEQ], ACT.Copy)
                else:
                    ins = nc.scalar.activation(dst, M[e % 4].rearrange("p (a b) -> p a b", a=2), ACT.Copy)
                sig(ins, "attT_act")

            project(B_Q, PQ[:, 0, 0:NCOL], RS[:, 0:1])
            for e, dst in enumerate((iqT[:, 0:2, :], iqT[:, 2:4, :], ikT)):
                operand(e, dst)
            begin(B_Q + 1)
            project(B_Q + 1, PQ[:, 0, NCOL:2 * NCOL], RS[:, 0:1])
            act.wait_ge(sem("scores"), 1)
            nc.scalar.activation(RL[:, 0:8:2, 0:P], M[0].rearrange("p (a b) -> p a b", a=4), ACT.Relu).then_inc(sem("relu"), 1)
            act.wait_ge(sem("scores"), 2)
            nc.scalar.activation(RL[:, 1:8:2, 0:P], M[1].rearrange("p (a b) -> p a b", a=4), ACT.Relu).then_inc(sem("relu"), 1)
            act.wait_ge(sem("acc"), 1)
            for n, (bank, h0) in enumerate(((2, 1), (3, 5), (0, 0), (1, 4))):
                act.wait_ge(sem("scores"), 3 + n)
                nc.scalar.activation(RL[:, h0:h0 + 3:2, :], M[bank].rearrange("p (a b) -> p a b", a=2), ACT.Relu).then_inc(sem("relu"), 1)
            begin(B_Q + 2)
            project(B_Q + 2, PQ[:, 0, NCOL * 2:NCOL * 3], RS[:, 0:1])
            for e, dst in ((3, kT), (5, qT[:, 2:4, :]), (7, qT[:, 6:8, :])):
                operand(e, dst)
            begin(B_Q + 3)
            project(B_Q + 3, PQ[:, 0, NCOL * 3:NCOL * 4], RS[:, 0:1])
            begin(B_Q + 4)
            project(B_Q + 4, PQ[:, 0, NCOL * 4:NCOL * 5], RS[:, 0:1])

            groups = [0]

            def attention(work, scale, src, dst):
                for k, (t, heads) in enumerate(work):
                    g = groups[0] + k
                    ns = keys_of(work, k)
                    act.wait_ge(sem("att_max"), g + 1)
                    if k >= 2:
                        act.wait_ge(sem("att_pt"), g - 1)
                    for j, h in enumerate(heads):
                        ins = nc.scalar.activation(dst[:, g % 2, j * ns:(j + 1) * ns], src(g)[:, j * ns:(j + 1) * ns], ACT.Exp, scale=scale(t, h),
                                                   bias=NEGM[:, 4 * (g % 8) + j:4 * (g % 8) + j + 1],
                                                   accum_out=SUMS[:, 4 * (g % 8) + j:4 * (g % 8) + j + 1])
                    ins.then_inc(sem("att_exp"), 1)
                    yield k
                groups[0] += len(work)

            for k in attention(WORK_A, lambda t, h: P ** -0.5, lambda g: LM[:, g % 2], LM):
                if k == 1:
                    begin(B_Q + 5)
                if k == 5:
                    project(B_Q + 5, PQ[:, 0, NCOL * 5:NCOL * 6], RS[:, 0:1])

            def gate(b, dst, t, scale, after=()):
                mm_finished(b)
                for s, v in after:
                    act.wait_ge(sem(s), v)
                return nc.scalar.activation(dst, G[b % 2][t][:, :], ACT.Tanh, scale=scale)

            act.wait_ge(sem("gdn_gcc"), 2)
            nc.scalar.activation(EG, GC[:, 0:16], ACT.Exp)
            nc.scalar.activation(ED, GC[:, 16:32], ACT.Exp).then_inc(sem("gdn_e"), 1)
            act.wait_ge(sem("stat_ss"), 2)

            def taken_back(e):
                act.wait_ge(sem("back_pe"), e + 1)
                if e >= 2:
                    act.wait_ge(sem("back_act"), e - 1)
                bank = M[2 + e % 2]
                for j in range(2):
                    for t in range(NT):
                        n = 2 * j + t
                        c = 16 * (e // 4) + 8 * t + 2 * (e % 4) + j
                        ins = nc.scalar.activation(junk[:, P * (4 * (e % 2) + n):][:, 0:P], bank[:, P * n:P * n + P], ACT.Square, accum_out=SSK[:, c:c + 1])
                if e >= 4:
                    h = 2 * (e % 4)
                    ins = nc.scalar.activation(KN[:, :, h:h + 2, :].rearrange("p t j d -> p j t d"), bank.rearrange("p (j t d) -> p j t d", j=2, t=2), ACT.Copy)
                ins.then_inc(sem("back_act"), 1)

            for e in range(13):
                if e < 12:
                    act.wait_ge(sem("conv_pe"), e + 1)
                    for j in range(2):
                        ct = 2 * e + j
                        ins = nc.scalar.activation(YT[:, ct, :], M[e % 2][:, SEQ * j:SEQ * j + SEQ], ACT.Copy, scale=cw[:, 3, ct:ct + 1])
                    ins.then_inc(sem("conv_act"), 1)
                if e >= 1:
                    act.wait_ge(sem("conv_dve"), e)
                    if e >= 3:
                        act.wait_ge(sem("gdn_y"), e - 2)
                    nc.scalar.activation(CT[:, (e - 1) % 2], YT[:, 2 * e - 2:2 * e, :], ACT.Tanh, scale=0.5).then_inc(sem("conv_tanh"), 1)
                if 4 <= e < 12:
                    taken_back(e - 4)
                if e in (4, 8):
                    b = B_GB + (e == 8)
                    for t in range(NT):
                        gate(b, TMP[:, t], t, HRS[:, t:t + 1], [("gate_used", b - B_GB)] if b > B_GB else []).then_inc(sem(f"ev{t}"), 1)
                if e in (1, 2, 5, 6, 9, 10):
                    split(B_GB + 1 + e // 4, (e - 1) % 4)
                if e == 12:
                    for t in range(NT):
                        sig(gate(B_Z, ZG[:, t, 0:NCOL], t, HRS[:, t:t + 1]), "z_tanh")
                    begin(B_Z + 1)
            for u in range(4):
                act.wait_ge(sem("gdn_dm"), u + 1)
                nc.scalar.activation(DM[:, 4 * u:4 * u + 4, :], DM[:, 4 * u:4 * u + 4, :], ACT.Exp).then_inc(sem("gdn_dme"), 1)
            for t in range(NT):
                sig(gate(B_Z + 1, ZG[:, t, NCOL:D], t, HRS[:, t:t + 1]), "z_tanh")
            for e in range(4):
                act.wait_ge(sem("gdn_ktT"), e + 1)
                nc.scalar.activation(KBT[:, 2 * e:2 * e + 2, :], M[(e + 2) % 4].rearrange("p (a b) -> p a b", a=2), ACT.Copy).then_inc(sem("gdn_kt"), 1)
            begin(B_GA)
            for lv in range(1, LEVELS):
                for u in range(4):
                    act.wait_ge(sem("inv_p"), 4 * lv + u + 1)
                    nc.scalar.activation(blocks_of(PS[:, 4 * u:4 * u + 4, :], lv, 0), half_bank(M[u], lv), ACT.Copy).then_inc(sem("inv_pc"), 1)
                if lv < LEVELS - 1:
                    for u in range(4):
                        act.wait_ge(sem("inv_xp"), 4 * (lv - 1) + u + 1)
                        new = blocks_of(M[u].rearrange("p (a b) -> p a b", a=4), lv, 0)
                        nc.scalar.activation(blocks_of(XI[:, 4 * u:4 * u + 4, :], lv, 0), new, ACT.Copy).then_inc(sem("inv_x"), 1)
                        if lv == 4 and u < 2:
                            gate(B_GA, TMP[:, u], u, HRS[:, u:u + 1], [("gate_used", 2)]).then_inc(sem(f"ev{u}"), 1)
            for half in range(2):
                if half == 0:
                    begin(B_GA + 1)
                act.wait_ge(sem("gdn_w"), half + 1)
                nc.scalar.activation(WT[:, 4 * half:4 * half + 4, :], M[half].rearrange("p (a b) -> p a b", a=4), ACT.Copy, scale=-1.0).then_inc(sem("gdn_wc"), 1)
            for half in range(2):
                act.wait_ge(sem("st_kv"), half + 1)
                nc.scalar.activation(ST[:, 4 * half:4 * half + 4, :], M[2 + half].rearrange("p (a b) -> p a b", a=4), ACT.Copy).then_inc(sem("st_new"), 1)

            def output_squares(t):
                for h in range(8):
                    ins = nc.scalar.activation(junk[:, P * h:P * h + P], O1[:, t, h, :], ACT.Square, accum_out=SSO[:, 8 * t + h:8 * t + h + 1])
                ins.then_inc(sem("o_sq"), 1)

            for half in range(2):
                act.wait_ge(sem("o_pe"), half + 1)
                sig(nc.scalar.activation(O1[:, 0, 4 * half:4 * half + 4, :], M[half].rearrange("p (a b) -> p a b", a=4), ACT.Copy), "o_copied")
            own("o_copied")
            act.wait_ge(sem("back_act"), 8)
            output_squares(0)
            act.wait_ge(sem("o_sq"), 1)
            act.wait_ge(sem("o_raw"), 2)
            output_squares(1)
            for t in range(NT):
                gate(B_GA + 1, TMP[:, t], t, HRS[:, t:t + 1], [("gate_used", 3)]).then_inc(sem(f"ev{t}"), 1)
            act.wait_ge(sem("o_sq"), 2)
            turn_hi()
            begin(B_O)
            begin(B_O + 1)
            turn_hi(NORMS["mlp"])
            act.wait_ge(sem("ev0"), B_UP)
            act.wait_ge(sem("ev1"), B_UP)
            squares(1, x)

            def square_hidden(b, i=None):
                for t in range(NT):
                    act.wait_ge(sem(f"ev{t}"), at(B_UP + b + 1, 2, i))
                    ins = nc.scalar.activation(hid[:, b % 2, t], hid[:, b % 2, t], ACT.Square)
                ins.then_inc(sem("hid_sq"), 1)

            def hidden_hi(b, i=None):
                for q in range(2):
                    act.wait_ge(sem("hid_pe"), at(2 * b + q + 1, 4, i))
                    nc.scalar.activation(hT_hi[:, bass.ds(at(4 * b + 2 * q, 8, i), 2), :], M[2 * (b % 2) + q].rearrange("p (a b) -> p a b", a=2), ACT.Copy)\
                        .then_inc(sem("hid_hi"), 1)

            begin(B_UP)
            square_hidden(0)
            with act.Fori(0, 3) as i:
                for j in range(2):
                    begin(B_UP + 1 + j, i)
                    hidden_hi(j, i)
                    square_hidden(1 + j, i)
            begin(B_UP + 7)
            hidden_hi(6)
            square_hidden(7)
            hidden_hi(7)
            begin(B_DN)
            begin(B_DN + 1)
            turn_hi(NORMS["mix2"])
            act.wait_ge(sem("ev0"), B_2)
            act.wait_ge(sem("ev1"), B_2)
            act.dma_start(WR, ret_w).then_inc(sem("ret_w_in"), 16)
            act.dma_start(MEM, mem_2[0].rearrange("(t p) d -> p t d", p=P)).then_inc(sem("mem_in"), 16)
            squares(2, x)
            act.wait_ge(sem("stat_rs"), 3)
            rs2 = RS[:, 4:5]
            for k in range(4):
                begin(B_2 + k)
                project(B_2 + k, P2R[:, 0, NCOL * k:NCOL * k + NCOL], rs2)
            begin(B_2 + 4)
            for e, dst in ((0, rqT[:, 0:2, :]), (2, rkT[:, 0:2, :])):
                act.wait_ge(sem("retT"), e + 1)
                nc.scalar.activation(dst, M[e].rearrange("p (a b) -> p a b", a=2), ACT.Copy).then_inc(sem("ret_act"), 1)
            project(B_2 + 4, P2F[:, 0, 0:NCOL], rs2)
            begin(B_2 + 5)
            project(B_2 + 5, P2F[:, 0, NCOL:2 * NCOL], rs2)
            begin(B_2 + 6)
            act.wait_ge(sem("ev0"), B_2 + 6)
            act.wait_ge(sem("ev1"), B_2 + 6)
            for t in range(NT):
                ins = nc.scalar.activation(SQR[:, t], P2F[:, t, 0:1024].rearrange("p (h d) -> p h d", d=64), ACT.Square)
            ins.then_inc(sem("fox_sq"), 1)
            project(B_2 + 6, P2F[:, 0, block_columns(B_2 + 6)], rs2)
            begin(B_2 + 7)
            project(B_2 + 7, P2F[:, 0, block_columns(B_2 + 7)], rs2)
            for t in range(NT):
                act.wait_ge(sem("ret_o"), t + 1)
                nc.scalar.activation(MG2[:, t, 0:NCOL], M[2 + t][:, :], ACT.Copy).then_inc(sem("ret_oc"), 1)
            turn_hi(NORMS["mem"])
            begin(B_KV)
            act.wait_ge(sem("mem_in"), 16)
            squares(3, MEM)
            act.wait_ge(sem("ev0"), B_2 + 4)
            act.wait_ge(sem("ev1"), B_2 + 4)
            nc.scalar.activation(TG, P2R[:, :, RG:RG + NCOL], ACT.Tanh, scale=0.5).then_inc(sem("rg_tanh"), 1)
            act.wait_ge(sem("ret_cen"), 1)
            nc.scalar.activation(RSQ, MG2[:, :, 0:NCOL], ACT.Square).then_inc(sem("ret_sq"), 1)
            act.wait_ge(sem("f_abs"), 1)
            sig(nc.scalar.activation(SP[:, 16:32], SP[:, 0:16], ACT.Exp, scale=-1.0), "g_exp")
            own("g_exp")
            nc.scalar.activation(SP[:, 16:32], SP[:, 16:32], ACT.Ln, bias=1.0).then_inc(sem("f_ln"), 1)
            act.wait_ge(sem("stat_rs"), 4)
            rs4 = RS[:, 6:7]
            project(B_KV, KV[:, 0, 0:NCOL], rs4)
            begin(B_KV + 1)
            project(B_KV + 1, KV[:, 0, NCOL:D], rs4)
            for e in range(0, 8, 2):
                act.wait_ge(sem("foxT_pe"), e + 1)
                dst = (qaT if e < 4 else kaT)[0:66, 2 * (e % 4):2 * (e % 4) + 2, :]
                nc.scalar.activation(dst, M[e % 4][0:66, :].rearrange("p (a b) -> p a b", a=2), ACT.Copy).then_inc(sem("foxT_act"), 1)
            for k in attention(WORK_A, lambda t, h: 1.0, lambda g: LM2[:, g % 2], LM2):
                if k < 2:
                    split(B_KV + 3, k)
                if k == 4:
                    project(B_KV + 2, KV[:, 0, D:D + NCOL], rs4)
                if k >= 4:
                    split(B_O2, k - 4)
            turn_hi(banks=range(2))
            project(B_KV + 3, KV[:, 0, D + NCOL:2 * D], rs4)
            turn_hi(banks=range(2, 4))
            begin(B_O2)
            act.wait_ge(sem("ev0"), B_O2)
            act.wait_ge(sem("ev1"), B_O2)
            nc.scalar.activation(SQX, KV[:, :, 0:D], ACT.Square).then_inc(sem("x_sqk"), 1)
            begin(B_O2 + 1)
            turn_hi(NORMS["xattn"])
            act.wait_ge(sem("ev0"), B_XQ)
            act.wait_ge(sem("ev1"), B_XQ)
            squares(4, x)
            act.wait_ge(sem("stat_rs"), 5)
            for k in range(2):
                begin(B_XQ + k)
                project(B_XQ + k, XQ[:, 0, NCOL * k:NCOL * k + NCOL], RS[:, 8:9])
                act.wait_ge(sem("ev0"), B_XQ + k + 1)
                act.wait_ge(sem("ev1"), B_XQ + k + 1)
                act.wait_ge(sem("stat_ss"), 10)
                act.wait_ge(sem("x_ms"), 1)
                if k == 1:
                    act.wait_ge(sem("x_sqq"), 1)
                for t in range(NT):
                    for h in (2 * k, 2 * k + 1):
                        ins = nc.scalar.activation(junk[:, 256 * (2 * t + h % 2):][:, 0:256], XQ[:, t, 256 * h:256 * h + 256], ACT.Square,
                                                   accum_out=SSX[:, 4 * t + h:4 * t + h + 1])
                ins.then_inc(sem("x_sqq"), 1)
                for e in (4 * k, 4 * k + 2):
                    act.wait_ge(sem("xT_pe"), e + 1)
                    dst = (xkT if e < 4 else xqT)[:, 2 * (e % 4):2 * (e % 4) + 2, :]
                    nc.scalar.activation(dst, M[e % 4].rearrange("p (a b) -> p a b", a=2), ACT.Copy).then_inc(sem("xT_act"), 1)
            act.wait_ge(sem("x_sc"), 1)
            for k in attention(WORK_X, lambda t, h: XSC[:, 4 * t + h:4 * t + h + 1], lambda g: M[g % 2], LM2):
                pass
            turn_hi()
            begin(B_XO)
            begin(B_XO + 1)
            turn_hi(NORMS["ffn"])
            act.wait_ge(sem("ev0"), B_GU)
            act.wait_ge(sem("ev1"), B_GU)
            squares(5, x)
            act.wait_ge(sem("stat_rs"), 6)

            def gate_tanh(p, i=None):
                b = B_GU + 2 * p
                mm_finished(b, i)
                n = blocks[b]["n"]
                for t in range(NT):
                    if i is not None or p > 0:
                        act.wait_ge(sem(f"ev{t}"), at(b - 1, 2, i))
                    nc.scalar.activation(sg2[:, 0, t, 0:n], G[b % 2][t][:, 0:n], ACT.Tanh, scale=RS5H[:, t:t + 1]).then_inc(sem("gate_tanh"), 1)

            def scale_hidden(p, i=None):
                n = blocks[B_GU + 2 * p]["n"]
                for t in range(NT):
                    act.wait_ge(sem(f"ev{t}"), at(B_GU + 2 * p + 2, 2, i))
                    ins = nc.scalar.activation(hid2[:, t, 0:n], hid2[:, t, 0:n], ACT.Copy, scale=RS5Q[:, t:t + 1])
                ins.then_inc(sem("hid2_sq"), 1)

            def hidden2_hi(p, i=None, q_n=2):
                for q in range(q_n):
                    act.wait_ge(sem("hid2_pe"), at(2 * p + q + 1, 2, i))
                    nc.scalar.activation(h2_hi[:, bass.ds(at(4 * p + 2 * q, 4, i), 2), :], M[q].rearrange("p (a b) -> p a b", a=2), ACT.Copy)\
                        .then_inc(sem("hid2_hi"), 1)

            act.wait_ge(sem("rs5"), 1)
            begin(B_GU)
            gate_tanh(0)
            begin(B_GU + 1)
            scale_hidden(0)
            with act.Fori(0, 3) as i:
                begin(B_GU + 2, i)
                gate_tanh(1, i)
                begin(B_GU + 3, i)
                hidden2_hi(0, i)
                scale_hidden(1, i)
            begin(B_GU + 8)
            gate_tanh(4)
            begin(B_GU + 9)
            hidden2_hi(3)
            scale_hidden(4)
            begin(B_GU + 10)
            gate_tanh(5)
            hidden2_hi(4)
            begin(B_GU + 11)
            scale_hidden(5)
            hidden2_hi(5, q_n=1)
            begin(B_D2)
            begin(B_D2 + 1)

        @block.vector
        def _(dve):
            seen = {}
            V = nc.vector

            def sig(ins, name):
                seen[name] = seen.get(name, 0) + 1
                ins.then_inc(sem(name), 1)

            def link(ins):
                sig(ins, "dve_step")
                dve.wait_ge(sem("dve_step"), seen["dve_step"])

            def split(b, c, i=None):
                if pool_chunk(b, c):
                    return
                n = blocks[b]["chunk0"] + c
                kn, width = chunk_shape(b, c)
                dve.wait_ge(sem("split_hi"), at(n + 1, 4, i))
                s = n % SLOTS
                V.tensor_tensor(w_lo[:, s, 0:kn, 0:width], raw[:, s, 0:kn, 0:width], w_hi[:, s, 0:kn, 0:width].bitcast(F32), ALU.subtract)\
                    .then_inc(sem("split_lo"), 1)

            def begin(b, i=None):
                for c in range(2, blocks[b]["chunks"]):
                    split(b, c, i)
                if b + 1 < B_END:
                    for c in range(2):
                        split(b + 1, c, i)

            def mm_finished(b, i=None):
                dve.wait_ge(sem("mm_done"), at(blocks[b]["chunk0"] + blocks[b]["chunks"], 4, i))

            def project(b, dst, scale, i=None):
                mm_finished(b, i)
                V.tensor_scalar(dst, G[b % 2][1][:, 0:blocks[b]["n"]], scale, None, ALU.mult).then_inc(sem("ev1"), 1)

            def residual(b, half, last=False):
                for t in range(NT):
                    if b in EARLY and t == 0:
                        dve.wait_ge(sem("first_tile"), EARLY.index(b) + 1)
                    else:
                        mm_finished(b)
                    cols = x[:, t, NCOL * half:NCOL * half + NCOL]
                    ins = V.tensor_tensor(cols, G[b % 2][t][:, :], cols, ALU.add)
                    ins.then_inc(sem("x_final") if last else sem(f"ev{t}"), 1)

            def turn_lo(norm=None, banks=range(4)):
                for q in banks:
                    dve.wait_ge(sem("turn_hi"), seen.get("turn_lo", 0) + 1)
                    if norm is None:
                        hi = s_hi[:, 2 * q:2 * q + 2, :].bitcast(F32)
                        ins = V.tensor_tensor(s_lo[:, 2 * q:2 * q + 2, :], M[q].rearrange("p (a b) -> p a b", a=2), hi, ALU.subtract)
                    else:
                        for kk in range(2):
                            kt = 2 * q + kk
                            ins = V.scalar_tensor_tensor(s_lo[:, kt, :], M[q][:, SEQ * kk:SEQ * kk + SEQ], gains[:, norm, kt:kt + 1],
                                                         s_hi[:, kt, :].bitcast(F32), ALU.mult, ALU.subtract)
                    sig(ins, "turn_lo")

            def mean_squares(norm):
                dve.wait_ge(sem("stat_ss"), 2 * norm + 2)
                V.tensor_scalar(RS[:, 2 * norm:2 * norm + 2], SS[:, 2 * norm:2 * norm + 2], 1 / D, EPS, ALU.mult, ALU.add).then_inc(sem("stat_ms"), 1)

            def rotate(x1, x2, cos, sin, prod, eng, lnk):
                eng.tensor_tensor(prod[0], x1, cos, ALU.mult)
                eng.tensor_tensor(prod[1], x2, sin, ALU.mult)
                eng.tensor_tensor(prod[2], x2, cos, ALU.mult)
                lnk(eng.tensor_tensor(prod[3], x1, sin, ALU.mult))
                eng.tensor_tensor(x1, prod[0], prod[1], ALU.subtract)
                return eng.tensor_tensor(x2, prod[2], prod[3], ALU.add)

            dve.wait_ge(sem("vec_pe"), 1)
            sig(V.tensor_copy(gains[:, 0, :], M[0][:, 0:8]), "vec_dve")
            split(0, 0)
            turn_lo(NORMS["mix"])
            split(0, 1)
            mean_squares(0)
            dve.wait_ge(sem("stat_rs"), 1)
            V.tensor_scalar(HRS, RS[:, 0:2], 0.5, None, ALU.mult)
            link(V.tensor_scalar(QRS, RS[:, 0:2], 0.25, None, ALU.mult))
            for k in range(5):
                begin(B_A + k)
                project(B_A + k, PA[:, 1, block_columns(B_A + k)], RS[:, 1:2])
                if k == 0:
                    dve.wait_ge(sem("vec_pe"), 2)
                    V.tensor_copy(gains[:, 1:6, :].rearrange("p a b -> p (a b)"), M[0][:, 8:48])
                    V.tensor_copy(cw.rearrange("p a b -> p (a b)"), M[0][:, 128:224]).then_inc(sem("vec_dve"), 1)
            begin(B_Q)
            dve.wait_ge(sem("ev0"), 5)
            dve.wait_ge(sem("ev1"), 5)
            dve.wait_ge(sem("vec_in"), 16 * 11)
            dve.wait_ge(sem("consts_in"), 16)
            sp2 = SP[:, 0:16].rearrange("p (t h) -> p t h", t=2)
            link(V.tensor_tensor(sp2, PA[:, :, 0:8], spread(vec[:, V_DT:V_DT + 8], 1, 2), ALU.add))
            link(V.tensor_scalar(GA_, SP[:, 0:16], 0.0, None, ALU.max))
            V.scalar_tensor_tensor(SP[:, 0:16], SP[:, 0:16], -1.0, SP[:, 0:16], ALU.mult, ALU.max).then_inc(sem("g_abs"), 1)
            heads = PA[:, :, AQ:AV].rearrange("p t (h d) -> p t h d", d=P)
            dve.wait_ge(sem("att_sq"), 1)
            link(V.tensor_reduce(SSA, SQ.rearrange("p t h d -> p (t h) d"), AX_X, ALU.add))
            V.tensor_scalar(SSA, SSA, 1 / P, EPS, ALU.mult, ALU.add).then_inc(sem("att_ms"), 1)
            V.tensor_scalar(IWS.rearrange("p (t h) -> p t h", t=2), PA[:, :, IW:IW + 8], 8 ** -0.5 * 64 ** -0.5, None, ALU.mult)
            project(B_Q, PQ[:, 1, 0:NCOL], RS[:, 1:2])
            dve.wait_ge(sem("att_rn"), 1)
            for t in range(NT):
                ins = V.tensor_tensor(heads[:, t], heads[:, t], spread(RNA[:, 10 * t:10 * t + 10], 2, P), ALU.mult)
            link(ins)
            for t in range(NT):
                V.tensor_tensor(heads[:, t, 0:8], heads[:, t, 0:8], spread(vec[:, V_QG:V_QG + P], 1, 8), ALU.mult)
                ins = V.tensor_tensor(heads[:, t, 8:10], heads[:, t, 8:10], spread(vec[:, V_KG:V_KG + P], 1, 2), ALU.mult)
            link(ins)
            ca, sa = (spread(cst[:, C_ROPE_A + 32 * k:C_ROPE_A + 32 * k + 32].rearrange("p (t d) -> p t d", t=2), 2, 10) for k in range(2))
            prods = [RT[:, k].rearrange("p (t h d) -> p t h d", t=2, h=10) for k in range(4)]
            sig(rotate(heads[:, :, :, 0:16], heads[:, :, :, 16:32], ca, sa, prods, V, link), "att_rot")
            begin(B_Q + 1)
            project(B_Q + 1, PQ[:, 1, NCOL:2 * NCOL], RS[:, 1:2])
            for t in range(NT):
                ns = P * (t + 1)
                dve.wait_ge(sem("relu"), 2 if t == 0 else 6)
                link(V.tensor_scalar(SC[:, t, 0:ns], RL[:, 0, 0:ns], IWS[:, 8 * t:8 * t + 1], None, ALU.mult))
                for h in range(1, 8):
                    ins = V.scalar_tensor_tensor(SC[:, t, 0:ns], RL[:, h, 0:ns], IWS[:, 8 * t + h:8 * t + h + 1], SC[:, t, 0:ns], ALU.mult, ALU.add)
                    if h < 7:
                        link(ins)
                    elif t == 0:
                        sig(ins, "acc")
                        dve.wait_ge(sem("acc"), 1)
                    else:
                        link(ins)
                diag = SC[:, t, P * t:P * t + P]
                link(V.tensor_tensor(diag, diag, cst[:, C_TRIX:C_TRIX + P], ALU.add))
            begin(B_Q + 2)
            dve.wait_ge(sem("b_tanh"), 1)
            link(V.tensor_scalar(BT, BT, 0.5, 0.5, ALU.mult, ALU.add))
            V.tensor_scalar(HBT, BT, 0.5, None, ALU.mult)
            dve.wait_ge(sem("g_ln"), 1)
            link(V.tensor_tensor(GA_, GA_, SP[:, 16:32], ALU.add))
            V.scalar_tensor_tensor(GA_.rearrange("p (t h) -> p t h", t=2), GA_.rearrange("p (t h) -> p t h", t=2), -1.0,
                                   spread(SP[:, 40:48], 1, 2), ALU.mult, ALU.mult).then_inc(sem("gdn_g"), 1)
            project(B_Q + 2, PQ[:, 1, NCOL * 2:NCOL * 3], RS[:, 1:2])
            for e, dst in ((4, qT[:, 0:2, :]), (6, qT[:, 4:6, :])):
                dve.wait_ge(sem("attT_pe"), e + 1)
                V.tensor_copy(dst, M[e % 4].rearrange("p (a b) -> p a b", a=2)).then_inc(sem("attT_dve"), 1)

            def select(rounds):
                for _ in rounds:
                    for t in range(NT):
                        ins = V.max(MX8[:, 8 * t:8 * t + 8], SC[:, t, 0:P * (t + 1)])
                    link(ins)
                    for t in range(NT):
                        ins = V.match_replace(SC[:, t, 0:P * (t + 1)], MX8[:, 8 * t:8 * t + 8], SC[:, t, 0:P * (t + 1)], TAKEN)
                    link(ins)

            select(range(4))
            begin(B_Q + 3)
            project(B_Q + 3, PQ[:, 1, NCOL * 3:NCOL * 4], RS[:, 1:2])
            begin(B_Q + 4)
            select(range(4))
            for t in range(NT):
                ns = P * (t + 1)
                link(V.tensor_scalar(BIAS[:, t, 0:ns], SC[:, t, 0:ns], BETWEEN, EXCLUDED, ALU.is_ge, ALU.mult))
                diag = BIAS[:, t, P * t:P * t + P]
                link(V.tensor_tensor(diag, diag, cst[:, C_TRI:C_TRI + P], ALU.add))

            groups = [0]

            def attention(work, scale, width, mask, lm, pts, dst):
                g0, n = groups[0], len(work)

                def greatest(k):
                    t, hs = work[k]
                    g, ns = g0 + k, keys_of(work, k)
                    a = 4 * (g % 8)
                    dve.wait_ge(sem("att_logits"), g + 1)
                    if mask is None:
                        link(V.tensor_reduce(NEGM[:, a:a + len(hs)], M[g % 2].rearrange("p (a b) -> p a b", b=ns), AX_X, ALU.max))
                    else:
                        if k >= 2:
                            dve.wait_ge(sem("att_pt"), g - 1)
                        for j in range(len(hs)):
                            ins = V.tensor_tensor_reduce(lm[:, g % 2, j * ns:(j + 1) * ns], M[g % 2][:, j * ns:(j + 1) * ns], mask(t), 1.0, -3.0e38,
                                                         ALU.add, ALU.max, NEGM[:, a + j:a + j + 1])
                        link(ins)
                    if mask is None:
                        V.tensor_tensor(NEGM[:, a:a + len(hs)], NEGM[:, a:a + len(hs)], scale(t, hs), ALU.mult).then_inc(sem("att_max"), 1)
                    else:
                        V.tensor_scalar(NEGM[:, a:a + len(hs)], NEGM[:, a:a + len(hs)], -scale, None, ALU.mult).then_inc(sem("att_max"), 1)

                def turned(k):
                    g = g0 + k
                    dve.wait_ge(sem("att_pt"), g + 1)
                    if k >= 2:
                        dve.wait_ge(sem("att_out"), g - 1)
                    V.tensor_copy(pts[:, g % 2, :], M[2][:, :]).then_inc(sem("att_ptc"), 1)

                def normed(k):
                    t, hs = work[k]
                    g = g0 + k
                    a = 4 * (g % 8)
                    link(V.reciprocal(RSUM[:, a:a + len(hs)], SUMS[:, a:a + len(hs)]))
                    dve.wait_ge(sem("att_out"), g + 1)
                    V.tensor_tensor(dst(t, hs), M[3][:, 0:width * len(hs)].rearrange("p (a b) -> p a b", b=width),
                                    spread(RSUM[:, a:a + len(hs)], 2, width), ALU.mult).then_inc(sem("att_norm"), 1)

                for k in range(n + 2):
                    if k < n:
                        greatest(k)
                    if 1 <= k <= n:
                        turned(k - 1)
                    if k >= 2:
                        normed(k - 2)
                    yield k
                groups[0] += n

            for k in attention(WORK_A, P ** -0.5, P, lambda t: BIAS[:, t, 0:P * (t + 1)], LM, PTS, lambda t, hs: OA[:, t, hs[0]:hs[-1] + 1, :]):
                if k == 1:
                    project(B_Q + 4, PQ[:, 1, NCOL * 4:NCOL * 5], RS[:, 1:2])
                if k == 2:
                    begin(B_Q + 5)
                if k == 5:
                    project(B_Q + 5, PQ[:, 1, NCOL * 5:NCOL * 6], RS[:, 1:2])

            def silu(e):
                dve.wait_ge(sem("conv_tanh"), e + 1)
                y = YT[:, 2 * e:2 * e + 2, :]
                sig(V.scalar_tensor_tensor(y, CT[:, e % 2], 1.0, y, ALU.add, ALU.mult), "gdn_y")

            def z_block(b, half):
                for t in range(NT):
                    dve.wait_ge(sem("z_tanh"), 2 * half + t + 1)
                    cols = ZG[:, t, NCOL * half:NCOL * half + NCOL]
                    V.scalar_tensor_tensor(cols, cols, 1.0, G[b % 2][t][:, :], ALU.add, ALU.mult).then_inc(sem(f"ev{t}"), 1)

            def decays(u):
                dve.wait_ge(sem("gdn_bc"), u + 1)
                for q in range(4):
                    n = 4 * u + q
                    ins = V.scalar_tensor_tensor(DM[:, n, :], M[u % 2][:, P * q:P * q + P], GC[:, n:n + 1], cst[:, C_NEG:C_NEG + P], ALU.subtract, ALU.add)
                ins.then_inc(sem("gdn_dm"), 1)

            dve.wait_ge(sem("gdn_gc"), 1)
            sig(V.tensor_copy(GC, M[2][:, 0:32]), "gdn_gcc")
            dve.wait_ge(sem("gdn_gcc"), 1)
            sig(V.tensor_tensor(GC[:, 16:32], GC[:, 16:32], GC[:, 0:16], ALU.subtract), "gdn_gcc")
            oa = OA.rearrange("p t h d -> p t (h d)")
            for e in range(16):
                if e < 12:
                    dve.wait_ge(sem("conv_act"), e + 1)
                    for tap in range(1, 4):
                        for j in range(2):
                            ct = 2 * e + j
                            y = YT[:, ct, tap:SEQ]
                            ins = V.scalar_tensor_tensor(y, M[e % 2][:, SEQ * j:SEQ * j + SEQ - tap], cw[:, 3 - tap, ct:ct + 1], y, ALU.mult, ALU.add)
                        if tap < 3:
                            link(ins)
                    sig(ins, "conv_dve")
                if 1 <= e <= 12:
                    silu(e - 1)
                if e >= 12:
                    dve.wait_ge(sem("back_pe"), e - 3)
                    h = 2 * (e - 12)
                    f = HBT.rearrange("p (t h) -> p h t", t=2)[:, h:h + 2, :]
                    sig(V.tensor_tensor(VB[:, :, h:h + 2, :].rearrange("p t j d -> p j t d"), M[2 + e % 2].rearrange("p (j t d) -> p j t d", j=2, t=2),
                                        spread(f, 3, P), ALU.mult), "gdn_vb")
                if e in (5, 9):
                    b = B_GB + (e == 9)
                    cols = slice(NCOL * (e == 9), NCOL * (e == 9) + NCOL)
                    for t in range(NT):
                        dve.wait_ge(sem(f"ev{t}"), b + 1)
                        ins = V.scalar_tensor_tensor(oa[:, t, cols], TMP[:, t], 1.0, oa[:, t, cols], ALU.add, ALU.mult)
                    ins.then_inc(sem("gate_used"), 1)
                if e == 12:
                    z_block(B_Z, 0)
                    dve.wait_ge(sem("back_act"), 8)
                    V.tensor_scalar(SSK, SSK, 0.25, EPS, ALU.mult, ALU.add).then_inc(sem("gdn_ms"), 1)
                if 12 <= e < 14:
                    decays(e - 12)
            decays(2)
            decays(3)
            split(B_GA, 0)
            dve.wait_ge(sem("gdn_rq"), 1)
            dve.wait_ge(sem("gdn_e"), 1)
            link(V.tensor_scalar(RQK, RQK, 0.5, None, ALU.mult))
            V.tensor_tensor(KDF, RQK[:, 16:24], ED[:, 0:8], ALU.mult).then_inc(sem("gdn_kdf"), 1)
            link(V.tensor_tensor(BRK, RQK[:, 16:32], BT, ALU.mult))
            for t in range(NT):
                V.tensor_tensor(KB[:, t], KN[:, t], spread(BRK[:, 8 * t:8 * t + 8], 2, P), ALU.mult).then_inc(sem("gdn_kb"), 1)
            link(V.tensor_scalar(RQK[:, 0:16], RQK[:, 0:16], P ** -0.5, None, ALU.mult))
            V.scalar_tensor_tensor(FSQ, RQK[:, 0:16], 1 / P, RQK[:, 0:16], ALU.mult, ALU.mult)
            link(V.tensor_tensor(FQ.rearrange("p (t h) -> p t h", t=2), RQK[:, 0:16].rearrange("p (t h) -> p t h", t=2), spread(QRS, 2, 8), ALU.mult))

            def decayed(dst, bank, u, name):
                for q in range(4):
                    n = 4 * u + q
                    ins = V.scalar_tensor_tensor(dst[:, n, :], bank[:, P * q:P * q + P], RQK[:, 16 + n:17 + n], DM[:, n, :], ALU.mult, ALU.mult)
                ins.then_inc(sem(name), 1)

            dve.wait_ge(sem("gdn_kd"), 1)
            dve.wait_ge(sem("gdn_kb"), 2)
            for u in range(4):
                dve.wait_ge(sem("gdn_kq"), u + 1)
                dve.wait_ge(sem("gdn_dme"), u + 1)
                decayed(QK, M[(u + 2) % 4], u, "gdn_qk")
            z_block(B_Z + 1, 1)
            split(B_GA, 1)
            for u in range(4):
                dve.wait_ge(sem("gdn_kk"), u + 1)
                decayed(AT, M[u], u, "gdn_at")

            eye = spread(ident, 1, 4)
            dve.wait_ge(sem("gdn_kbg"), 1)
            for u in range(4):
                n = slice(4 * u, 4 * u + 4)
                dve.wait_ge(sem("inv_p"), u + 1)
                V.tensor_tensor(XI[:, n, :], eye, M[u].rearrange("p (a b) -> p a b", a=4), ALU.subtract).then_inc(sem("inv_x"), 1)
                V.tensor_tensor(XT[:, n, :], eye, LT[:, n, :], ALU.subtract).then_inc(sem("inv_xt"), 1)

            begin(B_GA)

            def gate_a(b, half):
                cols = slice(NCOL * half, NCOL * half + NCOL)
                for t in range(NT):
                    dve.wait_ge(sem(f"ev{t}"), b + 1)
                    ins = V.scalar_tensor_tensor(ZG[:, t, cols], TMP[:, t], 1.0, ZG[:, t, cols], ALU.add, ALU.mult)
                sig(ins, "gate_used")

            for lv in range(1, LEVELS):
                for u in range(4):
                    n = slice(4 * u, 4 * u + 4)
                    dve.wait_ge(sem("inv_tp"), 4 * (lv - 1) + u + 1)
                    odd = blocks_of(XT[:, n, :], lv, 1)
                    V.scalar_tensor_tensor(odd, half_bank(M[u], lv), cst[:, C_EVEN + lv:C_EVEN + lv + 1], odd, ALU.mult, ALU.add)\
                        .then_inc(sem("inv_xt"), 1)
                if lv == 1:
                    zg = ZG.rearrange("p t (h d) -> p (t h) d", d=P)
                    link(V.tensor_tensor(zg, zg, spread(vec[:, V_GN:V_GN + P], 1, 16), ALU.mult))
                if lv == 5:
                    gate_a(B_GA, 0)
            begin(B_GA + 1)
            for half in range(2):
                dve.wait_ge(sem("gdn_u"), half + 1)
                V.tensor_copy(UV[:, 0, 4 * half:4 * half + 4, :], M[2 + half].rearrange("p (a b) -> p a b", a=4)).then_inc(sem("gdn_uc"), 1)
            for half in range(2):
                dve.wait_ge(sem("st_ws"), half + 1)
                V.tensor_copy(UV[:, 1, 4 * half:4 * half + 4, :], M[2 + half].rearrange("p (a b) -> p a b", a=4)).then_inc(sem("st_v"), 1)

            def output_norm(t):
                c = slice(8 * t, 8 * t + 8)
                dve.wait_ge(sem("o_sq"), t + 1)
                link(V.tensor_tensor(SSO[:, c], SSO[:, c], FSQ[:, c], ALU.mult))
                V.tensor_scalar(SSO[:, c], SSO[:, c], EPS, None, ALU.add).then_inc(sem("o_ms"), 1)

            def output_factors(t):
                c = slice(8 * t, 8 * t + 8)
                dve.wait_ge(sem("o_rs"), t + 1)
                link(V.tensor_tensor(RSO[:, c], RSO[:, c], FQ[:, c], ALU.mult))
                link(V.tensor_tensor(O1[:, t], O1[:, t], spread(RSO[:, c], 2, P), ALU.mult))

            def times_z(t):
                o = O1[:, t].rearrange("p h d -> p (h d)")
                link(V.tensor_tensor(o, o, ZG[:, t], ALU.mult))

            output_norm(0)
            for half in range(2):
                hh = slice(4 * half, 4 * half + 4)
                dve.wait_ge(sem("o_pe"), 3 + half)
                ins = V.tensor_tensor(O1[:, 1, hh, :], M[half].rearrange("p (a b) -> p a b", a=4), spread(EG[:, 8 + 4 * half:12 + 4 * half], 2, P), ALU.mult)
            link(ins)
            for half in range(2):
                hh = slice(4 * half, 4 * half + 4)
                dve.wait_ge(sem("o_pe"), 5 + half)
                sig(V.tensor_tensor(O1[:, 1, hh, :], M[2 + half].rearrange("p (a b) -> p a b", a=4), O1[:, 1, hh, :], ALU.add), "o_raw")
            output_factors(0)
            times_z(0)
            output_norm(1)
            times_z(1)
            output_factors(1)
            halves = [(slice(NCOL * n, NCOL * n + NCOL), O1[:, :, 4 * n:4 * n + 4, :].rearrange("p t h d -> p t (h d)")) for n in range(2)]
            cols, o = halves[0]
            sig(V.scalar_tensor_tensor(o, oa[:, :, cols], 0.5, o, ALU.mult, ALU.add), "o_done")
            cols, o = halves[1]
            for t in range(NT):
                dve.wait_ge(sem(f"ev{t}"), B_GA + 2)
                link(V.scalar_tensor_tensor(o[:, t], TMP[:, t], 1.0, o[:, t], ALU.add, ALU.mult))
                ins = V.scalar_tensor_tensor(o[:, t], oa[:, t, cols], 0.5, o[:, t], ALU.mult, ALU.add)
                if t == 0:
                    turn_lo(banks=range(2))
            sig(ins, "o_done")
            turn_lo(banks=range(2, 4))
            begin(B_O)
            residual(B_O, 0)
            begin(B_O + 1)
            residual(B_O + 1, 1)
            turn_lo(NORMS["mlp"])
            mean_squares(1)
            dve.wait_ge(sem("stat_rs"), 2)

            def relu(b, i=None):
                mm_finished(B_UP + b, i)
                for t in range(NT):
                    if i is not None or b >= 2:
                        dve.wait_ge(sem("hid_pe"), at(2 * (b - 2) + 2, 4, i))
                    V.tensor_scalar(hid[:, b % 2, t], G[(B_UP + b) % 2][t][:, :], RS[:, 2 + t:3 + t], 0.0, ALU.mult, ALU.max).then_inc(sem(f"ev{t}"), 1)

            def hidden_lo(b, i=None):
                for q in range(2):
                    dve.wait_ge(sem("hid_hi"), at(2 * b + q + 1, 4, i))
                    kk = bass.ds(at(4 * b + 2 * q, 8, i), 2)
                    V.tensor_tensor(hT_lo[:, kk, :], M[2 * (b % 2) + q].rearrange("p (a b) -> p a b", a=2), hT_hi[:, kk, :].bitcast(F32), ALU.subtract)\
                        .then_inc(sem("hid_lo"), 1)

            begin(B_UP)
            relu(0)
            begin(B_UP + 1)
            relu(1)
            hidden_lo(0)
            begin(B_UP + 2)
            relu(2)
            hidden_lo(1)
            with dve.Fori(0, 2) as i:
                for j in range(2):
                    begin(B_UP + 3 + j, i)
                    relu(3 + j, i)
                    hidden_lo(2 + j, i)
            begin(B_UP + 7)
            relu(7)
            hidden_lo(6)
            hidden_lo(7)
            for j in range(2):
                begin(B_DN + j)
                residual(B_DN + j, j)
            turn_lo(NORMS["mix2"])
            mean_squares(2)
            dve.wait_ge(sem("stat_rs"), 3)
            rs2 = RS[:, 5:6]
            for k in range(4):
                begin(B_2 + k)
                project(B_2 + k, P2R[:, 1, NCOL * k:NCOL * k + NCOL], rs2)
                if k == 1:
                    dve.wait_ge(sem("ev0"), B_2 + 2)
                    dve.wait_ge(sem("ev1"), B_2 + 2)
                    qk = P2R[:, :, 0:1024].rearrange("p t (h d) -> p t h d", d=64)
                    cr, sr = (spread(cst[:, C_ROPE_R + 64 * n:C_ROPE_R + 64 * n + 64].rearrange("p (t d) -> p t d", t=2), 2, 16) for n in range(2))
                    pr = [RT2[:, n].rearrange("p (t h d) -> p t h d", t=2, h=16) for n in range(4)]
                    sig(rotate(qk[:, :, :, 0:32], qk[:, :, :, 32:64], cr, sr, pr, V, link), "ret_rot")
            begin(B_2 + 4)
            dve.wait_ge(sem("ret_rot"), 1)
            for e, dst in ((1, rqT[:, 2:4, :]), (3, rkT[:, 2:4, :])):
                dve.wait_ge(sem("retT"), e + 1)
                V.tensor_copy(dst, M[e].rearrange("p (a b) -> p a b", a=2)).then_inc(sem("ret_dve"), 1)
            project(B_2 + 4, P2F[:, 1, 0:NCOL], rs2)
            begin(B_2 + 5)
            dve.wait_ge(sem("ret_w_in"), 16)
            for e in range(4):
                dve.wait_ge(sem("ret_s"), e + 1)
                V.tensor_tensor(PT2[:, 512 * e:512 * e + 512], M[e][:, :], WR[:, 512 * e:512 * e + 512], ALU.mult).then_inc(sem("ret_w"), 1)
            for e in range(2):
                dve.wait_ge(sem("ret_s"), e + 5)
                V.tensor_tensor(PT2[:, 2048 + 512 * e:][:, 0:512], M[e][:, :], WR[:, 2048 + 512 * e:][:, 0:512], ALU.mult).then_inc(sem("ret_w"), 1)
            project(B_2 + 5, P2F[:, 1, NCOL:2 * NCOL], rs2)
            begin(B_2 + 6)
            dve.wait_ge(sem("fox_sq"), 1)
            link(V.tensor_reduce(SSF, SQR.rearrange("p t h d -> p (t h) d"), AX_X, ALU.add))
            V.tensor_scalar(SSF, SSF, 1 / 64, EPS, ALU.mult, ALU.add).then_inc(sem("fox_ms"), 1)
            project(B_2 + 6, P2F[:, 1, block_columns(B_2 + 6)], rs2)
            begin(B_2 + 7)
            project(B_2 + 7, P2F[:, 1, block_columns(B_2 + 7)], rs2)
            ret = [MG2[:, t, 0:NCOL].rearrange("p (h d) -> p h d", d=64) for t in range(NT)]
            for t in range(NT):
                dve.wait_ge(sem("ret_oc"), t + 1)
                ins = V.tensor_reduce(MU[:, 8 * t:8 * t + 8], ret[t], AX_X, ALU.add)
            link(ins)
            turn_lo(NORMS["mem"])
            begin(B_KV)
            mean_squares(3)
            link(V.tensor_scalar(MU, MU, 1 / 64, None, ALU.mult))
            for t in range(NT):
                ins = V.tensor_tensor(ret[t], ret[t], spread(MU[:, 8 * t:8 * t + 8], 2, 64), ALU.subtract)
            ins.then_inc(sem("ret_cen"), 1)
            dve.wait_ge(sem("ev0"), B_2 + 8)
            dve.wait_ge(sem("ev1"), B_2 + 8)
            link(V.tensor_tensor(sp2, P2F[:, :, 1536:1544], spread(vec[:, V_BF:V_BF + 8], 1, 2), ALU.add))
            link(V.tensor_scalar(FL.rearrange("p t h -> p (t h)"), SP[:, 0:16], 0.0, None, ALU.min))
            V.scalar_tensor_tensor(SP[:, 0:16], SP[:, 0:16], -1.0, SP[:, 0:16], ALU.mult, ALU.max).then_inc(sem("f_abs"), 1)
            dve.wait_ge(sem("ret_sq"), 1)
            link(V.tensor_reduce(VAR, RSQ.rearrange("p t (h d) -> p (t h) d", d=64), AX_X, ALU.add))
            V.tensor_scalar(VAR, VAR, 1 / 64, EPS, ALU.mult, ALU.add).then_inc(sem("ret_ms"), 1)
            dve.wait_ge(sem("f_ln"), 1)
            V.tensor_tensor(FL.rearrange("p t h -> p (t h)"), FL.rearrange("p t h -> p (t h)"), SP[:, 16:32], ALU.subtract).then_inc(sem("fox_f"), 1)
            dve.wait_ge(sem("fox_rn"), 1)
            for n, dst in enumerate((QA, KA)):
                for t in range(NT):
                    src = P2F[:, t, NCOL * n:NCOL * n + NCOL].rearrange("p (h d) -> p h d", d=64)
                    ins = V.tensor_tensor(dst[:, t, :, 0:64], src, spread(RNF[:, 16 * t + 8 * n:][:, 0:8], 2, 64), ALU.mult)
            link(ins)
            for n, (dst, g) in enumerate(((QA, V_FQ), (KA, V_FK))):
                d = dst.rearrange("p t h d -> p (t h) d")[:, :, 0:64]
                if n == 0:
                    V.scalar_tensor_tensor(d, d, 1 / 8, spread(vec[:, g:g + 64], 1, 16), ALU.mult, ALU.mult)
                else:
                    V.tensor_tensor(d, d, spread(vec[:, g:g + 64], 1, 16), ALU.mult)
            V.memset(QA[:, :, :, 65:66], 1.0)
            V.memset(KA[:, :, :, 64:65], 1.0)
            dve.wait_ge(sem("stat_rs"), 4)
            rs4 = RS[:, 7:8]
            project(B_KV, KV[:, 1, 0:NCOL], rs4)
            dve.wait_ge(sem("fox_fc"), 1)
            fc = M[0][:, 0:16].rearrange("p (t h) -> p t h", t=2)
            V.tensor_copy(QA[:, :, :, 64], fc)
            V.tensor_scalar(KA[:, :, :, 65], fc, -1.0, None, ALU.mult).then_inc(sem("fox_aug"), 1)
            begin(B_KV + 1)
            project(B_KV + 1, KV[:, 1, NCOL:D], rs4)
            for e in range(1, 8, 2):
                dve.wait_ge(sem("foxT_pe"), e + 1)
                dst = (qaT if e < 4 else kaT)[0:66, 2 * (e % 4):2 * (e % 4) + 2, :]
                V.tensor_copy(dst, M[e % 4][0:66, :].rearrange("p (a b) -> p a b", a=2)).then_inc(sem("foxT_dve"), 1)
            for k in attention(WORK_A, 1.0, 64, fox_mask, LM2, PTS2,
                               lambda t, hs: MG2[:, t, NCOL + 64 * hs[0]:NCOL + 64 * hs[-1] + 64].rearrange("p (a b) -> p a b", b=64)):
                if k in (1, 3):
                    split(B_KV + 3, k // 2)
                if k == 2:
                    dve.wait_ge(sem("rg_tanh"), 1)
                    link(V.scalar_tensor_tensor(TG, TG, 1.0, P2R[:, :, RG:RG + NCOL], ALU.add, ALU.mult))
                    for t in range(NT):
                        ins = V.scalar_tensor_tensor(TG[:, t], TG[:, t], 0.5, vec[:, V_RO:V_RO + NCOL], ALU.mult, ALU.mult)
                    link(ins)
                if k == 3:
                    dve.wait_ge(sem("ret_rs"), 1)
                    for t in range(NT):
                        ins = V.tensor_tensor(ret[t], ret[t], spread(RSTD[:, 8 * t:8 * t + 8], 2, 64), ALU.mult)
                    link(ins)
                    sig(V.tensor_tensor(MG2[:, :, 0:NCOL], MG2[:, :, 0:NCOL], TG, ALU.mult), "ret_done")
                if k == 4:
                    project(B_KV + 2, KV[:, 1, D:D + NCOL], rs4)
                if k == 5:
                    split(B_O2, 0)
                if k == 6:
                    turn_lo(banks=range(2))
            project(B_KV + 3, KV[:, 1, D + NCOL:2 * D], rs4)
            split(B_O2, 1)
            turn_lo(banks=range(2, 4))
            begin(B_O2)
            dve.wait_ge(sem("x_sqk"), 1)
            link(V.tensor_reduce(SSX, SQX.rearrange("p t (h d) -> p (t h) d", d=256), AX_X, ALU.add))
            V.tensor_scalar(SSX, SSX, 1 / 256, EPS, ALU.mult, ALU.add).then_inc(sem("x_ms"), 1)
            residual(B_O2, 0)
            begin(B_O2 + 1)
            residual(B_O2 + 1, 1)
            turn_lo(NORMS["xattn"])
            mean_squares(4)
            link(V.tensor_tensor(vec[:, V_XK:V_XK + 256], vec[:, V_XK:V_XK + 256], vec[:, V_XQ:V_XQ + 256], ALU.mult))
            dve.wait_ge(sem("x_rn"), 1)
            kv = [KV[:, t, 0:D].rearrange("p (h d) -> p h d", d=256) for t in range(NT)]
            for t in range(NT):
                ins = V.tensor_tensor(kv[t], kv[t], spread(RNX[:, 4 * t:4 * t + 4], 2, 256), ALU.mult)
            link(ins)
            for t in range(NT):
                ins = V.tensor_tensor(kv[t], kv[t], spread(vec[:, V_XK:V_XK + 256], 1, 4), ALU.mult)
            ins.then_inc(sem("x_k"), 1)
            dve.wait_ge(sem("stat_rs"), 5)
            for k in range(2):
                begin(B_XQ + k)
                project(B_XQ + k, XQ[:, 1, NCOL * k:NCOL * k + NCOL], RS[:, 9:10])
                for e in (4 * k + 1, 4 * k + 3):
                    dve.wait_ge(sem("xT_pe"), e + 1)
                    dst = (xkT if e < 4 else xqT)[:, 2 * (e % 4):2 * (e % 4) + 2, :]
                    V.tensor_copy(dst, M[e % 4].rearrange("p (a b) -> p a b", a=2)).then_inc(sem("xT_dve"), 1)
                    if e == 5:
                        dve.wait_ge(sem("x_sqq"), 2)
                        V.tensor_scalar(SSX, SSX, 1 / 256, EPS, ALU.mult, ALU.add).then_inc(sem("x_ms"), 1)
            dve.wait_ge(sem("x_rn"), 2)
            V.tensor_scalar(XSC, RNX[:, 8:16], 1 / 16, None, ALU.mult).then_inc(sem("x_sc"), 1)
            link(V.tensor_scalar(RNX[:, 8:16], RNX[:, 8:16], -1 / 16, None, ALU.mult))
            for k in attention(WORK_X, lambda t, hs: RNX[:, 8 + 4 * t + hs[0]:8 + 4 * t + hs[-1] + 1], 256, None, None, PTS2,
                               lambda t, hs: XO[:, t, 256 * hs[0]:256 * hs[-1] + 256].rearrange("p (a b) -> p a b", b=256)):
                if k == 4:
                    turn_lo(banks=range(2))
            turn_lo(banks=range(2, 4))
            for j in range(2):
                begin(B_XO + j)
                residual(B_XO + j, j)
            turn_lo(NORMS["ffn"])
            mean_squares(5)
            dve.wait_ge(sem("stat_rs"), 6)
            link(V.tensor_scalar(RS5H, RS[:, 10:12], 0.5, None, ALU.mult))
            V.tensor_tensor(RS5Q, RS5H, RS[:, 10:12], ALU.mult).then_inc(sem("rs5"), 1)

            def gate_mul(p, i=None):
                b = B_GU + 2 * p
                n = blocks[b]["n"]
                for t in range(NT):
                    dve.wait_ge(sem("gate_tanh"), at(2 * p + t + 1, 2, i))
                    V.scalar_tensor_tensor(sg2[:, 1, t, 0:n], sg2[:, 0, t, 0:n], 1.0, G[b % 2][t][:, 0:n], ALU.add, ALU.mult).then_inc(sem(f"ev{t}"), 1)

            def up_mul(p, i=None):
                b = B_GU + 2 * p + 1
                n = blocks[b]["n"]
                mm_finished(b, i)
                for t in range(NT):
                    dve.wait_ge(sem(f"ev{t}"), at(b, 2, i))
                    if i is not None or p > 0:
                        dve.wait_ge(sem("hid2_pe"), at(2 * p, 2, i))
                    V.tensor_tensor(hid2[:, t, 0:n], sg2[:, 1, t, 0:n], G[b % 2][t][:, 0:n], ALU.mult).then_inc(sem(f"ev{t}"), 1)

            def hidden2_lo(p, i=None, q_n=2):
                for q in range(q_n):
                    dve.wait_ge(sem("hid2_hi"), at(2 * p + q + 1, 2, i))
                    kk = bass.ds(at(4 * p + 2 * q, 4, i), 2)
                    V.tensor_tensor(h2_lo[:, kk, :], M[q].rearrange("p (a b) -> p a b", a=2), h2_hi[:, kk, :].bitcast(F32), ALU.subtract)\
                        .then_inc(sem("hid2_lo"), 1)

            begin(B_GU)
            gate_mul(0)
            begin(B_GU + 1)
            up_mul(0)
            with dve.Fori(0, 3) as i:
                begin(B_GU + 2, i)
                gate_mul(1, i)
                begin(B_GU + 3, i)
                hidden2_lo(0, i)
                up_mul(1, i)
            begin(B_GU + 8)
            gate_mul(4)
            begin(B_GU + 9)
            hidden2_lo(3)
            up_mul(4)
            begin(B_GU + 10)
            gate_mul(5)
            hidden2_lo(4)
            begin(B_GU + 11)
            up_mul(5)
            hidden2_lo(5, q_n=1)
            begin(B_D2)
            residual(B_D2, 0)
            begin(B_D2 + 1)
            residual(B_D2 + 1, 1, last=True)

        @block.gpsimd
        def _(pool):
            def split(b, c):
                n = blocks[b]["chunk0"] + c
                kn, width = chunk_shape(b, c)
                pool.wait_ge(sem("split_hi"), n + 1)
                s = n % SLOTS
                pool.tensor_tensor(w_lo[:, s, 0:kn, 0:width], raw[:, s, 0:kn, 0:width], w_hi[:, s, 0:kn, 0:width].bitcast(F32), ALU.subtract)\
                    .then_inc(sem("split_lo_pool"), 1)

            def power(dst, src, n, wait, value, name):
                pool.wait_ge(sem(wait), value)
                pool.tensor_tensor(dst, src, MHALF[:, 0:n], ALU.pow).then_inc(sem(name), 1)

            for n, g in enumerate((norm_mlp_g, g_mix_2, g_xattn_2, g_mem_2, g_ffn_2)):
                pool.dma_start(hidden_rows[8 * n + 8:8 * n + 16, :], g[0].rearrange("(k p) -> k p", p=P)).then_inc(sem("rows_in"), 16)
            pool.dma_start(conv_rows[0:96, :], conv_w[0].rearrange("j (k p) -> (j k) p", p=P)).then_inc(sem("rows_in"), 16)
            for dst, src in ((vec[:, V_QG:V_QG + P], q_norm_g[0]), (vec[:, V_KG:V_KG + P], k_norm_g[0]), (vec[:, V_GN:V_GN + P], gdn_norm_g[0]),
                             (vec[:, V_DT:V_DT + 8], dt_bias[0]), (vec[:, V_AL:V_AL + 8], a_log[0]), (vec[:, V_BF:V_BF + 8], b_forget_2[0]),
                             (vec[:, V_FQ:V_FQ + 64], g_fox_q_2[0]), (vec[:, V_FK:V_FK + 64], g_fox_k_2[0]),
                             (vec[:, V_XQ:V_XQ + 256], g_xq_2[0]), (vec[:, V_XK:V_XK + 256], g_xk_2[0]),
                             (vec[:, V_RO:V_RO + NCOL], g_ret_out_2[0].rearrange("h d -> (h d)"))):
                pool.dma_start(dst, src.partition_broadcast(P)).then_inc(sem("vec_in"), 16)
            pool.memset(MHALF, -0.5).then_inc(sem("pool_half"), 1)
            pool.wait_ge(sem("pool_half"), 1)

            def norm_power(k):
                power(RS[:, 2 * k:2 * k + 2], RS[:, 2 * k:2 * k + 2], 2, "stat_ms", k + 1, "stat_rs")

            norm_power(0)
            pool.wait_ge(sem("consts_in"), 16)
            pool.wait_ge(sem("ev0"), 5)
            pool.wait_ge(sem("ev1"), 5)
            idx = PA[:, :, IQ:IW].rearrange("p t (h d) -> p t h d", d=64)
            ci, si = (spread(cst[:, C_ROPE_I + 16 * k:C_ROPE_I + 16 * k + 16].rearrange("p (t d) -> p t d", t=2), 2, 9) for k in range(2))
            x1, x2 = idx[:, :, :, 0:8], idx[:, :, :, 8:16]
            pr = [RTI[:, k].rearrange("p (t h d) -> p t h d", t=2, h=9) for k in range(4)]
            for n, (a, f) in enumerate(((x1, ci), (x2, si), (x2, ci), (x1, si))):
                for t in range(NT):
                    ins = pool.tensor_tensor(pr[n][:, t], a[:, t], f[:, t], ALU.mult)
            ins.then_inc(sem("pool_step"), 1)
            pool.wait_ge(sem("pool_step"), 1)
            for t in range(NT):
                pool.tensor_tensor(x1[:, t], pr[0][:, t], pr[1][:, t], ALU.subtract)
                ins = pool.tensor_tensor(x2[:, t], pr[2][:, t], pr[3][:, t], ALU.add)
            ins.then_inc(sem("pool_step"), 1)
            pool.wait_ge(sem("pool_step"), 2)
            for n in range(2):
                ins = pool.tensor_copy(IKD[:, :, n, :], PA[:, :, IK:IW])
            ins.then_inc(sem("idx_rot"), 1)
            power(RNA, SSA, 20, "att_ms", 1, "att_rn")
            for b in range(B_Q + 2, B_GB + 1):
                split(b, 1)
            pool.wait_ge(sem("gdn_g"), 1)
            pool.wait_ge(sem("att_norm"), 6)
            split(B_GB + 1, 0)
            split(B_GB + 1, 1)
            pool.tensor_tensor(GU, spread(GA_, 2, P), spread(cst[:, C_CUM:C_CUM + P], 1, 16), ALU.mult).then_inc(sem("gdn_gu"), 1)
            for b in (B_Z, B_Z + 1):
                for c in range(2):
                    split(b, c)
            power(RQK, SSK, 32, "gdn_ms", 1, "gdn_rq")
            pool.wait_ge(sem("gdn_y"), 12)
            pool.wait_ge(sem("gdn_kdf"), 1)
            pool.tensor_tensor(KD, KN[:, 0], spread(KDF, 2, P), ALU.mult).then_inc(sem("gdn_kd"), 1)
            pool.wait_ge(sem("gdn_kb"), 2)
            pool.tensor_tensor(KBG, KB[:, 1], spread(EG[:, 8:16], 2, P), ALU.mult).then_inc(sem("gdn_kbg"), 1)
            for lv in range(LEVELS):
                for u in range(4):
                    if lv == 0:
                        pool.wait_ge(sem("gdn_kk"), 4)
                        pool.wait_ge(sem("gdn_at"), u + 1)
                    else:
                        pool.wait_ge(sem("inv_p"), 4 * (lv - 1) + u + 1)
                        if lv == 1:
                            pool.wait_ge(sem("inv_xt"), u + 1)
                    n = slice(4 * u, 4 * u + 4)
                    parts = [LT[:, n, :], AT[:, n, :], spread(cst[:, C_LEV + P * lv:C_LEV + P * lv + P], 1, 4)]
                    if lv > 0:
                        parts = [blocks_of(v, lv, 1) for v in parts]
                    pool.tensor_tensor(*parts, ALU.mult).then_inc(sem("inv_lt"), 1)
            for t in range(NT):
                power(RSO[:, 8 * t:8 * t + 8], SSO[:, 8 * t:8 * t + 8], 8, "o_ms", t + 1, "o_rs")
            norm_power(1)
            norm_power(2)
            power(RNF, SSF, 32, "fox_ms", 1, "fox_rn")
            norm_power(3)
            power(RSTD, VAR, 16, "ret_ms", 1, "ret_rs")
            power(RNX[:, 0:8], SSX, 8, "x_ms", 1, "x_rn")
            norm_power(4)
            power(RNX[:, 8:16], SSX, 8, "x_ms", 2, "x_rn")
            norm_power(5)
            split(B_D2, 1)


_INS = ['x', 'norm_mix_g', 'w_in', 'conv_w', 'a_log', 'dt_bias', 'gdn_norm_g', 'q_norm_g', 'k_norm_g', 'w_out', 'norm_mlp_g',
        'w_mlp_up', 'w_mlp_down', 'mem_2', 'g_mix_2', 'w_in_2', 'b_forget_2', 'g_ret_out_2', 'g_fox_q_2', 'g_fox_k_2', 'w_out_2',
        'g_xattn_2', 'w_xq_2', 'w_xkv_2', 'g_mem_2', 'g_xq_2', 'g_xk_2', 'w_xo_2', 'g_ffn_2', 'w_gate_2', 'w_up_2', 'w_down_2']


def kernel(**inputs):
    import numpy as _np
    import concourse.bacc as _bacc
    from concourse import mybir as _mybir
    from concourse.bass_utils import run_bass_kernel_spmd as _run

    nc = _bacc.Bacc("TRN2", target_bir_lowering=False, num_devices=1)
    arrays, args = {}, []
    given = [(name, _np.ascontiguousarray(inputs[name])) for name in _INS]
    given += [("constants", constants()), ("retention", retention_weights())]
    for name, a in given:
        arrays[f"in_{name}_dram"] = a
        args.append(nc.dram_tensor(f"in_{name}_dram", a.shape, _mybir.dt.from_np(a.dtype), kind="ExternalInput").ap())
    args.append(nc.dram_tensor("out_0_dram", (1, SEQ, D), _mybir.dt.float32, kind="ExternalOutput").ap())
    build(nc, *args)
    r = _run(nc, [arrays], core_ids=[0])
    return r.results[0]["out_0_dram"]
```
